# Optimizing a Trainium2 kernel written in Bass

```python
import jax
import jax.numpy as jnp
from jax import lax
import numpy as np

D_MODEL = 1024
BATCH = 1
SEQ = 256
DEPTH = 2

N_EVEN = (DEPTH + 1) // 2
N_ODD = DEPTH // 2
EPS = 1e-6

GM_HEADS = 8
GM_HEAD_DIM = D_MODEL // (2 * GM_HEADS)
GM_WIDTH = GM_HEADS * GM_HEAD_DIM
GM_CHUNK = 128

MLA_HEADS = 8
MLA_Q_RANK = 3 * D_MODEL // 8
MLA_KV_RANK = D_MODEL // 4
MLA_NOPE_DIM = 64
MLA_ROPE_DIM = 32
MLA_QK_DIM = MLA_NOPE_DIM + MLA_ROPE_DIM
MLA_V_DIM = D_MODEL // (2 * MLA_HEADS)
MLA_WIDTH = MLA_HEADS * MLA_V_DIM
ROPE_THETA = 10000.0
ATTN_BLOCK = 128

IN_WIDTH = 2 * GM_WIDTH + MLA_Q_RANK + MLA_KV_RANK + MLA_ROPE_DIM
MIX_WIDTH = GM_WIDTH + MLA_WIDTH

CONV_CH = D_MODEL
CONV_WIDTH = 31

PEER_HEADS = 8
PEER_N_KEYS = 128
PEER_N_EXPERTS = PEER_N_KEYS * PEER_N_KEYS
PEER_KEY_DIM = 256
PEER_HALF = PEER_KEY_DIM // 2
PEER_TOPK = 16
PEER_BLOCK = 128

kernel_name = 'hybrid_gmlp_mla_conformer_peer'

def rms_norm(x, g):
    xf = x.astype(jnp.float32)
    y = xf * lax.rsqrt(jnp.mean(xf * xf, axis=-1, keepdims=True) + EPS)
    return (y * g.astype(jnp.float32)).astype(x.dtype)

def apply_rope(x, positions):
    half = MLA_ROPE_DIM // 2
    inv_freq = ROPE_THETA ** (-jnp.arange(half, dtype=jnp.float32) / half)
    ang = positions.astype(jnp.float32)[..., None] * inv_freq
    cos = jnp.cos(ang)[:, :, None, :]
    sin = jnp.sin(ang)[:, :, None, :]
    xf = x.astype(jnp.float32)
    x1, x2 = xf[..., :half], xf[..., half:]
    out = jnp.concatenate([x1 * cos - x2 * sin, x1 * sin + x2 * cos], axis=-1)
    return out.astype(x.dtype)

def chunked_spatial_gating(u, v, v_gain, w_s, b_s):
    B, S, H, Dh = u.shape
    n_chunks = S // GM_CHUNK
    u = jax.nn.gelu(u)
    v = rms_norm(jax.nn.gelu(v), v_gain)
    causal = jnp.tril(jnp.ones((GM_CHUNK, GM_CHUNK), dtype=bool))
    w = jnp.where(causal[None], w_s, 0).astype(v.dtype)
    vc = v.reshape(B, n_chunks, GM_CHUNK, H, Dh)
    mixed = jnp.einsum('hts,bcshd->bcthd', w, vc) + b_s.T.astype(v.dtype)[None, None, :, :, None]
    return (u * mixed.reshape(B, S, H, Dh)).reshape(B, S, H * Dh)

def causal_block_attention(q, k, v):
    S = q.shape[1]
    scale = MLA_QK_DIM ** -0.5
    outs = []
    for blk in range(S // ATTN_BLOCK):
        q0 = blk * ATTN_BLOCK
        kend = q0 + ATTN_BLOCK
        s = jnp.einsum('bqhd,bkhd->bhqk', q[:, q0:kend], k[:, :kend],
                       preferred_element_type=jnp.float32) * scale
        causal = (q0 + jnp.arange(ATTN_BLOCK))[:, None] >= jnp.arange(kend)[None, :]
        s = jnp.where(causal, s, -1e30)
        p = jax.nn.softmax(s, axis=-1).astype(v.dtype)
        outs.append(jnp.einsum('bhqk,bkhd->bqhd', p, v[:, :kend]))
    return jnp.concatenate(outs, axis=1)

def latent_attention(q_lat, kv_lat, k_pe, positions, q_lat_gain, w_uq, kv_lat_gain, w_ukv,
                     q_gain, k_gain):
    B, S, _ = q_lat.shape
    q = (rms_norm(q_lat, q_lat_gain) @ w_uq).reshape(B, S, MLA_HEADS, MLA_QK_DIM)
    kv = (rms_norm(kv_lat, kv_lat_gain) @ w_ukv).reshape(B, S, MLA_HEADS, MLA_NOPE_DIM + MLA_V_DIM)
    k_nope, v = kv[..., :MLA_NOPE_DIM], kv[..., MLA_NOPE_DIM:]
    k_rope = jnp.broadcast_to(k_pe[:, :, None, :], (B, S, MLA_HEADS, MLA_ROPE_DIM))
    k = jnp.concatenate([k_nope, k_rope], axis=-1)
    q = rms_norm(q, q_gain)
    k = rms_norm(k, k_gain)
    q = jnp.concatenate([q[..., :MLA_NOPE_DIM], apply_rope(q[..., MLA_NOPE_DIM:], positions)], axis=-1)
    k = jnp.concatenate([k[..., :MLA_NOPE_DIM], apply_rope(k[..., MLA_NOPE_DIM:], positions)], axis=-1)
    o = causal_block_attention(q, k, v)
    return o.reshape(B, S, MLA_WIDTH)

def parallel_gmlp_mla(h, positions, w_in, gm_v_gain, gm_w_s, gm_b_s, mla_q_lat_gain, mla_w_uq,
                      mla_kv_lat_gain, mla_w_ukv, mla_q_gain, mla_k_gain, w_out):
    B, S, _ = h.shape
    z = h @ w_in
    cuts = [GM_WIDTH, 2 * GM_WIDTH, 2 * GM_WIDTH + MLA_Q_RANK,
            2 * GM_WIDTH + MLA_Q_RANK + MLA_KV_RANK]
    u, v, q_lat, kv_lat, k_pe = jnp.split(z, cuts, axis=-1)
    a = chunked_spatial_gating(u.reshape(B, S, GM_HEADS, GM_HEAD_DIM),
                               v.reshape(B, S, GM_HEADS, GM_HEAD_DIM), gm_v_gain, gm_w_s, gm_b_s)
    b = latent_attention(q_lat, kv_lat, k_pe, positions, mla_q_lat_gain, mla_w_uq,
                         mla_kv_lat_gain, mla_w_ukv, mla_q_gain, mla_k_gain)
    return jnp.concatenate([a, b], axis=-1) @ w_out

def conformer_conv(h, w_pw1, b_pw1, w_dw, b_dw, norm_gain, w_pw2, b_pw2):
    z = h @ w_pw1 + b_pw1
    a, g = jnp.split(z, 2, axis=-1)
    z = a * jax.nn.sigmoid(g)
    z = lax.conv_general_dilated(z, w_dw[:, None, :].astype(z.dtype), window_strides=(1,),
                                 padding=[(CONV_WIDTH - 1, 0)],
                                 dimension_numbers=('NWC', 'WIO', 'NWC'),
                                 feature_group_count=CONV_CH) + b_dw
    z = jax.nn.silu(rms_norm(z, norm_gain))
    return z @ w_pw2 + b_pw2

def peer_layer(h, w_q, sub_keys, expert_u, expert_v):
    B, S, D = h.shape
    hb = h.reshape((B * S) // PEER_BLOCK, PEER_BLOCK, D)

    def retrieve(xb):
        T = xb.shape[0]
        q = (xb @ w_q).reshape(T, PEER_HEADS, 2, PEER_HALF)
        s = jnp.einsum('thcd,chnd->thcn', q, sub_keys, preferred_element_type=jnp.float32)
        top_s, top_i = lax.top_k(s, PEER_TOPK)
        cand_s = top_s[..., 0, :, None] + top_s[..., 1, None, :]
        cand_i = top_i[..., 0, :, None] * PEER_N_KEYS + top_i[..., 1, None, :]
        best_s, best_pos = lax.top_k(cand_s.reshape(T, PEER_HEADS, PEER_TOPK * PEER_TOPK), PEER_TOPK)
        idx = jnp.take_along_axis(cand_i.reshape(T, PEER_HEADS, PEER_TOPK * PEER_TOPK), best_pos, axis=-1)
        gate = jax.nn.softmax(best_s, axis=-1).astype(xb.dtype)
        act = jax.nn.gelu(jnp.einsum('thkd,td->thk', expert_u[idx], xb))
        return jnp.einsum('thk,thkd->td', gate * act, expert_v[idx])

    return lax.map(retrieve, hb).reshape(B, S, D)

def setup_inputs(seed: int = 0) -> dict:
    key = jax.random.key(seed)
    ks = iter(jax.random.split(key, 40))

    def nrm(shape, scale):
        return jax.random.normal(next(ks), shape, jnp.float32) * scale

    def gain(shape):
        return 1.0 + 0.05 * jax.random.normal(next(ks), shape, jnp.float32)

    x = jax.random.normal(next(ks), (BATCH, SEQ, D_MODEL), jnp.float32)
    offsets = jax.random.randint(next(ks), (BATCH, 1), 0, 4096, dtype=jnp.int32)
    positions = offsets + jnp.arange(SEQ, dtype=jnp.int32)[None, :]
    return {
        'x': x,
        'positions': positions,
        'mix_norm_even': gain((N_EVEN, D_MODEL)),
        'w_in': nrm((N_EVEN, D_MODEL, IN_WIDTH), D_MODEL ** -0.5),
        'gm_v_gain': gain((N_EVEN, GM_HEADS, GM_HEAD_DIM)),
        'gm_w_s': nrm((N_EVEN, GM_HEADS, GM_CHUNK, GM_CHUNK), GM_CHUNK ** -0.5),
        'gm_b_s': 1.0 + 0.1 * nrm((N_EVEN, GM_HEADS, GM_CHUNK), 1.0),
        'mla_q_lat_gain': gain((N_EVEN, MLA_Q_RANK)),
        'mla_w_uq': nrm((N_EVEN, MLA_Q_RANK, MLA_HEADS * MLA_QK_DIM), MLA_Q_RANK ** -0.5),
        'mla_kv_lat_gain': gain((N_EVEN, MLA_KV_RANK)),
        'mla_w_ukv': nrm((N_EVEN, MLA_KV_RANK, MLA_HEADS * (MLA_NOPE_DIM + MLA_V_DIM)), MLA_KV_RANK ** -0.5),
        'mla_q_gain': gain((N_EVEN, MLA_QK_DIM)),
        'mla_k_gain': gain((N_EVEN, MLA_QK_DIM)),
        'w_out': nrm((N_EVEN, MIX_WIDTH, D_MODEL), MIX_WIDTH ** -0.5),
        'mix_norm_odd': gain((N_ODD, D_MODEL)),
        'conv_w_pw1': nrm((N_ODD, D_MODEL, 2 * CONV_CH), D_MODEL ** -0.5),
        'conv_b_pw1': nrm((N_ODD, 2 * CONV_CH), 0.02),
        'conv_w_dw': nrm((N_ODD, CONV_WIDTH, CONV_CH), CONV_WIDTH ** -0.5),
        'conv_b_dw': nrm((N_ODD, CONV_CH), 0.02),
        'conv_norm_gain': gain((N_ODD, CONV_CH)),
        'conv_w_pw2': nrm((N_ODD, CONV_CH, D_MODEL), CONV_CH ** -0.5),
        'conv_b_pw2': nrm((N_ODD, D_MODEL), 0.02),
        'ffn_norm': gain((DEPTH, D_MODEL)),
        'peer_w_q': nrm((DEPTH, D_MODEL, PEER_HEADS * PEER_KEY_DIM), D_MODEL ** -0.5),
        'peer_sub_keys': nrm((DEPTH, 2, PEER_HEADS, PEER_N_KEYS, PEER_HALF), PEER_HALF ** -0.5),
        'peer_u': nrm((DEPTH, PEER_N_EXPERTS, D_MODEL), D_MODEL ** -0.5),
        'peer_v': nrm((DEPTH, PEER_N_EXPERTS, D_MODEL), PEER_HEADS ** -0.5),
    }

def reference(x, positions, mix_norm_even, w_in, gm_v_gain, gm_w_s, gm_b_s, mla_q_lat_gain,
              mla_w_uq, mla_kv_lat_gain, mla_w_ukv, mla_q_gain, mla_k_gain, w_out, mix_norm_odd,
              conv_w_pw1, conv_b_pw1, conv_w_dw, conv_b_dw, conv_norm_gain, conv_w_pw2, conv_b_pw2,
              ffn_norm, peer_w_q, peer_sub_keys, peer_u, peer_v):
    for layer in range(DEPTH):
        i = layer // 2
        if layer % 2 == 0:
            h = rms_norm(x, mix_norm_even[i])
            x = x + parallel_gmlp_mla(h, positions, w_in[i], gm_v_gain[i], gm_w_s[i], gm_b_s[i],
                                      mla_q_lat_gain[i], mla_w_uq[i], mla_kv_lat_gain[i],
                                      mla_w_ukv[i], mla_q_gain[i], mla_k_gain[i], w_out[i])
        else:
            h = rms_norm(x, mix_norm_odd[i])
            x = x + conformer_conv(h, conv_w_pw1[i], conv_b_pw1[i], conv_w_dw[i], conv_b_dw[i],
                                   conv_norm_gain[i], conv_w_pw2[i], conv_b_pw2[i])
        h = rms_norm(x, ffn_norm[layer])
        x = x + peer_layer(h, peer_w_q[layer], peer_sub_keys[layer], peer_u[layer], peer_v[layer])
    return x


_drawn_inputs = setup_inputs


def setup_inputs(seed=0):
    import zlib

    import numpy as np

    out = dict(_drawn_inputs(seed))
    spreads = {}
    factors = {'mla_q_gain': 2.788, 'conv_b_pw1': 3.161}
    for name, (base, spread) in spreads.items():
        noise = np.random.default_rng([zlib.crc32(name.encode()), seed]).standard_normal(out[name].shape)
        drawn = base * np.exp(spread * noise) if base else spread * noise
        out[name] = jnp.asarray(drawn.astype(out[name].dtype))
    for name, factor in factors.items():
        out[name] = (out[name] * factor).astype(out[name].dtype)
    return out
```

```python
from contextlib import ExitStack

import numpy as np

import concourse.bass as bass
from concourse import mybir

ALU = mybir.AluOpType
ACT = mybir.ActivationFunctionType
AX = mybir.AxisListType
F32 = mybir.dt.float32
F32R = mybir.dt.float32r
U32 = mybir.dt.uint32
I32 = mybir.dt.int32

P = 128
D = 1024
SEQ = 256
NBLK = SEQ // P
KC = D // P
EPS = 1e-6
NEG = -1e30

GH, GD = 8, 64
MH, NOPE, ROPE, VD = 8, 64, 32, 64
QK = NOPE + ROPE
HALF = ROPE // 2
QRANK, KVRANK = 384, 256
LAT = QRANK + KVRANK + ROPE
INW = 2 * GH * GD + LAT
QCH, KVCH = QRANK // P, KVRANK // P
THETA = 10000.0

TAPS = 31

PH = 8
NKEYS = 128
TOPK = 16
LISTS = 2 * PH
UNITS = NBLK * PH
ROWS = [(0, 1, 16), (1, 3, 8), (4, 12, 3)]
ROW_START = [0] + [16 + 8 * (a - 1) for a in range(1, 4)] + [40 + 3 * (a - 4) for a in range(4, 16)]
CANDS = 76

RAW = 4
PARTS = 2
SLAB = 1024


def slab_plan():
    plan, first = [], {}

    def add(name, count, width):
        first[name] = len(plan)
        plan.extend((name, k, width) for k in range(count))

    add("w_in_gm", KC, 1024)
    add("w_in_lat", KC, LAT)
    add("w_uq", QCH, MH * QK)
    add("w_ukv", KVCH, MH * (NOPE + VD))
    add("w_out", KC, D)
    for layer in range(2):
        if layer:
            add("pw1", 2 * KC, SLAB)
            add("pw2", KC, D)
        add(f"w_q{layer}", LISTS, SLAB)
        add(f"u{layer}", NKEYS, SLAB)
        add(f"v{layer}", NKEYS, SLAB)
    return plan, first


def build(nc, t):
    plan, first = slab_plan()
    NSLAB = len(plan)

    ctx = ExitStack()
    with ctx:
        def sb(name, shape, dt=F32):
            return ctx.enter_context(nc.sbuf_tensor(name, shape, dt))

        sems = {}

        def S(name):
            if name not in sems:
                sems[name] = ctx.enter_context(nc.semaphore(name))
            return sems[name]

        big = sb("big", [P, NKEYS * SEQ])
        x_res = sb("x_res", [P, NBLK, D])
        hT_hi = sb("hT_hi", [P, KC, SEQ], F32R)
        hT_lo = sb("hT_lo", [P, KC, SEQ], F32R)
        raw = sb("raw", [P, RAW, SLAB])
        part_hi = sb("part_hi", [P, PARTS, SLAB], F32R)
        part_lo = sb("part_lo", [P, PARTS, SLAB], F32R)
        ident = sb("ident", [P, P])
        iota = sb("iota", [P, P])
        ones = sb("ones", [P, P])
        norm_gain = sb("norm_gain", [P, 5, KC])
        lat_gain = sb("lat_gain", [P, QCH + KVCH])
        taps = sb("taps", [P, KC, TAPS])
        conv_cols = sb("conv_cols", [P, 4, KC])
        stat = sb("stat", [P, 5, 4])
        row_start = sb("row_start", [P, TOPK])
        row_step = sb("row_step", [P, TOPK - 1])
        pick_i = sb("pick_i", [P, UNITS, TOPK])
        pick_j = sb("pick_j", [P, UNITS, TOPK])
        pick_s = sb("pick_s", [P, UNITS, TOPK])
        gate_sum = sb("gate_sum", [P, 2, UNITS])
        pickT = sb("pickT", [P, 3, SEQ])
        hot_i = sb("hot_i", [P, 2, 4, P])
        hot_j = sb("hot_j", [P, 2, 4, P])
        bank = [ctx.enter_context(nc.psum_tensor(f"bank{b}", [P, 512], F32)) for b in range(8)]

        used = [0]

        def part_of_big(*shape):
            n = int(np.prod(shape))
            v = big[:, used[0]:used[0] + n]
            used[0] += n
            assert used[0] <= NKEYS * SEQ
            if len(shape) == 2:
                return v.rearrange("p (a b) -> p a b", b=shape[1])
            if len(shape) == 3:
                return v.rearrange("p (a b c) -> p a b c", b=shape[1], c=shape[2])
            if len(shape) == 4:
                return v.rearrange("p (a b c d) -> p a b c d", b=shape[1], c=shape[2], d=shape[3])
            return v

        m_u = part_of_big(NBLK, 512)
        m_v = part_of_big(NBLK, 512)
        m_vsq = part_of_big(NBLK, 512)
        m_lat = part_of_big(NBLK, LAT)
        m_ws = part_of_big(GH, P)
        m_vgain = part_of_big(512)
        m_qkgain = part_of_big(2, QK)
        m_bs = part_of_big(GH)
        m_qk = part_of_big(NBLK * 2, MH, QK)
        m_val = part_of_big(NBLK, MH, VD)
        m_sq = part_of_big(NBLK * 2, MH, QK)
        m_qkT = part_of_big(2, MH, SEQ)
        m_p = part_of_big(MH, 3 * P)
        m_pT = part_of_big(MH, 3, P)
        m_cat = part_of_big(NBLK, D)
        m_mask = part_of_big(3 * P)
        m_rt = part_of_big(6, 16, HALF)
        m_ang = part_of_big(8, NBLK, HALF)
        m_freq = part_of_big(HALF)
        m_posi = part_of_big(NBLK)
        m_pos = part_of_big(NBLK)
        m_st = part_of_big(8, 2 * UNITS)

        act_all = big[:, :].rearrange("p (j t) -> p j t", t=SEQ)
        used[0] = NKEYS * SEQ // 2
        h_tok = part_of_big(NBLK, D)
        scores = part_of_big(UNITS, 2 * NKEYS)
        qT = part_of_big(2, SEQ)
        keysT = part_of_big(LISTS, NKEYS)
        stage = part_of_big(2, NKEYS)
        top_v = part_of_big(2, TOPK)
        top_iu = part_of_big(2, TOPK).bitcast(U32)
        top_if = part_of_big(2, TOPK)
        cand = part_of_big(CANDS)
        best_v = part_of_big(TOPK)
        best_pu = part_of_big(TOPK).bitcast(U32)
        best_p = part_of_big(TOPK)
        step_i = part_of_big(TOPK)
        col_b = part_of_big(TOPK)
        sum_i = part_of_big(TOPK)
        sum_r = part_of_big(TOPK)
        dec_ge = part_of_big(TOPK, TOPK)
        dec_m = part_of_big(TOPK, TOPK)
        dec_n = part_of_big(TOPK, TOPK)
        dec_e = part_of_big(TOPK, TOPK)

        used[0] = 0
        c_pad = part_of_big(KC, TAPS - 1 + SEQ)
        c_sig = part_of_big(2, SEQ)
        c_acc = part_of_big(KC, SEQ)
        c_sq = part_of_big(KC, SEQ)
        c_std = part_of_big(SEQ)
        c_rstd = part_of_big(SEQ)
        c_bias2 = part_of_big(D)
        assert used[0] < NKEYS * SEQ // 2

        def slab_src(name, k):
            if name == "w_in_gm":
                return t["w_in"][0, k * P:(k + 1) * P, 0:1024]
            if name == "w_in_lat":
                return t["w_in"][0, k * P:(k + 1) * P, 1024:INW]
            if name == "w_uq":
                return t["mla_w_uq"][0, k * P:(k + 1) * P, :]
            if name == "w_ukv":
                return t["mla_w_ukv"][0, k * P:(k + 1) * P, :]
            if name == "w_out":
                return t["w_out"][0, k * P:(k + 1) * P, :]
            if name == "pw2":
                return t["conv_w_pw2"][0, k * P:(k + 1) * P, :]
            src = {"pw1": t["conv_w_pw1"]}.get(name)
            if src is None:
                src = t[{"w_q": "peer_w_q", "u": "peer_u", "v": "peer_v"}[name[:-1]]][int(name[-1])]
            return src[bass.ds(k, 1)].rearrange("a p n -> (a p) n")

        def load_slab(sp, name, k, n, width, i=0):
            if n >= RAW:
                sp.wait_ge(S("slab_lo"), n - RAW + 1 + 4 * i)
            sp.dma_start(raw[:, n % RAW, 0:width], slab_src(name, k)).then_inc(S(f"slab_landed{n % RAW}"), 16)

        def split_hi(act, n, i=0):
            if isinstance(i, int) and n + 4 * i >= NSLAB:
                return
            w = plan[n][2]
            act.wait_ge(S(f"slab_landed{n % RAW}"), 16 * (n // RAW + 1) + 16 * i)
            if n >= PARTS:
                act.wait_ge(S("slab_used"), n - PARTS + 1 + 4 * i)
            act.activation(part_hi[:, n % PARTS, 0:w], raw[:, n % RAW, 0:w], ACT.Copy).then_inc(S("slab_hi"), 1)

        def split_lo(dve, n, i=0):
            if isinstance(i, int) and n + 4 * i >= NSLAB:
                return
            w = plan[n][2]
            dve.wait_ge(S("slab_hi"), n + 1 + 4 * i)
            dve.tensor_tensor(part_lo[:, n % PARTS, 0:w], raw[:, n % RAW, 0:w],
                              part_hi[:, n % PARTS, 0:w].bitcast(F32), ALU.subtract).then_inc(S("slab_lo"), 1)

        def matmul3(pe, out, a_hi, a_lo, b_hi, b_lo, start, stop):
            pe.matmul(out, a_hi, b_hi, start=start, stop=False)
            pe.matmul(out, a_hi, b_lo, start=False, stop=False)
            return pe.matmul(out, a_lo, b_hi, start=False, stop=stop)

        def rows_product(pe, name, count, cols, chunk0=0):
            for k in range(count):
                n = first[name] + k
                pe.wait_ge(S("slab_lo"), n + 1)
                for blk in range(NBLK):
                    for c, (a, b) in enumerate(cols):
                        tk = slice(blk * P, (blk + 1) * P)
                        mm = matmul3(pe, bank[2 * blk + c][:, 0:b - a], hT_hi[:, chunk0 + k, tk],
                                     hT_lo[:, chunk0 + k, tk], part_hi[:, n % PARTS, a:b],
                                     part_lo[:, n % PARTS, a:b], k == 0, k == count - 1)
                mm.then_inc(S("slab_used"), 1)

        def cols_product(pe, n, out, i=0):
            pe.wait_ge(S("slab_lo"), n + 1 + 4 * i)
            for c in range(KC):
                w = slice(c * P, (c + 1) * P)
                mm = matmul3(pe, out, part_hi[:, n % PARTS, w], part_lo[:, n % PARTS, w],
                             hT_hi[:, c, :], hT_lo[:, c, :], c == 0, c == KC - 1)
            mm.then_inc(S("slab_used"), 1)

        def norm_act(act, g):
            act.wait_ge(S("x_ready"), g + 1)
            if g == 0:
                act.wait_ge(S("x_loaded"), 16)
            for blk in range(NBLK):
                a = act.activation(h_tok[:, blk, :], x_res[:, blk, :], ACT.Square, accum_out=stat[:, g, blk:blk + 1])
            a.then_inc(S("x_squared"), 1)
            act.wait_ge(S("x_var"), g + 1)
            act.activation(stat[:, g, 2:4], stat[:, g, 0:2], ACT.Sqrt).then_inc(S("x_std"), 1)
            transposed_act(act, [norm_gain[:, g, c:c + 1] for c in range(KC)], f"n{g}")

        def norm_dve(dve, g):
            dve.wait_ge(S("x_squared"), g + 1)
            dve.tensor_scalar(stat[:, g, 0:2], stat[:, g, 0:2], 1.0 / D, EPS, ALU.mult, ALU.add).then_inc(S("x_var"), 1)
            dve.wait_ge(S("x_std"), g + 1)
            dve.reciprocal(stat[:, g, 0:2], stat[:, g, 2:4]).then_inc(S("x_rstd"), 1)
            dve.wait_ge(S("x_rstd"), g + 1)
            for blk in range(NBLK):
                a = dve.tensor_scalar(h_tok[:, blk, :], x_res[:, blk, :], stat[:, g, blk:blk + 1], None, ALU.mult)
            a.then_inc(S("h_ready"), 1)
            transposed_dve(dve, [norm_gain[:, g, c:c + 1] for c in range(KC)], f"n{g}")

        def norm_pe(pe, g):
            pe.wait_ge(S("h_ready"), g + 1)
            transposed_pe(pe, h_tok, KC, f"n{g}")

        def transposed_pe(pe, src, chunks, tag):
            for c in range(chunks):
                r, half = c // 2, c % 2
                if half == 0 and r >= 2:
                    pe.wait_ge(S(f"{tag}_lo"), min(2 * (r - 1), chunks))
                for blk in range(NBLK):
                    a = pe.transpose(bank[6 + r % 2][:, (2 * half + blk) * P:(2 * half + blk + 1) * P],
                                     src[:, blk, c * P:(c + 1) * P], ident[:, :])
                a.then_inc(S(f"{tag}_t"), 1)

        def transposed_act(act, gains, tag):
            n = len(gains)
            for c in range(n):
                act.wait_ge(S(f"{tag}_t"), min(2 * (c // 2) + 2, n))
                act.activation(hT_hi[:, c, :], bank[6 + c // 2 % 2][:, c % 2 * SEQ:(c % 2 + 1) * SEQ], ACT.Copy,
                               scale=gains[c] if gains[c] is not None else 1.0).then_inc(S(f"{tag}_hi"), 1)

        def transposed_dve(dve, gains, tag):
            n = len(gains)
            for c in range(n):
                dve.wait_ge(S(f"{tag}_hi"), min(2 * (c // 2) + 2, n))
                dve.scalar_tensor_tensor(out=hT_lo[:, c, :], in0=bank[6 + c // 2 % 2][:, c % 2 * SEQ:(c % 2 + 1) * SEQ],
                                         scalar=gains[c] if gains[c] is not None else 1.0,
                                         in1=hT_hi[:, c, :].bitcast(F32), op0=ALU.mult,
                                         op1=ALU.subtract).then_inc(S(f"{tag}_lo"), 1)

        block = ctx.enter_context(nc.Block())

        @block.sync
        def _(sp):
            for n in range(first["w_q0"]):
                load_slab(sp, plan[n][0], plan[n][1], n, plan[n][2])
                if n == 1:
                    sp.dma_start(x_res[:, :, :], t["x"].rearrange("a (b p) d -> p (a b) d", p=P)).then_inc(S("x_loaded"), 16)

            def loop(name, count):
                with sp.Fori(0, count // 4) as i:
                    for u in range(4):
                        load_slab(sp, name, 4 * i + u, first[name] + u, SLAB, i)

            for layer in range(2):
                if layer:
                    loop("pw1", 2 * KC)
                    for k in range(KC):
                        load_slab(sp, "pw2", k, first["pw2"] + k, D)
                loop(f"w_q{layer}", LISTS)
                loop(f"u{layer}", NKEYS)
                loop(f"v{layer}", NKEYS)
            sp.wait_ge(S("x_ready"), 5)
            sp.dma_start(t["out"].rearrange("a (b p) d -> p (a b) d", p=P), x_res[:, :, :]).then_inc(S("stored"), 16)
            sp.wait_ge(S("stored"), 16)

        @block.gpsimd
        def _(pool):
            small = [
                ("in_ng", norm_gain[:, 0:4, :], t["norm_gains"]),
                ("in_lg", lat_gain[:, :], t["latent_gains"]),
                ("in_pos", m_posi.bitcast(I32), t["positions"]),
                ("in_vg", m_vgain, t["gm_v_gain"].rearrange("a h d -> a (h d)").broadcast_to([P, 512])),
                ("in_qkg", m_qkgain[:, 0, :], t["mla_q_gain"].broadcast_to([P, QK])),
                ("in_qkg", m_qkgain[:, 1, :], t["mla_k_gain"].broadcast_to([P, QK])),
                ("in_ws", m_ws, t["gm_w_sT"]),
                ("in_bs", m_bs, t["gm_b_sT"]),
                ("in_taps", taps[:, :, :], t["conv_w_dwT"]),
                ("in_cc", conv_cols[:, :, :], t["conv_columns"]),
            ]
            pool.memset(ident[:, :], 0.0).then_inc(S("pool_step"), 1)
            pool.wait_ge(S("pool_step"), 1)
            pool.affine_select(out=ident[:, :], in_=ident[:, :], compare_op=ALU.not_equal, fill=1.0, base=0,
                               pattern=[[-1, P]], channel_multiplier=1).then_inc(S("c_ident"), 1)
            for s, dst, src in small:
                pool.dma_start(dst, src).then_inc(S(s), 16)
            pool.iota(iota[:, :], pattern=[[1, P]], base=0, channel_multiplier=0,
                      allow_small_or_imprecise_dtypes=True).then_inc(S("c_iota"), 1)
            pool.memset(ones[:, :], 1.0).then_inc(S("fbank_free"), 2)
            for k in range(HALF):
                f = pool.memset(m_freq[:, k:k + 1], float(np.float32(THETA) ** (-np.float32(k) / np.float32(HALF))))
            f.then_inc(S("c_freq"), 1)
            for a in range(TOPK):
                pool.memset(row_start[:, a:a + 1], float(ROW_START[a]))
                if a:
                    f = pool.memset(row_step[:, a - 1:a], float(ROW_START[a] - ROW_START[a - 1]))
            f.then_inc(S("c_rows"), 1)
            pool.memset(m_mask, 0.0).then_inc(S("pool_step"), 1)
            pool.wait_ge(S("pool_step"), 2)
            pool.affine_select(out=m_mask[:, 0:P], in_=m_mask[:, 0:P], compare_op=ALU.is_ge, fill=NEG, base=0,
                               pattern=[[-1, P]], channel_multiplier=1)
            pool.affine_select(out=m_mask[:, 2 * P:3 * P], in_=m_mask[:, 2 * P:3 * P], compare_op=ALU.is_ge, fill=NEG,
                               base=0, pattern=[[-1, P]], channel_multiplier=1).then_inc(S("c_mask"), 1)
            pool.wait_ge(S("in_ws"), 16)
            pool.affine_select(out=m_ws, in_=m_ws, compare_op=ALU.is_ge, fill=0.0, base=0,
                               pattern=[[0, GH], [1, P]], channel_multiplier=-1).then_inc(S("ws_causal"), 1)
            for layer in range(2):
                if layer:
                    pool.wait_ge(S("x_ready"), 3)
                    pool.memset(c_pad[:, :, 0:TAPS - 1], 0.0).then_inc(S("c_padded"), 1)
                    pool.dma_start(c_bias2, t["conv_b_pw2"].broadcast_to([P, D])).then_inc(S("in_b2"), 16)
                else:
                    pool.wait_ge(S("x_ready"), 2)
                pool.dma_start(keysT, t["peer_keysT"][layer]).then_inc(S("in_keys"), 16)

        def conv_act(act):
            n0 = first["pw1"]
            norm_act(act, 2)
            with act.Fori(0, KC // 2) as i:
                for u in range(2):
                    split_hi(act, n0 + 2 * u + 1, i)
                    split_hi(act, n0 + 2 * u + 2, i)
                    act.wait_ge(S("slab_used"), n0 + 2 * u + 2 + 4 * i)
                    act.wait_ge(S("sig_free"), 2 * i + u + 1)
                    act.activation(c_sig[:, u, :], bank[5 + 2 * u][:, 0:SEQ], ACT.Sigmoid,
                                   bias=conv_cols[:, 1, bass.ds(2 * i + u, 1)]).then_inc(S("sig_ready"), 1)
            act.wait_ge(S("conv_done"), 1)
            act.activation(c_sq, c_acc, ACT.Square).then_inc(S("conv_squared"), 1)
            act.wait_ge(S("conv_var"), 1)
            act.activation(c_std, c_std, ACT.Sqrt).then_inc(S("conv_std"), 1)
            act.wait_ge(S("conv_normed"), 1)
            act.activation(c_acc, c_sq, ACT.Silu).then_inc(S("conv_silu"), 1)
            act.wait_ge(S("conv_silu"), 1)
            act.activation(hT_hi[:, :, :], c_acc, ACT.Copy).then_inc(S("conv_hi"), 1)
            for k in range(KC):
                split_hi(act, first["pw2"] + k + 1)

        def peer_act(act, layer):
            norm_act(act, 1 + 2 * layer)
            nq, nu, nv = first[f"w_q{layer}"], first[f"u{layer}"], first[f"v{layer}"]
            with act.Fori(0, 2) as i:
                for u in range(8):
                    split_hi(act, nq + u + 1, 2 * i)
                    act.wait_ge(S("slab_used"), nq + u + 1 + 8 * i)
                    if u >= 2:
                        act.wait_ge(S(f"scored{layer}"), 8 * i + u - 1)
                    act.activation(qT[:, u % 2, :], bank[4 + u % 2][:, 0:SEQ], ACT.Copy).then_inc(S("fbank_free"), 1)
                    if u in (4, 7):
                        r = u // 4 - (u == 4)
                        act.wait_ge(S(f"scored{layer}"), 8 * i + (4 if u == 4 else 8))
                        for blk in range(NBLK):
                            a = act.activation(scores[:, bass.ds(blk * PH + 4 * i + 2 * r, 2), :],
                                               bank[2 * r + blk][:, :].rearrange("p (h n) -> p h n", h=2), ACT.Copy)
                        a.then_inc(S(f"scores_out{layer}"), 1)

            def experts(a, b):
                with act.Fori(a, b) as i:
                    for u in range(4):
                        split_hi(act, nu + u + 1, i)
                        act.wait_ge(S("slab_used"), nu + u + 1 + 4 * i)
                        act.activation(act_all[:, bass.ds(4 * i + u, 1), :], bank[4 + u % 2][:, 0:SEQ].rearrange("p (a t) -> p a t", a=1),
                                       ACT.Gelu_apprx_tanh).then_inc(S("fbank_free"), 1)

            experts(0, UNITS)
            act.wait_ge(S(f"gate_shift{layer}"), 1)
            act.activation(pick_s[:, :, :], pick_s[:, :, :], ACT.Exp).then_inc(S(f"gate_exp{layer}"), 1)
            experts(UNITS, 2 * UNITS)

            act.wait_ge(S(f"gated{layer}"), 64)

            def values(i):
                for u in range(4):
                    if not (isinstance(i, int) and i == 0 and u < 2):
                        act.wait_ge(S("slab_used"), nv + u - 1 + 4 * i)
                    else:
                        act.wait_ge(S("slab_used"), nv)
                    act.activation(hT_hi[:, u % 2, :], act_all[:, bass.ds(4 * i + u, 1), :].rearrange("p a t -> p (a t)"),
                                   ACT.Copy).then_inc(S(f"w_hi{layer}"), 1)
                    split_hi(act, nv + u + 1, i)

            values(0)
            with act.Fori(1, NKEYS // 4 - 1) as i:
                values(i)
            values(NKEYS // 4 - 1)

        @block.scalar
        def _(act):
            act.wait_ge(S("in_ng"), 16)
            split_hi(act, 0)
            norm_act(act, 0)

            for k in range(KC):
                split_hi(act, first["w_in_gm"] + k + 1)
            act.wait_ge(S("slab_used"), KC)
            for dst, c in ((m_u, 0), (m_v, 1)):
                for blk in range(NBLK):
                    act.activation(dst[:, blk, :], bank[2 * blk + c][:, :], ACT.Gelu_apprx_tanh).then_inc(S("gm_gelu"), 1)
            for k in range(KC):
                split_hi(act, first["w_in_lat"] + k + 1)
            act.wait_ge(S("slab_used"), 2 * KC)
            for blk in range(NBLK):
                act.activation(m_lat[:, blk, 0:512], bank[2 * blk][:, :], ACT.Copy)
                a = act.activation(m_lat[:, blk, 512:LAT], bank[2 * blk + 1][:, 0:LAT - 512], ACT.Copy)
            a.then_inc(S("lat_ready"), 1)
            act.wait_ge(S("lat_ready"), 1)
            for blk in range(NBLK):
                act.activation(m_sq[:, blk, 0:4, :], m_lat[:, blk, 0:QRANK], ACT.Square, accum_out=m_st[:, 0, blk:blk + 1])
                a = act.activation(m_sq[:, 2 + blk, 0:4, 0:64], m_lat[:, blk, QRANK:QRANK + KVRANK], ACT.Square,
                                   accum_out=m_st[:, 0, 2 + blk:3 + blk])
            a.then_inc(S("lat_squared"), 1)
            act.wait_ge(S("lat_var"), 1)
            act.activation(m_st[:, 2, 0:4], m_st[:, 1, 0:4], ACT.Sqrt).then_inc(S("lat_std"), 1)
            act.wait_ge(S("gm_var"), 1)
            act.activation(m_st[:, 4, 0:16], m_st[:, 3, 0:16], ACT.Sqrt).then_inc(S("gm_std"), 1)
            act.wait_ge(S("ang_ready"), 1)
            act.activation(m_ang[:, 6:8, :, :], m_ang[:, 4:6, :, :], ACT.Sin).then_inc(S("sincos"), 1)
            act.wait_ge(S("slab_used"), 2 * KC)
            transposed_act(act, [lat_gain[:, c:c + 1] for c in range(QCH + KVCH)], "lt")

            for k in range(QCH):
                split_hi(act, first["w_uq"] + k + 1)
            act.wait_ge(S("slab_used"), first["w_ukv"])
            for blk in range(NBLK):
                for c in range(2):
                    a = act.activation(m_qk[:, 2 * blk, 4 * c:4 * c + 4, :], bank[2 * blk + c][:, 0:4 * QK], ACT.Copy)
            a.then_inc(S("q_ready"), 1)
            for k in range(KVCH):
                split_hi(act, first["w_ukv"] + k + 1)
            act.wait_ge(S("slab_used"), first["w_out"])
            for blk in range(NBLK):
                for c in range(2):
                    kv = bank[2 * blk + c][:, :].rearrange("p (h e) -> p h e", e=NOPE + VD)
                    act.activation(m_qk[:, 2 * blk + 1, 4 * c:4 * c + 4, 0:NOPE], kv[:, :, 0:NOPE], ACT.Copy)
                    a = act.activation(m_val[:, blk, 4 * c:4 * c + 4, :], kv[:, :, NOPE:], ACT.Copy)
            a.then_inc(S("kv_ready"), 1)
            act.wait_ge(S("kv_ready"), 1)
            act.wait_ge(S("k_pe"), 1)
            act.activation(m_sq, m_qk, ACT.Square).then_inc(S("qk_squared"), 1)
            act.wait_ge(S("qk_var"), 1)
            act.activation(m_st[:, 2, :], m_st[:, 1, :], ACT.Sqrt).then_inc(S("qk_std"), 1)
            for r in range(8):
                act.wait_ge(S("qkT_t"), r + 1)
                blk, which, half = r // 4, r // 2 % 2, r % 2
                act.activation(m_qkT[0:QK, which, 4 * half:4 * half + 4, blk * P:(blk + 1) * P],
                               bank[6 + r % 2][0:QK, :].rearrange("p (h t) -> p h t", t=P), ACT.Copy).then_inc(S("qkT"), 1)
            for h in range(MH):
                act.wait_ge(S("s_max"), h + 1)
                for blk, (a0, a1) in enumerate(((0, P), (P, 3 * P))):
                    a = act.activation(m_p[:, h, a0:a1], m_p[:, h, a0:a1], ACT.Exp, bias=m_st[:, 5 + blk, h:h + 1],
                                       accum_out=m_st[:, 7, blk * MH + h:blk * MH + h + 1])
                a.then_inc(S("probs"), 1)
            for h in range(MH):
                act.wait_ge(S("pT_t"), h + 1)
                act.activation(m_pT[:, h, :, :], bank[6 + h % 2][:, 0:3 * P].rearrange("p (a t) -> p a t", t=P),
                               ACT.Copy).then_inc(S("pT"), 1)
            transposed_act(act, [None] * KC, "ct")
            for k in range(KC):
                split_hi(act, first["w_out"] + k + 1)

            for layer in range(2):
                if layer:
                    conv_act(act)
                peer_act(act, layer)

        def add_banks(dve, n):
            dve.wait_ge(S("slab_used"), n)
            for blk in range(NBLK):
                for c in range(2):
                    a = dve.tensor_tensor(x_res[:, blk, 512 * c:512 * (c + 1)], bank[2 * blk + c][:, :],
                                          x_res[:, blk, 512 * c:512 * (c + 1)], ALU.add)
            a.then_inc(S("x_ready"), 1)

        def conv_dve(dve):
            n0 = first["pw1"]
            norm_dve(dve, 2)
            dve.wait_ge(S("in_taps"), 16)
            dve.wait_ge(S("in_cc"), 16)
            dve.wait_ge(S("c_padded"), 1)
            dve.memset(c_sig, 0.0).then_inc(S("sig_free"), 2)
            with dve.Fori(0, KC // 2) as i:
                for u in range(2):
                    split_lo(dve, n0 + 2 * u + 1, i)
                    split_lo(dve, n0 + 2 * u + 2, i)
                    c = 2 * i + u
                    dve.wait_ge(S("sig_ready"), c + 1)
                    dve.scalar_tensor_tensor(out=c_pad[:, bass.ds(c, 1), TAPS - 1:].rearrange("p a t -> p (a t)"),
                                             in0=bank[4 + 2 * u][:, 0:SEQ], scalar=conv_cols[:, 0, bass.ds(c, 1)],
                                             in1=c_sig[:, u, :], op0=ALU.add, op1=ALU.mult).then_inc(S("sig_free"), 1)
                    dve.wait_ge(S("sig_free"), c + 3)
                    acc = c_acc[:, bass.ds(c, 1), :].rearrange("p a t -> p (a t)")
                    for k in range(TAPS):
                        z = c_pad[:, bass.ds(c, 1), k:k + SEQ].rearrange("p a t -> p (a t)")
                        w = taps[:, bass.ds(c, 1), k:k + 1].rearrange("p a t -> p (a t)")
                        if k == 0:
                            a = dve.tensor_scalar(acc, z, w, conv_cols[:, 2, bass.ds(c, 1)], ALU.mult, ALU.add)
                        else:
                            dve.wait_ge(S("tap_done"), TAPS * c + k)
                            a = dve.scalar_tensor_tensor(out=acc, in0=z, scalar=w, in1=acc, op0=ALU.mult, op1=ALU.add)
                        a.then_inc(S("tap_done"), 1)
            dve.wait_ge(S("tap_done"), TAPS * KC)
            dve.tensor_copy(stat[:, 4, 0:1], c_acc[:, 0, 0:1]).then_inc(S("conv_done"), 1)
            dve.wait_ge(S("conv_summed"), 1)
            dve.tensor_scalar(c_std, bank[4][:, 0:SEQ], 1.0 / D, EPS, ALU.mult, ALU.add).then_inc(S("conv_var"), 1)
            dve.wait_ge(S("conv_std"), 1)
            dve.reciprocal(c_rstd, c_std).then_inc(S("conv_rstd"), 1)
            dve.wait_ge(S("conv_rstd"), 1)
            for c in range(KC):
                a = dve.scalar_tensor_tensor(out=c_sq[:, c, :], in0=c_acc[:, c, :], scalar=conv_cols[:, 3, c:c + 1],
                                             in1=c_rstd, op0=ALU.mult, op1=ALU.mult)
            a.then_inc(S("conv_normed"), 1)
            dve.wait_ge(S("conv_hi"), 1)
            dve.tensor_tensor(hT_lo[:, :, :], c_acc, hT_hi[:, :, :].bitcast(F32), ALU.subtract).then_inc(S("conv_lo"), 1)
            dve.wait_ge(S("in_b2"), 16)
            for blk in range(NBLK):
                a = dve.tensor_tensor(x_res[:, blk, :], x_res[:, blk, :], c_bias2, ALU.add)
            a.then_inc(S("bias2_added"), 1)
            for k in range(KC):
                split_lo(dve, first["pw2"] + k + 1)
            dve.wait_ge(S("bias2_added"), 1)
            add_banks(dve, first["w_q1"])

        def peer_dve(dve, layer):
            norm_dve(dve, 1 + 2 * layer)
            nq, nu, nv = first[f"w_q{layer}"], first[f"u{layer}"], first[f"v{layer}"]
            with dve.Fori(0, LISTS // 4) as i:
                for u in range(4):
                    split_lo(dve, nq + u + 1, i)

            STEPS = 33
            picked = S(f"picked{layer}")
            dve.wait_ge(S(f"scores_out{layer}"), 4)
            dve.wait_ge(S("c_rows"), 1)
            dve.wait_ge(S("c_iota"), 1)
            with dve.Fori(0, UNITS) as i:
                done = [0]

                def step(ins):
                    done[0] += 1
                    ins.then_inc(picked, 1)
                    return done[0]

                def after(n):
                    dve.wait_ge(picked, STEPS * i + n)

                def after8(n):
                    dve.wait_ge(picked, STEPS * i + n)
                    dve.sem_inc(S("waits_passed"), 1)

                split_lo(dve, nu + 1, i)
                after8(step(dve.tensor_copy(stage, scores[:, bass.ds(i, 1), :].rearrange("p a (c n) -> p (a c) n", c=2))))
                v8 = [step(dve.max(top_v[:, c, 0:8], stage[:, c, :])) for c in range(2)]
                for c in range(2):
                    after8(v8[c])
                    step(dve.max_index(top_iu[:, c, 0:8], top_v[:, c, 0:8], stage[:, c, :]))
                r8 = []
                for c in range(2):
                    after8(done[0] - 1)
                    r8.append(step(dve.match_replace(stage[:, c, :], top_v[:, c, 0:8], stage[:, c, :], -3e38)))
                split_lo(dve, nu + 2, i)
                v16 = []
                for c in range(2):
                    after8(r8[c])
                    v16.append(step(dve.max(top_v[:, c, 8:16], stage[:, c, :])))
                for c in range(2):
                    after8(v16[c])
                    f = step(dve.max_index(top_iu[:, c, 8:16], top_v[:, c, 8:16], stage[:, c, :]))
                at = 0
                for a0, rows, cols in ROWS:
                    c = step(dve.tensor_tensor(
                        cand[:, at:at + rows * cols].rearrange("p (a b) -> p a b", b=cols),
                        top_v[:, 0, a0:a0 + rows].unsqueeze(2).broadcast_to([P, rows, cols]),
                        top_v[:, 1, 0:cols].unsqueeze(1).broadcast_to([P, rows, cols]), ALU.add))
                    at += rows * cols
                after8(f)
                step(dve.tensor_copy(top_if, top_iu))
                after8(c)
                b = step(dve.max(best_v[:, 0:8], cand))
                after8(b)
                step(dve.max_index(best_pu[:, 0:8], best_v[:, 0:8], cand))
                after8(done[0])
                b = step(dve.match_replace(cand, best_v[:, 0:8], cand, -3e38))
                split_lo(dve, nu + 3, i)
                after8(b)
                b = step(dve.max(best_v[:, 8:16], cand))
                after8(b)
                b = step(dve.max_index(best_pu[:, 8:16], best_v[:, 8:16], cand))
                d = step(dve.tensor_tensor(step_i[:, 0:15], top_if[:, 0, 1:16], top_if[:, 0, 0:15], ALU.subtract))
                after(b)
                b = step(dve.tensor_copy(best_p, best_pu))
                after(b)
                ge = step(dve.tensor_tensor(dec_ge[:, :, 0:15], best_p.unsqueeze(2).broadcast_to([P, TOPK, 15]),
                                            row_start[:, 1:16].unsqueeze(1).broadcast_to([P, TOPK, 15]), ALU.is_ge))
                step(dve.tensor_copy(pick_s[:, bass.ds(i, 1), :], best_v.unsqueeze(1)))
                after(ge)
                m1 = step(dve.tensor_tensor(dec_m[:, :, 0:15], dec_ge[:, :, 0:15],
                                            row_step[:, :].unsqueeze(1).broadcast_to([P, TOPK, 15]), ALU.mult))
                m2 = step(dve.tensor_tensor(dec_n[:, :, 0:15], dec_ge[:, :, 0:15],
                                            step_i[:, 0:15].unsqueeze(1).broadcast_to([P, TOPK, 15]), ALU.mult))
                split_lo(dve, nu + 4, i)
                after(m1)
                r1 = step(dve.tensor_reduce(sum_r, dec_m[:, :, 0:15], AX.X, ALU.add))
                after(m2)
                r2 = step(dve.tensor_reduce(sum_i, dec_n[:, :, 0:15], AX.X, ALU.add))
                after(r1)
                b = step(dve.tensor_tensor(col_b, best_p, sum_r, ALU.subtract))
                after(r2)
                step(dve.tensor_scalar(pick_i[:, bass.ds(i, 1), :], sum_i.unsqueeze(1), top_if[:, 0, 0:1], None, ALU.add))
                after(b)
                e = step(dve.tensor_tensor(dec_e, col_b.unsqueeze(2).broadcast_to([P, TOPK, TOPK]),
                                           iota[:, 0:TOPK].unsqueeze(1).broadcast_to([P, TOPK, TOPK]), ALU.is_equal))
                after(e)
                e = step(dve.tensor_tensor(dec_m, dec_e, top_if[:, 1, :].unsqueeze(1).broadcast_to([P, TOPK, TOPK]), ALU.mult))
                after(e)
                step(dve.tensor_reduce(pick_j[:, bass.ds(i, 1), :], dec_m, AX.X, ALU.add))
                assert done[0] == STEPS
                after(STEPS)

            dve.tensor_tensor(pick_s[:, :, 1:16], pick_s[:, :, 1:16], pick_s[:, :, 0:1].broadcast_to([P, UNITS, 15]),
                              ALU.subtract).then_inc(S(f"g_a{layer}"), 1)
            dve.wait_ge(S(f"g_a{layer}"), 1)
            dve.tensor_tensor(pick_s[:, :, 0:1], pick_s[:, :, 0:1], pick_s[:, :, 0:1],
                              ALU.subtract).then_inc(S(f"gate_shift{layer}"), 1)
            dve.wait_ge(S(f"gate_exp{layer}"), 1)
            dve.tensor_reduce(gate_sum[:, 0, :], pick_s[:, :, :], AX.X, ALU.add).then_inc(S(f"g_b{layer}"), 1)
            dve.wait_ge(S(f"g_b{layer}"), 1)
            dve.reciprocal(gate_sum[:, 1, :], gate_sum[:, 0, :]).then_inc(S(f"g_c{layer}"), 1)
            dve.wait_ge(S(f"g_c{layer}"), 1)
            dve.tensor_tensor(pick_s[:, :, :], pick_s[:, :, :],
                              gate_sum[:, 1, :].unsqueeze(2).broadcast_to([P, UNITS, TOPK]),
                              ALU.mult).then_inc(S(f"gates{layer}"), 1)

            with dve.Fori(UNITS, 2 * UNITS) as i:
                for u in range(4):
                    split_lo(dve, nu + u + 1, i)

            dve.wait_ge(S(f"pickT_t{layer}"), 1)
            dve.tensor_copy(pickT[:, 0:2, :], bank[6][:, :].rearrange("p (a t) -> p a t", t=SEQ))
            dve.tensor_copy(pickT[:, 2, :], bank[7][:, 0:SEQ]).then_inc(S(f"pickT{layer}"), 1)
            dve.wait_ge(S(f"pickT{layer}"), 1)
            dve.wait_ge(S("fbank_free"), 2 + (layer + 1) * (LISTS + NKEYS))

            def hots(g, slot):
                for k in range(4):
                    tk = bass.ds(4 * g + k, 1)
                    dve.tensor_scalar(hot_i[:, slot, k, :], iota[:, :], pickT[:, 0, tk], pickT[:, 2, tk],
                                      ALU.is_equal, ALU.mult)
                    a = dve.tensor_scalar(hot_j[:, slot, k, :], iota[:, :], pickT[:, 1, tk], None, ALU.is_equal)
                a.then_inc(S(f"hots{layer}"), 1)

            def gate(g, slot):
                dve.wait_ge(S(f"gmat{layer}"), g + 1)
                a = act_all[:, :, bass.ds(4 * g, 4)]
                dve.tensor_tensor(a, bank[4 + slot][:, :].rearrange("p (t j) -> p j t", t=4), a,
                                  ALU.mult).then_inc(S(f"gated{layer}"), 1)

            hots(0, 0)
            hots(1, 1)
            with dve.Fori(0, SEQ // 8 - 1) as i:
                for u in range(2):
                    gate(2 * i + u, u)
                    hots(2 * i + u + 2, u)
            gate(SEQ // 4 - 2, 0)
            gate(SEQ // 4 - 1, 1)
            dve.wait_ge(S(f"gated{layer}"), SEQ // 4)

            def values(i):
                for u in range(4):
                    split_lo(dve, nv + u + 1, i)
                    dve.wait_ge(S(f"w_hi{layer}"), 4 * i + u + 1)
                    dve.tensor_tensor(hT_lo[:, u % 2, :], act_all[:, bass.ds(4 * i + u, 1), :].rearrange("p a t -> p (a t)"),
                                      hT_hi[:, u % 2, :].bitcast(F32), ALU.subtract).then_inc(S(f"w_lo{layer}"), 1)

            values(0)
            with dve.Fori(1, NKEYS // 4 - 1) as i:
                values(i)
            values(NKEYS // 4 - 1)
            add_banks(dve, nv + NKEYS)

        @block.vector
        def _(dve):
            dve.wait_ge(S("in_ng"), 16)
            dve.memset(stat[:, 4, :], 0.0).then_inc(S("x_ready"), 1)
            dve.wait_ge(S("x_loaded"), 16)
            split_lo(dve, 0)
            norm_dve(dve, 0)
            count = [0]

            def chain(ins):
                count[0] += 1
                ins.then_inc(S("dve_chain"), 1)
                dve.wait_ge(S("dve_chain"), count[0])

            def wide(v, n):
                return v.unsqueeze(2).broadcast_to([P, v.shape[1], n])

            for k in range(KC):
                split_lo(dve, first["w_in_gm"] + k + 1)
            dve.wait_ge(S("in_pos"), 16)
            dve.wait_ge(S("c_freq"), 1)
            chain(dve.tensor_copy(m_pos, m_posi.bitcast(I32)))
            for blk in range(NBLK):
                a = dve.tensor_scalar(m_ang[:, 0, blk, :], m_freq, m_pos[:, blk:blk + 1], None, ALU.mult)
            chain(a)
            for k, shift in ((0, 0.0), (1, 0.25)):
                magic = 1.5 * 2.0 ** 23
                chain(dve.tensor_scalar(m_ang[:, 1, :, :], m_ang[:, 0, :, :], float(1 / (2 * np.pi)), shift, ALU.mult, ALU.add))
                chain(dve.tensor_scalar(m_ang[:, 2, :, :], m_ang[:, 1, :, :], magic, None, ALU.add))
                chain(dve.tensor_scalar(m_ang[:, 2, :, :], m_ang[:, 2, :, :], magic, None, ALU.subtract))
                two_pi = 2 * np.pi
                c1 = 6.28125
                c2 = float(np.float32(np.round((two_pi - c1) * 2.0 ** 20) / 2.0 ** 20))
                c3 = float(np.float32(two_pi - c1 - c2))
                src = m_ang[:, 0, :, :]
                for c in (c1, c2, c3):
                    chain(dve.scalar_tensor_tensor(out=m_ang[:, 3, :, :], in0=m_ang[:, 2, :, :], scalar=-c, in1=src,
                                                   op0=ALU.mult, op1=ALU.add))
                    src = m_ang[:, 3, :, :]
                chain(dve.tensor_scalar(m_ang[:, 3, :, :], m_ang[:, 3, :, :], float(np.pi / 2) if k else 0.0, float(np.float32(3.1415925)), ALU.add, ALU.min))
                chain(dve.tensor_scalar(m_ang[:, 4 + k, :, :], m_ang[:, 3, :, :], -float(np.float32(3.1415925)), None, ALU.max))
            dve.tensor_copy(m_st[:, 7, 0:1], m_ang[:, 5, 0, 0:1]).then_inc(S("ang_ready"), 1)
            dve.wait_ge(S("gm_gelu"), 4)
            chain(dve.tensor_tensor(m_vsq, m_v, m_v, ALU.mult))
            chain(dve.tensor_reduce(m_st[:, 0, 16:32], m_vsq.rearrange("p a (h d) -> p (a h) d", d=GD), AX.X, ALU.add))
            dve.tensor_scalar(m_st[:, 3, 0:16], m_st[:, 0, 16:32], 1.0 / GD, EPS, ALU.mult, ALU.add).then_inc(S("gm_var"), 1)
            for k in range(KC):
                split_lo(dve, first["w_in_lat"] + k + 1)
            dve.wait_ge(S("lat_squared"), 1)
            dve.tensor_scalar(m_st[:, 1, 0:2], m_st[:, 0, 0:2], 1.0 / QRANK, EPS, ALU.mult, ALU.add)
            dve.tensor_scalar(m_st[:, 1, 2:4], m_st[:, 0, 2:4], 1.0 / KVRANK, EPS, ALU.mult, ALU.add).then_inc(S("lat_var"), 1)
            dve.wait_ge(S("lat_std"), 1)
            chain(dve.reciprocal(m_st[:, 1, 0:4], m_st[:, 2, 0:4]))
            for blk in range(NBLK):
                dve.tensor_scalar(m_lat[:, blk, 0:QRANK], m_lat[:, blk, 0:QRANK], m_st[:, 1, blk:blk + 1], None, ALU.mult)
                a = dve.tensor_scalar(m_lat[:, blk, QRANK:QRANK + KVRANK], m_lat[:, blk, QRANK:QRANK + KVRANK],
                                      m_st[:, 1, 2 + blk:3 + blk], None, ALU.mult)
            a.then_inc(S("lat_normed"), 1)
            dve.wait_ge(S("gm_std"), 1)
            chain(dve.reciprocal(m_st[:, 3, 16:32], m_st[:, 4, 0:16]))
            v3 = m_v.rearrange("p a (h d) -> p (a h) d", d=GD)
            chain(dve.tensor_tensor(v3, v3, wide(m_st[:, 3, 16:32], GD), ALU.mult))
            dve.wait_ge(S("in_vg"), 16)
            for blk in range(NBLK):
                a = dve.tensor_tensor(m_v[:, blk, :], m_v[:, blk, :], m_vgain, ALU.mult)
            a.then_inc(S("v_normed"), 1)
            transposed_dve(dve, [lat_gain[:, c:c + 1] for c in range(QCH + KVCH)], "lt")
            for k in range(QCH + KVCH):
                split_lo(dve, first["w_uq"] + k + 1)
            dve.wait_ge(S("lat_ready"), 1)
            for blk in range(NBLK):
                a = dve.tensor_copy(m_qk[:, 2 * blk + 1, :, NOPE:],
                                    m_lat[:, blk, LAT - ROPE:LAT].unsqueeze(1).broadcast_to([P, MH, ROPE]))
            a.then_inc(S("k_pe"), 1)
            dve.wait_ge(S("mixed"), 1)
            dve.wait_ge(S("in_bs"), 16)
            for blk in range(NBLK):
                a = dve.tensor_tensor(m_cat[:, blk, 0:512].rearrange("p (h d) -> p h d", d=GD),
                                      bank[4 + blk][:, :].rearrange("p (h d) -> p h d", d=GD), wide(m_bs, GD), ALU.add)
            chain(a)
            a = dve.tensor_tensor(m_cat[:, :, 0:512], m_cat[:, :, 0:512], m_u, ALU.mult)
            a.then_inc(S("gm_done"), 1)
            dve.wait_ge(S("qk_squared"), 1)
            chain(dve.tensor_reduce(m_st[:, 0, :], m_sq.rearrange("p a h d -> p (a h) d"), AX.X, ALU.add))
            dve.tensor_scalar(m_st[:, 1, :], m_st[:, 0, :], 1.0 / QK, EPS, ALU.mult, ALU.add).then_inc(S("qk_var"), 1)
            dve.wait_ge(S("qk_std"), 1)
            chain(dve.reciprocal(m_st[:, 0, :], m_st[:, 2, :]))
            qk3 = m_qk.rearrange("p a h d -> p (a h) d")
            chain(dve.tensor_tensor(qk3, qk3, wide(m_st[:, 0, :], QK), ALU.mult))
            dve.wait_ge(S("in_qkg"), 32)
            for b in range(2 * NBLK):
                a = dve.tensor_tensor(m_qk[:, b, :, :], m_qk[:, b, :, :],
                                      m_qkgain[:, b % 2, :].unsqueeze(1).broadcast_to([P, MH, QK]), ALU.mult)
            chain(a)
            dve.wait_ge(S("sincos"), 1)
            for blk in range(NBLK):
                rows = qk3[:, 16 * blk:16 * blk + 16, :]
                x1, x2 = rows[:, :, NOPE:NOPE + HALF], rows[:, :, NOPE + HALF:QK]
                sin = m_ang[:, 6, blk, :].unsqueeze(1).broadcast_to([P, 16, HALF])
                cos = m_ang[:, 7, blk, :].unsqueeze(1).broadcast_to([P, 16, HALF])
                for k, (xx, cs) in enumerate(((x1, cos), (x2, sin), (x1, sin), (x2, cos))):
                    a = dve.tensor_tensor(m_rt[:, k, :, :], xx, cs, ALU.mult)
                chain(a)
                dve.tensor_tensor(x1, m_rt[:, 0, :, :], m_rt[:, 1, :, :], ALU.subtract)
                chain(dve.tensor_tensor(x2, m_rt[:, 2, :, :], m_rt[:, 3, :, :], ALU.add))
                dve.tensor_copy(m_st[:, 7, blk:blk + 1], qk3[:, 16 * blk, 0:1]).then_inc(S("roped"), 1)
            dve.wait_ge(S("c_mask"), 1)
            for h in range(MH):
                dve.wait_ge(S("s_ready"), h + 1)
                chain(dve.scalar_tensor_tensor(out=m_p[:, h, :], in0=bank[4 + h % 2][:, 0:3 * P], scalar=float(QK) ** -0.5,
                                               in1=m_mask, op0=ALU.mult, op1=ALU.add))
                dve.tensor_reduce(m_st[:, 5, h:h + 1], m_p[:, h, 0:P], AX.X, ALU.max, negate=True)
                dve.tensor_reduce(m_st[:, 6, h:h + 1], m_p[:, h, P:3 * P], AX.X, ALU.max, negate=True).then_inc(S("s_max"), 1)
            dve.wait_ge(S("probs"), MH)
            chain(dve.reciprocal(m_st[:, 4, 0:16], m_st[:, 7, 0:16]))
            dve.wait_ge(S("attended"), 1)
            for blk in range(NBLK):
                a = dve.tensor_tensor(m_cat[:, blk, 512:1024].rearrange("p (h d) -> p h d", d=VD),
                                      bank[4 + blk][:, :].rearrange("p (h d) -> p h d", d=VD),
                                      wide(m_st[:, 4, blk * MH:(blk + 1) * MH], VD), ALU.mult)
            a.then_inc(S("cat_ready"), 1)
            transposed_dve(dve, [None] * KC, "ct")
            for k in range(KC):
                split_lo(dve, first["w_out"] + k + 1)
            add_banks(dve, first["w_q0"])

            for layer in range(2):
                if layer:
                    conv_dve(dve)
                peer_dve(dve, layer)

        def conv_pe(pe):
            n0 = first["pw1"]
            norm_pe(pe, 2)
            pe.wait_ge(S("n2_lo"), KC)
            with pe.Fori(0, KC // 2) as i:
                for u in range(2):
                    pe.wait_ge(S("sig_free"), 2 * i + u + 1)
                    cols_product(pe, n0 + 2 * u, bank[4 + 2 * u][:, 0:SEQ], i)
                    cols_product(pe, n0 + 2 * u + 1, bank[5 + 2 * u][:, 0:SEQ], i)
            pe.wait_ge(S("conv_squared"), 1)
            for c in range(KC):
                a = pe.matmul(bank[4][:, 0:SEQ], ones[:, :], c_sq[:, c, :], start=c == 0, stop=c == KC - 1)
            a.then_inc(S("conv_summed"), 1)
            pe.wait_ge(S("conv_lo"), 1)
            rows_product(pe, "pw2", KC, [(0, 512), (512, 1024)])

        def peer_pe(pe, layer):
            norm_pe(pe, 1 + 2 * layer)
            nq, nu, nv = first[f"w_q{layer}"], first[f"u{layer}"], first[f"v{layer}"]
            base = layer * (LISTS + NKEYS)
            pe.wait_ge(S(f"n{1 + 2 * layer}_lo"), KC)
            pe.wait_ge(S("in_keys"), 16 * (layer + 1))
            if layer:
                pe.wait_ge(S("conv_var"), 1)

            with pe.Fori(0, 2) as i:
                def query(u):
                    pe.wait_ge(S("fbank_free"), base + 8 * i + u + 1)
                    cols_product(pe, nq + u, bank[4 + u % 2][:, 0:SEQ], 2 * i)

                def score(u):
                    pe.wait_ge(S("fbank_free"), base + 8 * i + u + 3)
                    for blk in range(NBLK):
                        a = pe.matmul(bank[2 * (u // 4) + blk][:, u % 4 * P:(u % 4 + 1) * P],
                                      qT[:, u % 2, blk * P:(blk + 1) * P],
                                      keysT[:, bass.ds(8 * i + u, 1), :].rearrange("p a n -> p (a n)"), start=True, stop=True)
                    a.then_inc(S(f"scored{layer}"), 1)

                query(0)
                for u in range(1, 8):
                    query(u)
                    score(u - 1)
                score(7)
                pe.wait_ge(S(f"scores_out{layer}"), 2 * i + 2)

            with pe.Fori(0, NKEYS // 4) as i:
                for u in range(4):
                    pe.wait_ge(S("fbank_free"), base + LISTS + 4 * i + u + 1)
                    cols_product(pe, nu + u, bank[4 + u % 2][:, 0:SEQ], i)
            pe.wait_ge(S(f"gates{layer}"), 1)
            for k, src in enumerate((pick_i, pick_j, pick_s)):
                for blk in range(NBLK):
                    out = bank[6 + k // 2][:, (k % 2) * SEQ + blk * P:(k % 2) * SEQ + (blk + 1) * P]
                    a = pe.transpose(out, src[:, blk * PH:(blk + 1) * PH, :].rearrange("p h k -> p (h k)"), ident[:, :])
            a.then_inc(S(f"pickT_t{layer}"), 1)
            pe.wait_ge(S("fbank_free"), base + 2 + LISTS + NKEYS)

            def gmat(g, slot):
                pe.wait_ge(S(f"hots{layer}"), g + 1)
                for k in range(4):
                    a = pe.matmul(bank[4 + slot][:, k * P:(k + 1) * P], hot_i[:, slot, k, :], hot_j[:, slot, k, :],
                                  start=True, stop=True)
                a.then_inc(S(f"gmat{layer}"), 1)

            with pe.Fori(0, SEQ // 8) as i:
                for u in range(2):
                    gmat(2 * i + u, u)

            def values(i, begin, end):
                for u in range(4):
                    j, n = 4 * i + u, nv + u
                    pe.wait_ge(S("slab_lo"), n + 1 + 4 * i)
                    pe.wait_ge(S(f"w_lo{layer}"), j + 1)
                    for blk in range(NBLK):
                        w = slice(blk * P, (blk + 1) * P)
                        for a, b in ((hT_hi, part_hi), (hT_hi, part_lo), (hT_lo, part_hi)):
                            for c in range(2):
                                mm = pe.matmul(bank[2 * blk + c][:, :], a[:, u % 2, w],
                                               b[:, n % PARTS, 512 * c:512 * (c + 1)],
                                               start=begin and u == 0 and a is hT_hi and b is part_hi,
                                               stop=end and u == 3 and a is hT_lo)
                    mm.then_inc(S("slab_used"), 1)

            values(0, True, False)
            with pe.Fori(1, NKEYS // 4 - 1) as i:
                values(i, False, False)
            values(NKEYS // 4 - 1, False, True)

        @block.tensor
        def _(pe):
            pe.wait_ge(S("c_ident"), 1)
            norm_pe(pe, 0)
            halves = [(0, 512), (512, 1024)]
            pe.wait_ge(S("n0_lo"), KC)
            rows_product(pe, "w_in_gm", KC, halves)
            pe.wait_ge(S("gm_gelu"), 4)
            rows_product(pe, "w_in_lat", KC, [(0, 512), (512, LAT)])
            pe.wait_ge(S("lat_normed"), 1)
            transposed_pe(pe, m_lat, QCH + KVCH, "lt")
            pe.wait_ge(S("v_normed"), 1)
            pe.wait_ge(S("ws_causal"), 1)
            for blk in range(NBLK):
                for h in range(GH):
                    a = pe.matmul(bank[4 + blk][:, h * GD:(h + 1) * GD], m_ws[:, h, :], m_v[:, blk, h * GD:(h + 1) * GD],
                                  start=True, stop=True)
            a.then_inc(S("mixed"), 1)
            pe.wait_ge(S("lt_lo"), QCH + KVCH)
            rows_product(pe, "w_uq", QCH, [(0, 4 * QK), (4 * QK, 8 * QK)])
            pe.wait_ge(S("q_ready"), 1)
            rows_product(pe, "w_ukv", KVCH, halves, QCH)
            for r in range(8):
                blk, which, half = r // 4, r // 2 % 2, r % 2
                pe.wait_ge(S("roped"), blk + 1)
                if r >= 2:
                    pe.wait_ge(S("qkT"), r - 1)
                for h in range(4):
                    a = pe.transpose(bank[6 + r % 2][0:QK, h * P:(h + 1) * P], m_qk[:, 2 * blk + which, 4 * half + h, :],
                                     ident[:, :])
                a.then_inc(S("qkT_t"), 1)
            pe.wait_ge(S("qkT"), 8)
            pe.wait_ge(S("gm_done"), 1)
            for h in range(MH):
                if h >= 2:
                    pe.wait_ge(S("s_max"), h - 1)
                q, k = m_qkT[0:QK, 0, h, :], m_qkT[0:QK, 1, h, :]
                pe.matmul(bank[4 + h % 2][:, 0:P], q[:, 0:P], k[:, 0:P], start=True, stop=True)
                pe.matmul(bank[4 + h % 2][:, P:3 * P], q[:, P:2 * P], k, start=True, stop=True).then_inc(S("s_ready"), 1)
            for h in range(MH):
                pe.wait_ge(S("probs"), h + 1)
                if h >= 2:
                    pe.wait_ge(S("pT"), h - 1)
                for c in range(3):
                    a = pe.transpose(bank[6 + h % 2][:, c * P:(c + 1) * P], m_p[:, h, c * P:(c + 1) * P], ident[:, :])
                a.then_inc(S("pT_t"), 1)
            pe.wait_ge(S("s_max"), MH)
            for h in range(MH):
                pe.wait_ge(S("pT"), h + 1)
                o = slice(h * VD, (h + 1) * VD)
                pe.matmul(bank[4][:, o], m_pT[:, h, 0, :], m_val[:, 0, h, :], start=True, stop=True)
                pe.matmul(bank[5][:, o], m_pT[:, h, 1, :], m_val[:, 0, h, :], start=True, stop=False)
                a = pe.matmul(bank[5][:, o], m_pT[:, h, 2, :], m_val[:, 1, h, :], start=False, stop=True)
            a.then_inc(S("attended"), 1)
            pe.wait_ge(S("cat_ready"), 1)
            transposed_pe(pe, m_cat, KC, "ct")
            pe.wait_ge(S("ct_lo"), KC)
            rows_product(pe, "w_out", KC, halves)

            for layer in range(2):
                if layer:
                    conv_pe(pe)
                peer_pe(pe, layer)

def kernel(**inputs):
    import numpy as _np
    import concourse.bacc as _bacc
    from concourse import mybir as _mybir
    from concourse.bass_utils import run_bass_kernel_spmd as _run

    a = {k: _np.asarray(v) for k, v in inputs.items()}

    def columns(w):
        return w.reshape(8, 128, 16, 128).transpose(2, 1, 0, 3).reshape(16, 128, 1024)

    pw1 = columns(a["conv_w_pw1"][0]).reshape(2, 8, 128, 1024).transpose(1, 0, 2, 3).reshape(16, 128, 1024)
    arrays = {k: a[k] for k in (
        "x", "w_in", "gm_v_gain", "mla_w_uq", "mla_w_ukv", "mla_q_gain", "mla_k_gain", "w_out", "conv_w_pw2",
        "conv_b_pw2")}

    def on_partitions(*vectors):
        return _np.stack([v.reshape(-1, 128).T for v in vectors], axis=1)

    arrays["positions"] = a["positions"][0].reshape(2, 128).T
    arrays["norm_gains"] = on_partitions(a["mix_norm_even"][0], a["ffn_norm"][0], a["mix_norm_odd"][0], a["ffn_norm"][1])
    arrays["latent_gains"] = _np.concatenate([a["mla_q_lat_gain"][0].reshape(3, 128).T,
                                              a["mla_kv_lat_gain"][0].reshape(2, 128).T], axis=1)
    arrays["conv_columns"] = on_partitions(a["conv_b_pw1"][0, 0:1024], a["conv_b_pw1"][0, 1024:2048],
                                           a["conv_b_dw"][0], a["conv_norm_gain"][0])
    arrays["gm_w_sT"] = a["gm_w_s"][0].transpose(2, 0, 1)
    arrays["gm_b_sT"] = a["gm_b_s"][0].T
    arrays["conv_w_pw1"] = pw1
    arrays["conv_w_dwT"] = a["conv_w_dw"][0].reshape(31, 8, 128).transpose(2, 1, 0)
    arrays["peer_w_q"] = _np.stack([columns(w) for w in a["peer_w_q"]])
    arrays["peer_keysT"] = a["peer_sub_keys"].transpose(0, 4, 2, 1, 3).reshape(2, 128, 16, 128)
    arrays["peer_u"] = a["peer_u"].reshape(2, 128, 128, 8, 128).transpose(0, 2, 4, 3, 1).reshape(2, 128, 128, 1024)
    arrays["peer_v"] = a["peer_v"].reshape(2, 128, 128, 1024).transpose(0, 2, 1, 3)
    arrays = {k: _np.ascontiguousarray(v) for k, v in arrays.items()}

    nc = _bacc.Bacc("TRN2", target_bir_lowering=False, num_devices=1)
    t = {k: nc.dram_tensor(k, v.shape, _mybir.dt.from_np(v.dtype), kind="ExternalInput").ap() for k, v in arrays.items()}
    t["out"] = nc.dram_tensor("out", (1, 256, 1024), _mybir.dt.float32, kind="ExternalOutput").ap()
    build(nc, t)
    r = _run(nc, [arrays], core_ids=[0])
    return r.results[0]["out"]
```

```python
from contextlib import ExitStack

import numpy as np

import concourse.bass as bass
from concourse import mybir

ALU = mybir.AluOpType
ACT = mybir.ActivationFunctionType
AX = mybir.AxisListType
F32 = mybir.dt.float32
F32R = mybir.dt.float32r
U32 = mybir.dt.uint32
I32 = mybir.dt.int32

P = 128
D = 1024
SEQ = 256
NBLK = SEQ // P
KC = D // P
EPS = 1e-6
NEG = -1e30

GH, GD = 8, 64
MH, NOPE, ROPE, VD = 8, 64, 32, 64
QK = NOPE + ROPE
HALF = ROPE // 2
QRANK, KVRANK = 384, 256
LAT = QRANK + KVRANK + ROPE
INW = 2 * GH * GD + LAT
QCH, KVCH = QRANK // P, KVRANK // P
THETA = 10000.0

TAPS = 31

PH = 8
NKEYS = 128
TOPK = 16
LISTS = 2 * PH
UNITS = NBLK * PH
ROWS = [(0, 1, 16), (1, 3, 8), (4, 12, 3)]
ROW_START = [0] + [16 + 8 * (a - 1) for a in range(1, 4)] + [40 + 3 * (a - 4) for a in range(4, 16)]
CANDS = 76
PICK_SLABS = 96

RAW = 4
PARTS = 4
AHEAD = 3
W_SLOTS = 4
PE_CONV = 3
DVE_CONV = KC - PE_CONV
SLAB = 1024


def slab_plan():
    plan, first = [], {}

    def add(name, count, width):
        first[name] = len(plan)
        plan.extend((name, k, width) for k in range(count))

    add("w_in_gm", KC, 1024)
    add("w_in_lat", KC, LAT)
    add("w_uq", QCH, MH * QK)
    add("w_ukv", KVCH, MH * (NOPE + VD))
    add("w_out", KC, D)
    for layer in range(2):
        if layer:
            add("pw1", 2 * KC, SLAB)
            add("pw2", KC, D)
        add(f"w_q{layer}", LISTS, SLAB)
        add(f"u{layer}", NKEYS, SLAB)
        add(f"v{layer}", NKEYS, SLAB)
    return plan, first


def build(nc, t):
    plan, first = slab_plan()
    NSLAB = len(plan)

    ctx = ExitStack()
    with ctx:
        def sb(name, shape, dt=F32):
            return ctx.enter_context(nc.sbuf_tensor(name, shape, dt))

        sems = {}

        def S(name):
            if name not in sems:
                sems[name] = ctx.enter_context(nc.semaphore(name))
            return sems[name]

        big = sb("big", [P, NKEYS * SEQ])
        x_res = sb("x_res", [P, NBLK, D])
        hT_hi = sb("hT_hi", [P, KC, SEQ], F32R)
        hT_lo = sb("hT_lo", [P, KC, SEQ], F32R)
        raw = sb("raw", [P, RAW, SLAB])
        part_hi = sb("part_hi", [P, PARTS, SLAB], F32R)
        part_lo = sb("part_lo", [P, PARTS, SLAB], F32R)
        ident = sb("ident", [P, P])
        iota = sb("iota", [P, P])
        norm_gain = sb("norm_gain", [P, 5, KC])
        lat_gain = sb("lat_gain", [P, QCH + KVCH])
        conv_cols = sb("conv_cols", [P, 4, KC])
        stat = sb("stat", [P, 4, 4])
        warm = sb("warm", [P, 2])
        pool_j = sb("pool_j", [P, 2, 2])
        act_j = sb("act_j", [P, 2, 2])
        row_start = sb("row_start", [P, TOPK])
        row_step = sb("row_step", [P, TOPK - 1])
        pick_i = sb("pick_i", [P, UNITS, TOPK])
        pick_j = sb("pick_j", [P, UNITS, TOPK])
        pick_s = sb("pick_s", [P, UNITS, TOPK])
        gate_sum = sb("gate_sum", [P, 2, UNITS])
        pickT = sb("pickT", [P, 3, SEQ])
        x_hold = nc.dram_tensor("x_hold", (P, NBLK * D), F32, kind="Internal").ap()
        hots_mem = x_res[:, :, :].rearrange("p b (s k c) -> p b s k c", s=2, c=P)
        hot_i, hot_j = hots_mem[:, 0], hots_mem[:, 1]
        bank = [ctx.enter_context(nc.psum_tensor(f"bank{b}", [P, 512], F32)) for b in range(8)]

        used = [0]

        def part_of_big(*shape):
            n = int(np.prod(shape))
            v = big[:, used[0]:used[0] + n]
            used[0] += n
            assert used[0] <= NKEYS * SEQ
            if len(shape) == 2:
                return v.rearrange("p (a b) -> p a b", b=shape[1])
            if len(shape) == 3:
                return v.rearrange("p (a b c) -> p a b c", b=shape[1], c=shape[2])
            if len(shape) == 4:
                return v.rearrange("p (a b c d) -> p a b c d", b=shape[1], c=shape[2], d=shape[3])
            return v

        m_u = part_of_big(NBLK, 512)
        m_v = part_of_big(NBLK, 512)
        m_vsq = part_of_big(NBLK, 512)
        m_lat = part_of_big(NBLK, LAT)
        m_ws = part_of_big(GH, P)
        m_vgain = part_of_big(512)
        m_qkgain = part_of_big(2, QK)
        m_bs = part_of_big(GH)
        m_qk = part_of_big(NBLK * 2, MH, QK)
        m_val = part_of_big(NBLK, MH, VD)
        m_sq = part_of_big(NBLK * 2, MH, QK)
        m_qkT = part_of_big(2, MH, SEQ)
        m_p = part_of_big(MH, 3 * P)
        m_pT = part_of_big(MH, 3, P)
        m_cat = part_of_big(NBLK, D)
        m_mask = part_of_big(3 * P)
        m_rt = part_of_big(6, 16, HALF)
        m_ang = part_of_big(8, NBLK, HALF)
        m_freq = part_of_big(HALF)
        m_posi = part_of_big(NBLK)
        m_pos = part_of_big(NBLK)
        m_st = part_of_big(8, 2 * UNITS)

        act_all = big[:, :].rearrange("p (j t) -> p j t", t=SEQ)
        used[0] = NKEYS * SEQ // 2
        h_tok = part_of_big(NBLK, D)
        qT = part_of_big(2, SEQ)
        keysT = part_of_big(LISTS, NKEYS)
        assert used[0] <= PICK_SLABS * SEQ
        used[0] = PICK_SLABS * SEQ
        scores = part_of_big(UNITS, 2 * NKEYS)
        stage = part_of_big(2, 2, NKEYS)
        top_v = part_of_big(2, 2, TOPK)
        top_iu = part_of_big(2, 2, TOPK).bitcast(U32)
        top_if = part_of_big(2, 2, TOPK)
        cand = part_of_big(2, CANDS)
        best_v = part_of_big(2, TOPK)
        best_pu = part_of_big(2, TOPK).bitcast(U32)
        best_p = part_of_big(2, TOPK)
        step_i = part_of_big(2, TOPK)
        col_b = part_of_big(2, TOPK)
        sum_i = part_of_big(2, TOPK)
        sum_r = part_of_big(2, TOPK)
        dec_ge = part_of_big(2, TOPK, TOPK)
        dec_m = part_of_big(2, TOPK, TOPK)
        dec_n = part_of_big(2, TOPK, TOPK)
        dec_e = part_of_big(2, TOPK, TOPK)
        dec_f = part_of_big(2, TOPK, TOPK)

        used[0] = 0
        c_pad = part_of_big(KC, TAPS - 1 + SEQ)
        c_sig = part_of_big(2, SEQ)
        c_acc = part_of_big(KC, SEQ)
        c_sq = part_of_big(KC, SEQ)
        c_std = part_of_big(SEQ)
        c_rstd = part_of_big(SEQ)
        c_bias2 = part_of_big(D)
        ones = part_of_big(P)
        taps = part_of_big(KC, TAPS)
        c_diag = part_of_big(PE_CONV * TAPS, P)

        def slab_src(name, k):
            if name == "w_in_gm":
                return t["w_in"][0, k * P:(k + 1) * P, 0:1024]
            if name == "w_in_lat":
                return t["w_in"][0, k * P:(k + 1) * P, 1024:INW]
            if name == "w_uq":
                return t["mla_w_uq"][0, k * P:(k + 1) * P, :]
            if name == "w_ukv":
                return t["mla_w_ukv"][0, k * P:(k + 1) * P, :]
            if name == "w_out":
                return t["w_out"][0, k * P:(k + 1) * P, :]
            if name == "pw2":
                return t["conv_w_pw2"][0, k * P:(k + 1) * P, :]
            src = {"pw1": t["conv_w_pw1"]}.get(name)
            if src is None:
                src = t[{"w_q": "peer_w_q", "u": "peer_u", "v": "peer_v"}[name[:-1]]][int(name[-1])]
            return src[bass.ds(k, 1)].rearrange("a p n -> (a p) n")

        def load_slab(sp, name, k, n, width, i=0):
            if n >= RAW:
                sp.wait_ge(S("slab_lo"), n - RAW + 1 + 4 * i)
            sp.dma_start(raw[:, n % RAW, 0:width], slab_src(name, k)).then_inc(S(f"slab_landed{n % RAW}"), 16)

        def split_hi(act, n, i=0):
            w = plan[n][2]
            act.wait_ge(S(f"slab_landed{n % RAW}"), 16 * (n // RAW + 1) + 16 * i)
            if n >= PARTS:
                act.wait_ge(S("slab_used"), n - PARTS + 1 + 4 * i)
            act.activation(part_hi[:, n % PARTS, 0:w], raw[:, n % RAW, 0:w], ACT.Copy).then_inc(S("slab_hi"), 1)

        def split_lo(dve, n, i=0):
            w = plan[n][2]
            dve.wait_ge(S("slab_hi"), n + 1 + 4 * i)
            dve.tensor_tensor(part_lo[:, n % PARTS, 0:w], raw[:, n % RAW, 0:w],
                              part_hi[:, n % PARTS, 0:w].bitcast(F32), ALU.subtract).then_inc(S("slab_lo"), 1)

        def ahead_hi(act, n, i=0):
            if not (isinstance(i, int) and n + AHEAD + 4 * i >= NSLAB):
                split_hi(act, n + AHEAD, i)

        def ahead_lo(dve, n, i=0):
            if not (isinstance(i, int) and n + AHEAD + 4 * i >= NSLAB):
                split_lo(dve, n + AHEAD, i)

        def matmul3(pe, out, a_hi, a_lo, b_hi, b_lo, start, stop):
            pe.matmul(out, a_hi, b_hi, start=start, stop=False)
            pe.matmul(out, a_hi, b_lo, start=False, stop=False)
            return pe.matmul(out, a_lo, b_hi, start=False, stop=stop)

        def rows_product(pe, name, count, cols, chunk0=0, ready=None):
            for k in range(count):
                n = first[name] + k
                pe.wait_ge(S("slab_lo"), n + 1)
                if ready:
                    pe.wait_ge(S(ready), chunk0 + k + 1)
                for blk in range(NBLK):
                    for c, (a, b) in enumerate(cols):
                        tk = slice(blk * P, (blk + 1) * P)
                        mm = matmul3(pe, bank[2 * blk + c][:, 0:b - a], hT_hi[:, chunk0 + k, tk],
                                     hT_lo[:, chunk0 + k, tk], part_hi[:, n % PARTS, a:b],
                                     part_lo[:, n % PARTS, a:b], k == 0, k == count - 1)
                mm.then_inc(S("slab_used"), 1)

        def cols_product(pe, n, out, i=0):
            pe.wait_ge(S("slab_lo"), n + 1 + 4 * i)
            for c in range(KC):
                w = slice(c * P, (c + 1) * P)
                mm = matmul3(pe, out, part_hi[:, n % PARTS, w], part_lo[:, n % PARTS, w],
                             hT_hi[:, c, :], hT_lo[:, c, :], c == 0, c == KC - 1)
            mm.then_inc(S("slab_used"), 1)

        def norm_act(act, g):
            act.activation(warm[:, 0:1], warm[:, 1:2], ACT.Sqrt)
            if g == 0:
                act.wait_ge(S("x_loaded"), 16)
            else:
                act.wait_ge(S("x_half_ready"), g)
            act.activation(h_tok[:, 0, :], x_res[:, 0, :], ACT.Square, accum_out=stat[:, g, 0:1]).then_inc(S("x_squared"), 1)
            act.wait_ge(S("x_var"), g + 1)
            act.activation(stat[:, g, 2:4], stat[:, g, 0:2], ACT.Sqrt).then_inc(S("x_std"), 1)
            transposed_act(act, [norm_gain[:, g, c:c + 1] for c in range(KC)], f"n{g}")

        def norm_dve(dve, g):
            if g == 0:
                dve.wait_ge(S("x_loaded"), 16)
            else:
                dve.wait_ge(S("x_ready"), g)
            dve.tensor_tensor_reduce(h_tok[:, 1, :], x_res[:, 1, :], x_res[:, 1, :], 1.0, 0.0, ALU.mult, ALU.add,
                                     stat[:, g, 1:2]).then_inc(S("x_squared1"), 1)
            dve.wait_ge(S("x_squared"), g + 1)
            dve.wait_ge(S("x_squared1"), g + 1)
            dve.tensor_scalar(stat[:, g, 0:2], stat[:, g, 0:2], 1.0 / D, EPS, ALU.mult, ALU.add).then_inc(S("x_var"), 1)
            dve.wait_ge(S("x_std"), g + 1)
            dve.reciprocal(stat[:, g, 0:2], stat[:, g, 2:4]).then_inc(S("x_rstd"), 1)
            dve.wait_ge(S("x_rstd"), g + 1)
            for blk in range(NBLK):
                dve.tensor_scalar(h_tok[:, blk, :], x_res[:, blk, :], stat[:, g, blk:blk + 1], None,
                                  ALU.mult).then_inc(S("h_ready"), 1)
            transposed_dve(dve, [norm_gain[:, g, c:c + 1] for c in range(KC)], f"n{g}")

        def norm_pe(pe, g):
            pe.wait_ge(S("h_ready"), 2 * g + 2)
            transposed_pe(pe, h_tok, KC, f"n{g}")

        def transposed_pe(pe, src, chunks, tag):
            for c in range(chunks):
                r, half = c // 2, c % 2
                if half == 0 and r >= 2:
                    pe.wait_ge(S(f"{tag}_lo"), min(2 * (r - 1), chunks))
                for blk in range(NBLK):
                    a = pe.transpose(bank[6 + r % 2][:, (2 * half + blk) * P:(2 * half + blk + 1) * P],
                                     src[:, blk, c * P:(c + 1) * P], ident[:, :])
                a.then_inc(S(f"{tag}_t"), 1)

        def transposed_act(act, gains, tag):
            n = len(gains)
            for c in range(n):
                act.wait_ge(S(f"{tag}_t"), min(2 * (c // 2) + 2, n))
                act.activation(hT_hi[:, c, :], bank[6 + c // 2 % 2][:, c % 2 * SEQ:(c % 2 + 1) * SEQ], ACT.Copy,
                               scale=gains[c] if gains[c] is not None else 1.0).then_inc(S(f"{tag}_hi"), 1)

        def transposed_dve(dve, gains, tag):
            n = len(gains)
            for c in range(n):
                dve.wait_ge(S(f"{tag}_hi"), min(2 * (c // 2) + 2, n))
                dve.scalar_tensor_tensor(out=hT_lo[:, c, :], in0=bank[6 + c // 2 % 2][:, c % 2 * SEQ:(c % 2 + 1) * SEQ],
                                         scalar=gains[c] if gains[c] is not None else 1.0,
                                         in1=hT_hi[:, c, :].bitcast(F32), op0=ALU.mult,
                                         op1=ALU.subtract).then_inc(S(f"{tag}_lo"), 1)

        block = ctx.enter_context(nc.Block())

        @block.sync
        def _(sp):
            for n in range(first["w_q0"]):
                load_slab(sp, plan[n][0], plan[n][1], n, plan[n][2])
                if n == 1:
                    sp.dma_start(x_res[:, :, :], t["x"].rearrange("a (b p) d -> p (a b) d", p=P)).then_inc(S("x_loaded"), 16)

            def loop(name, count):
                with sp.Fori(0, count // 4) as i:
                    for u in range(4):
                        load_slab(sp, name, 4 * i + u, first[name] + u, SLAB, i)

            for layer in range(2):
                if layer:
                    loop("pw1", 2 * KC)
                    for k in range(KC):
                        load_slab(sp, "pw2", k, first["pw2"] + k, D)
                loop(f"w_q{layer}", LISTS)
                loop(f"u{layer}", NKEYS)
                loop(f"v{layer}", NKEYS)
            sp.wait_ge(S("x_ready"), 4)
            sp.dma_start(t["out"].rearrange("a (b p) d -> p (a b) d", p=P), x_res[:, :, :]).then_inc(S("stored"), 16)
            sp.wait_ge(S("stored"), 16)

        @block.gpsimd
        def _(pool):
            small = [
                ("in_ng", norm_gain[:, 0:4, :], t["norm_gains"]),
                ("in_lg", lat_gain[:, :], t["latent_gains"]),
                ("in_pos", m_posi.bitcast(I32), t["positions"]),
                ("in_vg", m_vgain, t["gm_v_gain"].rearrange("a h d -> a (h d)").broadcast_to([P, 512])),
                ("in_qkg", m_qkgain[:, 0, :], t["mla_q_gain"].broadcast_to([P, QK])),
                ("in_qkg", m_qkgain[:, 1, :], t["mla_k_gain"].broadcast_to([P, QK])),
                ("in_ws", m_ws, t["gm_w_sT"]),
                ("in_bs", m_bs, t["gm_b_sT"]),
                ("in_cc", conv_cols[:, :, :], t["conv_columns"]),
            ]
            pool.memset(ident[:, :], 0.0).then_inc(S("pool_step"), 1)
            pool.wait_ge(S("pool_step"), 1)
            pool.affine_select(out=ident[:, :], in_=ident[:, :], compare_op=ALU.not_equal, fill=1.0, base=0,
                               pattern=[[-1, P]], channel_multiplier=1).then_inc(S("c_ident"), 1)
            pool.memset(warm[:, :], 1.0).then_inc(S("c_warm"), 1)
            for s, dst, src in small:
                pool.dma_start(dst, src).then_inc(S(s), 16)
            pool.iota(iota[:, :], pattern=[[1, P]], base=0, channel_multiplier=0,
                      allow_small_or_imprecise_dtypes=True).then_inc(S("c_iota"), 1)
            pool.memset(row_step[:, :], 0.0).then_inc(S("fbank_free"), 2)
            pool.wait_ge(S("fbank_free"), 2)
            for k in range(HALF):
                f = pool.memset(m_freq[:, k:k + 1], float(np.float32(THETA) ** (-np.float32(k) / np.float32(HALF))))
            f.then_inc(S("c_freq"), 1)
            for a in range(TOPK):
                pool.memset(row_start[:, a:a + 1], float(ROW_START[a]))
                if a:
                    f = pool.memset(row_step[:, a - 1:a], float(ROW_START[a] - ROW_START[a - 1]))
            f.then_inc(S("c_rows"), 1)
            pool.memset(m_mask, 0.0).then_inc(S("pool_step"), 1)
            pool.wait_ge(S("pool_step"), 2)
            pool.affine_select(out=m_mask[:, 0:P], in_=m_mask[:, 0:P], compare_op=ALU.is_ge, fill=NEG, base=0,
                               pattern=[[-1, P]], channel_multiplier=1)
            pool.affine_select(out=m_mask[:, 2 * P:3 * P], in_=m_mask[:, 2 * P:3 * P], compare_op=ALU.is_ge, fill=NEG,
                               base=0, pattern=[[-1, P]], channel_multiplier=1).then_inc(S("c_mask"), 1)
            pool.wait_ge(S("in_ws"), 16)
            pool.affine_select(out=m_ws, in_=m_ws, compare_op=ALU.is_ge, fill=0.0, base=0,
                               pattern=[[0, GH], [1, P]], channel_multiplier=-1).then_inc(S("ws_causal"), 1)
            for layer in range(2):
                if layer:
                    pool.wait_ge(S("x_ready"), 2)
                    pool.dma_start(taps, t["conv_w_dwT"]).then_inc(S("in_taps"), 16)
                    pool.memset(c_pad[:, :, 0:TAPS - 1], 0.0)
                    pool.memset(ones, 1.0).then_inc(S("c_padded"), 1)
                    pool.dma_start(c_bias2, t["conv_b_pw2"].broadcast_to([P, D])).then_inc(S("in_b2"), 16)
                else:
                    pool.wait_ge(S("x_ready"), 1)
                if layer:
                    pool.wait_ge(S("conv_tapped"), PE_CONV)
                pool.dma_start(keysT, t["peer_keysT"][layer]).then_inc(S("in_keys"), 16)

                def hots(g, slot):
                    pool.tensor_copy(pool_j[:, slot, :], pickT[:, 1, bass.ds(4 * g, 2)]).then_inc(S(f"pool_j{layer}"), 1)
                    pool.wait_ge(S(f"pool_j{layer}"), g + 1)
                    pool.sem_inc(S("pool_waits_passed"), 1)
                    for k in range(2):
                        a = pool.tensor_scalar(hot_j[:, slot, k, :], iota[:, :], pool_j[:, slot, k:k + 1], None, ALU.is_equal)
                    a.then_inc(S(f"hot_j{layer}"), 1)

                pool.wait_ge(S(f"pickT{layer}"), 1)
                pool.wait_ge(S("x_saved"), 16 * (layer + 1))
                hots(0, 0)
                hots(1, 1)
                with pool.Fori(0, SEQ // 8 - 1) as i:
                    for u in range(2):
                        pool.wait_ge(S(f"gmat{layer}"), 2 * i + u + 1)
                        hots(2 * i + u + 2, u)

        def conv_act(act):
            n0 = first["pw1"]
            norm_act(act, 2)
            act.activation(warm[:, 0:1], warm[:, 1:2], ACT.Sigmoid)
            act.wait_ge(S("in_taps"), 16)
            diags = [(c, k) for c in range(DVE_CONV, KC) for k in range(TAPS)]
            per = -(-len(diags) // KC)
            for c in range(KC):
                ahead_hi(act, n0 + 2 * c)
                for m, (cc, k) in list(enumerate(diags))[per * c:per * (c + 1)]:
                    act.activation(c_diag[:, m, :], ident[:, :], ACT.Copy, scale=taps[:, cc, k:k + 1]).then_inc(S("diag"), 1)
                ahead_hi(act, n0 + 2 * c + 1)
                act.wait_ge(S("slab_used"), n0 + 2 * c + 2)
                if c >= 2:
                    act.wait_ge(S("glu"), c - 1)
                act.activation(c_sig[:, c % 2, :], bank[5 + 2 * (c % 2)][:, 0:SEQ], ACT.Sigmoid,
                               bias=conv_cols[:, 1, c:c + 1]).then_inc(S("sig_ready"), 1)
            act.activation(warm[:, 0:1], warm[:, 1:2], ACT.Sqrt)
            for c in range(KC):
                if c >= DVE_CONV:
                    act.wait_ge(S("conv_tapped"), c - DVE_CONV + 1)
                    act.activation(c_acc[:, c, :], bank[c - DVE_CONV][:, 0:SEQ], ACT.Identity,
                                   bias=conv_cols[:, 2, c:c + 1]).then_inc(S("conv_out"), 1)
                    act.wait_ge(S("conv_out"), c - DVE_CONV + 1)
                else:
                    act.wait_ge(S("tap_done"), TAPS * (c + 1))
                act.activation(c_sq[:, c, :], c_acc[:, c, :], ACT.Square).then_inc(S("conv_squared"), 1)
            act.wait_ge(S("conv_var"), 1)
            act.activation(c_std, c_std, ACT.Sqrt).then_inc(S("conv_std"), 1)
            act.activation(warm[:, 0:1], warm[:, 1:2], ACT.Silu)
            for c in range(KC):
                act.wait_ge(S("conv_normed"), c + 1)
                act.activation(hT_hi[:, c, :], c_sq[:, c, :], ACT.Silu)
                act.activation(c_acc[:, c, :], c_sq[:, c, :], ACT.Silu).then_inc(S("conv_silu"), 1)
            for k in range(KC):
                ahead_hi(act, first["pw2"] + k)

        def peer_act(act, layer):
            act.wait_ge(S("x_ready"), 1 + 2 * layer)
            act.dma_start(x_hold, x_res[:, :, :].rearrange("p b d -> p (b d)")).then_inc(S("x_saved"), 16)
            norm_act(act, 1 + 2 * layer)
            nq, nu, nv = first[f"w_q{layer}"], first[f"u{layer}"], first[f"v{layer}"]
            with act.Fori(0, 2) as i:
                for u in range(8):
                    ahead_hi(act, nq + u, 2 * i)
                    act.wait_ge(S("slab_used"), nq + u + 1 + 8 * i)
                    if u >= 2:
                        act.wait_ge(S(f"scored{layer}"), 8 * i + u - 1)
                    act.activation(qT[:, u % 2, :], bank[4 + u % 2][:, 0:SEQ], ACT.Copy).then_inc(S("fbank_free"), 1)
                    if u in (4, 7):
                        r = u // 4 - (u == 4)
                        act.wait_ge(S(f"scored{layer}"), 8 * i + (4 if u == 4 else 8))
                        for blk in range(NBLK):
                            a = act.activation(scores[:, bass.ds(blk * PH + 4 * i + 2 * r, 2), :],
                                               bank[2 * r + blk][:, :].rearrange("p (h n) -> p h n", h=2), ACT.Copy)
                        a.then_inc(S(f"scores_out{layer}"), 1)

            def experts(a, b):
                with act.Fori(a, b) as i:
                    for u in range(4):
                        ahead_hi(act, nu + u, i)
                        act.wait_ge(S("slab_used"), nu + u + 1 + 4 * i)
                        act.activation(act_all[:, bass.ds(4 * i + u, 1), :], bank[4 + u % 2][:, 0:SEQ].rearrange("p (a t) -> p a t", a=1),
                                       ACT.Gelu_apprx_tanh).then_inc(S("fbank_free"), 1)

            act.activation(warm[:, 0:1], warm[:, 1:2], ACT.Gelu_apprx_tanh)
            experts(0, PICK_SLABS // 4)
            act.wait_ge(S(f"gate_shift{layer}"), 1)
            act.activation(pick_s[:, :, :], pick_s[:, :, :], ACT.Exp).then_inc(S(f"gate_exp{layer}"), 1)
            act.activation(warm[:, 0:1], warm[:, 1:2], ACT.Gelu_apprx_tanh)
            experts(PICK_SLABS // 4, NKEYS // 4)

            def hots(g, slot):
                act.activation(act_j[:, slot, :], pickT[:, 1, bass.ds(4 * g + 2, 2)], ACT.Copy, scale=-1.0).then_inc(S(f"act_j{layer}"), 1)
                act.wait_ge(S(f"act_j{layer}"), g + 1)
                for k in range(2):
                    a = act.activation(hot_j[:, slot, 2 + k, :], iota[:, :], ACT.Abs, bias=act_j[:, slot, k:k + 1])
                a.then_inc(S(f"far_j{layer}"), 1)
                act.wait_ge(S(f"far_j{layer}"), g + 1)
                act.activation(hot_j[:, slot, 2:4, :], hot_j[:, slot, 2:4, :], ACT.Relu, bias=warm[:, 1:2],
                               scale=-1.0).then_inc(S(f"hot_j2{layer}"), 1)

            act.wait_ge(S(f"pickT{layer}"), 1)
            act.wait_ge(S("x_saved"), 16 * (layer + 1))
            hots(0, 0)
            hots(1, 1)
            with act.Fori(0, SEQ // 8 - 1) as i:
                for u in range(2):
                    act.wait_ge(S(f"gmat{layer}"), 2 * i + u + 1)
                    hots(2 * i + u + 2, u)
            act.wait_ge(S(f"gated{layer}"), SEQ // 4)
            act.wait_ge(S("x_saved"), 16 * (layer + 1))
            act.dma_start(x_res[:, :, :].rearrange("p b d -> p (b d)"), x_hold).then_inc(S("x_back"), 16)

            def weight_hi(u, i):
                if isinstance(i, int) and 4 * i + u >= NKEYS:
                    return
                early = isinstance(i, int) and 4 * i + u < W_SLOTS
                act.wait_ge(S("slab_used"), nv if early else nv + u - W_SLOTS + 1 + 4 * i)
                act.activation(hT_hi[:, u % W_SLOTS, :], act_all[:, bass.ds(4 * i + u, 1), :].rearrange("p a t -> p (a t)"),
                               ACT.Copy).then_inc(S(f"w_hi{layer}"), 1)

            def values(i):
                for u in range(4):
                    weight_hi(u + 2, i)
                    ahead_hi(act, nv + u, i)

            weight_hi(0, 0)
            weight_hi(1, 0)
            values(0)
            with act.Fori(1, NKEYS // 4 - 1) as i:
                values(i)
            values(NKEYS // 4 - 1)

        @block.scalar
        def _(act):
            act.wait_ge(S("in_ng"), 16)
            act.wait_ge(S("c_warm"), 1)
            for n in range(AHEAD):
                split_hi(act, n)
            norm_act(act, 0)

            for k in range(KC):
                ahead_hi(act, first["w_in_gm"] + k)
            act.wait_ge(S("slab_used"), KC)
            for dst, c in ((m_u, 0), (m_v, 1)):
                for blk in range(NBLK):
                    act.activation(dst[:, blk, :], bank[2 * blk + c][:, :], ACT.Gelu_apprx_tanh).then_inc(S("gm_gelu"), 1)
            for k in range(KC):
                ahead_hi(act, first["w_in_lat"] + k)
            act.wait_ge(S("slab_used"), 2 * KC)
            for blk in range(NBLK):
                act.activation(m_lat[:, blk, 0:512], bank[2 * blk][:, :], ACT.Copy)
                a = act.activation(m_lat[:, blk, 512:LAT], bank[2 * blk + 1][:, 0:LAT - 512], ACT.Copy)
            a.then_inc(S("lat_ready"), 1)
            act.wait_ge(S("lat_ready"), 1)
            for blk in range(NBLK):
                act.activation(m_sq[:, blk, 0:4, :], m_lat[:, blk, 0:QRANK], ACT.Square, accum_out=m_st[:, 0, blk:blk + 1])
                a = act.activation(m_sq[:, 2 + blk, 0:4, 0:64], m_lat[:, blk, QRANK:QRANK + KVRANK], ACT.Square,
                                   accum_out=m_st[:, 0, 2 + blk:3 + blk])
            a.then_inc(S("lat_squared"), 1)
            act.wait_ge(S("lat_var"), 1)
            act.activation(m_st[:, 2, 0:4], m_st[:, 1, 0:4], ACT.Sqrt).then_inc(S("lat_std"), 1)
            act.wait_ge(S("gm_var"), 1)
            act.activation(m_st[:, 4, 0:16], m_st[:, 3, 0:16], ACT.Sqrt).then_inc(S("gm_std"), 1)
            act.wait_ge(S("ang_ready"), 1)
            act.activation(m_ang[:, 6:8, :, :], m_ang[:, 4:6, :, :], ACT.Sin).then_inc(S("sincos"), 1)
            act.wait_ge(S("slab_used"), 2 * KC)
            transposed_act(act, [lat_gain[:, c:c + 1] for c in range(QCH + KVCH)], "lt")

            for k in range(QCH):
                ahead_hi(act, first["w_uq"] + k)
            act.wait_ge(S("slab_used"), first["w_ukv"])
            for blk in range(NBLK):
                for c in range(2):
                    a = act.activation(m_qk[:, 2 * blk, 4 * c:4 * c + 4, :], bank[2 * blk + c][:, 0:4 * QK], ACT.Copy)
            a.then_inc(S("q_ready"), 1)
            for k in range(KVCH):
                ahead_hi(act, first["w_ukv"] + k)
            act.wait_ge(S("slab_used"), first["w_out"])
            for blk in range(NBLK):
                for c in range(2):
                    kv = bank[2 * blk + c][:, :].rearrange("p (h e) -> p h e", e=NOPE + VD)
                    act.activation(m_qk[:, 2 * blk + 1, 4 * c:4 * c + 4, 0:NOPE], kv[:, :, 0:NOPE], ACT.Copy)
                    a = act.activation(m_val[:, blk, 4 * c:4 * c + 4, :], kv[:, :, NOPE:], ACT.Copy)
            a.then_inc(S("kv_ready"), 1)
            act.wait_ge(S("kv_ready"), 1)
            act.wait_ge(S("k_pe"), 1)
            act.activation(m_sq, m_qk, ACT.Square).then_inc(S("qk_squared"), 1)
            act.wait_ge(S("qk_var"), 1)
            act.activation(m_st[:, 2, :], m_st[:, 1, :], ACT.Sqrt).then_inc(S("qk_std"), 1)
            for r in range(8):
                act.wait_ge(S("qkT_t"), r + 1)
                blk, which, half = r // 4, r // 2 % 2, r % 2
                act.activation(m_qkT[0:QK, which, 4 * half:4 * half + 4, blk * P:(blk + 1) * P],
                               bank[6 + r % 2][0:QK, :].rearrange("p (h t) -> p h t", t=P), ACT.Copy).then_inc(S("qkT"), 1)
            for h in range(MH):
                act.wait_ge(S("s_max"), h + 1)
                for blk, (a0, a1) in enumerate(((0, P), (P, 3 * P))):
                    a = act.activation(m_p[:, h, a0:a1], m_p[:, h, a0:a1], ACT.Exp, bias=m_st[:, 5 + blk, h:h + 1],
                                       accum_out=m_st[:, 7, blk * MH + h:blk * MH + h + 1])
                a.then_inc(S("probs"), 1)
            for h in range(MH):
                act.wait_ge(S("pT_t"), h + 1)
                act.activation(m_pT[:, h, :, :], bank[6 + h % 2][:, 0:3 * P].rearrange("p (a t) -> p a t", t=P),
                               ACT.Copy).then_inc(S("pT"), 1)
            transposed_act(act, [None] * KC, "ct")
            for k in range(KC):
                ahead_hi(act, first["w_out"] + k)

            for layer in range(2):
                if layer:
                    conv_act(act)
                peer_act(act, layer)

        def add_banks(dve, n):
            dve.wait_ge(S("slab_used"), n)
            for blk in range(NBLK):
                for c in range(2):
                    a = dve.tensor_tensor(x_res[:, blk, 512 * c:512 * (c + 1)], bank[2 * blk + c][:, :],
                                          x_res[:, blk, 512 * c:512 * (c + 1)], ALU.add)
                a.then_inc(S("x_ready" if blk else "x_half_ready"), 1)

        def conv_dve(dve):
            n0 = first["pw1"]
            norm_dve(dve, 2)
            dve.wait_ge(S("in_taps"), 16)
            dve.wait_ge(S("in_cc"), 16)
            dve.wait_ge(S("c_padded"), 1)

            def tap(c, k):
                z, w = c_pad[:, c, k:k + SEQ], taps[:, c, k:k + 1]
                if k == 0:
                    a = dve.tensor_scalar(c_acc[:, c, :], z, w, conv_cols[:, 2, c:c + 1], ALU.mult, ALU.add)
                else:
                    dve.wait_ge(S("tap_done"), TAPS * c + k)
                    a = dve.scalar_tensor_tensor(out=c_acc[:, c, :], in0=z, scalar=w, in1=c_acc[:, c, :],
                                                 op0=ALU.mult, op1=ALU.add)
                a.then_inc(S("tap_done"), 1)

            work = [(c, k) for c in range(DVE_CONV) for k in range(TAPS)]
            for c in range(KC):
                ahead_lo(dve, n0 + 2 * c)
                ahead_lo(dve, n0 + 2 * c + 1)
                dve.wait_ge(S("sig_ready"), c + 1)
                dve.scalar_tensor_tensor(out=c_pad[:, c, TAPS - 1:], in0=bank[4 + 2 * (c % 2)][:, 0:SEQ],
                                         scalar=conv_cols[:, 0, c:c + 1], in1=c_sig[:, c % 2, :],
                                         op0=ALU.add, op1=ALU.mult).then_inc(S("glu"), 1)
                dve.wait_ge(S("glu"), c + 1)
                for _ in range(7):
                    tap(*work.pop(0))
            for c, k in work:
                tap(c, k)
            dve.wait_ge(S("in_b2"), 16)
            for blk in range(NBLK):
                a = dve.tensor_tensor(x_res[:, blk, :], x_res[:, blk, :], c_bias2, ALU.add)
            a.then_inc(S("bias2_added"), 1)
            dve.wait_ge(S("conv_summed"), 1)
            dve.tensor_scalar(c_std, bank[4][:, 0:SEQ], 1.0 / D, EPS, ALU.mult, ALU.add).then_inc(S("conv_var"), 1)
            dve.wait_ge(S("conv_std"), 1)
            dve.reciprocal(c_rstd, c_std).then_inc(S("conv_rstd"), 1)
            dve.wait_ge(S("conv_rstd"), 1)
            dve.wait_ge(S("conv_squared"), KC)
            for c in range(KC):
                dve.scalar_tensor_tensor(out=c_sq[:, c, :], in0=c_acc[:, c, :], scalar=conv_cols[:, 3, c:c + 1],
                                         in1=c_rstd, op0=ALU.mult, op1=ALU.mult).then_inc(S("conv_normed"), 1)
            for c in range(KC):
                dve.wait_ge(S("conv_silu"), c + 1)
                dve.tensor_tensor(hT_lo[:, c, :], c_acc[:, c, :], hT_hi[:, c, :].bitcast(F32),
                                  ALU.subtract).then_inc(S("conv_lo"), 1)
            for k in range(KC):
                ahead_lo(dve, first["pw2"] + k)
            dve.wait_ge(S("bias2_added"), 1)
            add_banks(dve, first["w_q1"])

        def peer_dve(dve, layer):
            norm_dve(dve, 1 + 2 * layer)
            nq, nu, nv = first[f"w_q{layer}"], first[f"u{layer}"], first[f"v{layer}"]
            with dve.Fori(0, LISTS // 4) as i:
                for u in range(4):
                    ahead_lo(dve, nq + u, i)

            STEPS = 46
            SPLITS = 12
            picked = S(f"picked{layer}")
            dve.wait_ge(S(f"scores_out{layer}"), 4)
            dve.wait_ge(S("c_rows"), 1)
            dve.wait_ge(S("c_iota"), 1)
            lists = [(h, c) for h in range(2) for c in range(2)]
            with dve.Fori(0, UNITS // 2) as i:
                done, split = [0], [0]

                def step(ins):
                    done[0] += 1
                    ins.then_inc(picked, 1)
                    return done[0]

                def after(n):
                    dve.wait_ge(picked, STEPS * i + n)

                def after8(n):
                    dve.wait_ge(picked, STEPS * i + n)
                    dve.sem_inc(S("waits_passed"), 1)

                def slab(count=1):
                    for _ in range(count):
                        ahead_lo(dve, nu + split[0], 3 * i)
                        split[0] += 1

                def per_row(v, n):
                    return v.unsqueeze(3).broadcast_to([P, 2, v.shape[2], n])

                def per_pick(v):
                    return v.unsqueeze(2).broadcast_to([P, 2, TOPK, v.shape[2]])

                at = step(dve.tensor_copy(stage.rearrange("p h c n -> p h (c n)"), scores[:, bass.ds(2 * i, 2), :]))
                slab()
                after8(at)
                found = [step(dve.max(top_v[:, h, c, 0:8], stage[:, h, c, :])) for h, c in lists]
                slab()
                after8(found[-1])
                for h, c in lists:
                    f = step(dve.max_index(top_iu[:, h, c, 0:8], top_v[:, h, c, 0:8], stage[:, h, c, :]))
                slab()
                after8(f)
                for h, c in lists:
                    f = step(dve.match_replace(stage[:, h, c, :], top_v[:, h, c, 0:8], stage[:, h, c, :], -3e38))
                slab()
                after8(f)
                for h, c in lists:
                    f = step(dve.max(top_v[:, h, c, 8:16], stage[:, h, c, :]))
                slab()
                after8(f)
                for h, c in lists:
                    f = step(dve.max_index(top_iu[:, h, c, 8:16], top_v[:, h, c, 8:16], stage[:, h, c, :]))
                at = 0
                for a0, rows, cols in ROWS:
                    for h in range(2):
                        s = dve.tensor_tensor(
                            cand[:, h, at:at + rows * cols].rearrange("p (a b) -> p a b", b=cols),
                            top_v[:, h, 0, a0:a0 + rows].unsqueeze(2).broadcast_to([P, rows, cols]),
                            top_v[:, h, 1, 0:cols].unsqueeze(1).broadcast_to([P, rows, cols]), ALU.add)
                    at += rows * cols
                summed = step(s)
                after(f)
                s = step(dve.tensor_copy(top_if, top_iu))
                slab()
                after(s)
                step(dve.tensor_tensor(step_i[:, :, 0:15], top_if[:, :, 0, 1:16], top_if[:, :, 0, 0:15], ALU.subtract))
                after8(summed)
                for h in range(2):
                    f = step(dve.max(best_v[:, h, 0:8], cand[:, h, :]))
                slab()
                after8(f)
                for h in range(2):
                    f = step(dve.max_index(best_pu[:, h, 0:8], best_v[:, h, 0:8], cand[:, h, :]))
                slab()
                after8(f)
                for h in range(2):
                    f = step(dve.match_replace(cand[:, h, :], best_v[:, h, 0:8], cand[:, h, :], -3e38))
                slab()
                after8(f)
                for h in range(2):
                    f = step(dve.max(best_v[:, h, 8:16], cand[:, h, :]))
                slab()
                after8(f)
                for h in range(2):
                    f = step(dve.max_index(best_pu[:, h, 8:16], best_v[:, h, 8:16], cand[:, h, :]))
                slab()
                after(f)
                f = step(dve.tensor_copy(best_p, best_pu))
                slab()
                after(f)
                ge = step(dve.tensor_tensor(dec_ge[:, :, :, 0:15], per_row(best_p, 15),
                                            row_start[:, 1:16].unsqueeze(1).unsqueeze(1).broadcast_to([P, 2, TOPK, 15]), ALU.is_ge))
                step(dve.tensor_copy(pick_s[:, bass.ds(2 * i, 2), :], best_v))
                after(ge)
                m1 = step(dve.tensor_tensor(dec_m[:, :, :, 0:15], dec_ge[:, :, :, 0:15],
                                            row_step[:, :].unsqueeze(1).unsqueeze(1).broadcast_to([P, 2, TOPK, 15]), ALU.mult))
                m2 = step(dve.tensor_tensor(dec_n[:, :, :, 0:15], dec_ge[:, :, :, 0:15], per_pick(step_i[:, :, 0:15]), ALU.mult))
                after(m1)
                r1 = step(dve.tensor_reduce(sum_r, dec_m[:, :, :, 0:15], AX.X, ALU.add))
                after(m2)
                r2 = step(dve.tensor_reduce(sum_i, dec_n[:, :, :, 0:15], AX.X, ALU.add))
                after(r1)
                b = step(dve.tensor_tensor(col_b, best_p, sum_r, ALU.subtract))
                after(r2)
                step(dve.tensor_tensor(pick_i[:, bass.ds(2 * i, 2), :], sum_i,
                                       top_if[:, :, 0, 0:1].broadcast_to([P, 2, TOPK]), ALU.add))
                after(b)
                e = step(dve.tensor_tensor(dec_e, per_row(col_b, TOPK), per_pick(iota[:, 0:TOPK].unsqueeze(1).broadcast_to([P, 2, TOPK])),
                                           ALU.is_equal))
                after(e)
                e = step(dve.tensor_tensor(dec_f, dec_e, per_pick(top_if[:, :, 1, :]), ALU.mult))
                after(e)
                step(dve.tensor_reduce(pick_j[:, bass.ds(2 * i, 2), :], dec_f, AX.X, ALU.add))
                assert done[0] == STEPS and split[0] == SPLITS, (done, split)
                after(STEPS)

            dve.tensor_tensor(pick_s[:, :, 1:16], pick_s[:, :, 1:16], pick_s[:, :, 0:1].broadcast_to([P, UNITS, 15]),
                              ALU.subtract).then_inc(S(f"g_a{layer}"), 1)
            dve.wait_ge(S(f"g_a{layer}"), 1)
            dve.tensor_tensor(pick_s[:, :, 0:1], pick_s[:, :, 0:1], pick_s[:, :, 0:1],
                              ALU.subtract).then_inc(S(f"gate_shift{layer}"), 1)
            dve.wait_ge(S(f"gate_exp{layer}"), 1)
            dve.tensor_reduce(gate_sum[:, 0, :], pick_s[:, :, :], AX.X, ALU.add).then_inc(S(f"g_b{layer}"), 1)
            dve.wait_ge(S(f"g_b{layer}"), 1)
            dve.reciprocal(gate_sum[:, 1, :], gate_sum[:, 0, :]).then_inc(S(f"g_c{layer}"), 1)
            dve.wait_ge(S(f"g_c{layer}"), 1)
            dve.tensor_tensor(pick_s[:, :, :], pick_s[:, :, :],
                              gate_sum[:, 1, :].unsqueeze(2).broadcast_to([P, UNITS, TOPK]),
                              ALU.mult).then_inc(S(f"gates{layer}"), 1)

            with dve.Fori(PICK_SLABS // 4, NKEYS // 4) as i:
                for u in range(4):
                    ahead_lo(dve, nu + u, i)

            dve.wait_ge(S(f"pickT_t{layer}"), 1)
            dve.tensor_copy(pickT[:, 0:2, :], bank[6][:, :].rearrange("p (a t) -> p a t", t=SEQ))
            dve.tensor_copy(pickT[:, 2, :], bank[7][:, 0:SEQ]).then_inc(S(f"pickT{layer}"), 1)
            dve.wait_ge(S(f"pickT{layer}"), 1)
            dve.wait_ge(S("x_saved"), 16 * (layer + 1))

            def hots(g, slot):
                for k in range(4):
                    tk = bass.ds(4 * g + k, 1)
                    a = dve.tensor_scalar(hot_i[:, slot, k, :], iota[:, :], pickT[:, 0, tk], pickT[:, 2, tk],
                                          ALU.is_equal, ALU.mult)
                a.then_inc(S(f"hot_i{layer}"), 1)

            def gate(g, slot):
                dve.wait_ge(S(f"gmat{layer}"), g + 1)
                a = act_all[:, :, bass.ds(4 * g, 4)]
                dve.tensor_tensor(a, bank[4 + slot][:, :].rearrange("p (t j) -> p j t", t=4), a,
                                  ALU.mult).then_inc(S(f"gated{layer}"), 1)

            hots(0, 0)
            hots(1, 1)
            dve.wait_ge(S("fbank_free"), 2 + (layer + 1) * (LISTS + NKEYS))
            with dve.Fori(0, SEQ // 8 - 1) as i:
                for u in range(2):
                    gate(2 * i + u, u)
                    hots(2 * i + u + 2, u)
            gate(SEQ // 4 - 2, 0)
            gate(SEQ // 4 - 1, 1)
            dve.wait_ge(S(f"gated{layer}"), SEQ // 4)

            def weight_lo(u, i):
                if isinstance(i, int) and 4 * i + u >= NKEYS:
                    return
                dve.wait_ge(S(f"w_hi{layer}"), 4 * i + u + 1)
                dve.tensor_tensor(hT_lo[:, u % W_SLOTS, :], act_all[:, bass.ds(4 * i + u, 1), :].rearrange("p a t -> p (a t)"),
                                  hT_hi[:, u % W_SLOTS, :].bitcast(F32), ALU.subtract).then_inc(S(f"w_lo{layer}"), 1)

            def values(i):
                for u in range(4):
                    weight_lo(u + 2, i)
                    ahead_lo(dve, nv + u, i)

            weight_lo(0, 0)
            weight_lo(1, 0)
            values(0)
            with dve.Fori(1, NKEYS // 4 - 1) as i:
                values(i)
            values(NKEYS // 4 - 1)
            dve.wait_ge(S("x_back"), 16 * (layer + 1))
            add_banks(dve, nv + NKEYS)

        @block.vector
        def _(dve):
            dve.wait_ge(S("in_ng"), 16)
            for n in range(AHEAD):
                split_lo(dve, n)
            norm_dve(dve, 0)
            count = [0]

            def chain(ins):
                count[0] += 1
                ins.then_inc(S("dve_chain"), 1)
                dve.wait_ge(S("dve_chain"), count[0])

            def wide(v, n):
                return v.unsqueeze(2).broadcast_to([P, v.shape[1], n])

            for k in range(KC):
                ahead_lo(dve, first["w_in_gm"] + k)
            dve.wait_ge(S("in_pos"), 16)
            dve.wait_ge(S("c_freq"), 1)
            chain(dve.tensor_copy(m_pos, m_posi.bitcast(I32)))
            for blk in range(NBLK):
                a = dve.tensor_scalar(m_ang[:, 0, blk, :], m_freq, m_pos[:, blk:blk + 1], None, ALU.mult)
            chain(a)
            for k, shift in ((0, 0.0), (1, 0.25)):
                magic = 1.5 * 2.0 ** 23
                chain(dve.tensor_scalar(m_ang[:, 1, :, :], m_ang[:, 0, :, :], float(1 / (2 * np.pi)), shift, ALU.mult, ALU.add))
                chain(dve.tensor_scalar(m_ang[:, 2, :, :], m_ang[:, 1, :, :], magic, None, ALU.add))
                chain(dve.tensor_scalar(m_ang[:, 2, :, :], m_ang[:, 2, :, :], magic, None, ALU.subtract))
                two_pi = 2 * np.pi
                c1 = 6.28125
                c2 = float(np.float32(np.round((two_pi - c1) * 2.0 ** 20) / 2.0 ** 20))
                c3 = float(np.float32(two_pi - c1 - c2))
                src = m_ang[:, 0, :, :]
                for c in (c1, c2, c3):
                    chain(dve.scalar_tensor_tensor(out=m_ang[:, 3, :, :], in0=m_ang[:, 2, :, :], scalar=-c, in1=src,
                                                   op0=ALU.mult, op1=ALU.add))
                    src = m_ang[:, 3, :, :]
                chain(dve.tensor_scalar(m_ang[:, 3, :, :], m_ang[:, 3, :, :], float(np.pi / 2) if k else 0.0, float(np.float32(3.1415925)), ALU.add, ALU.min))
                chain(dve.tensor_scalar(m_ang[:, 4 + k, :, :], m_ang[:, 3, :, :], -float(np.float32(3.1415925)), None, ALU.max))
            dve.tensor_copy(m_st[:, 7, 0:1], m_ang[:, 5, 0, 0:1]).then_inc(S("ang_ready"), 1)
            dve.wait_ge(S("gm_gelu"), 4)
            chain(dve.tensor_tensor(m_vsq, m_v, m_v, ALU.mult))
            chain(dve.tensor_reduce(m_st[:, 0, 16:32], m_vsq.rearrange("p a (h d) -> p (a h) d", d=GD), AX.X, ALU.add))
            dve.tensor_scalar(m_st[:, 3, 0:16], m_st[:, 0, 16:32], 1.0 / GD, EPS, ALU.mult, ALU.add).then_inc(S("gm_var"), 1)
            for k in range(KC):
                ahead_lo(dve, first["w_in_lat"] + k)
            dve.wait_ge(S("lat_squared"), 1)
            dve.tensor_scalar(m_st[:, 1, 0:2], m_st[:, 0, 0:2], 1.0 / QRANK, EPS, ALU.mult, ALU.add)
            dve.tensor_scalar(m_st[:, 1, 2:4], m_st[:, 0, 2:4], 1.0 / KVRANK, EPS, ALU.mult, ALU.add).then_inc(S("lat_var"), 1)
            dve.wait_ge(S("lat_std"), 1)
            chain(dve.reciprocal(m_st[:, 1, 0:4], m_st[:, 2, 0:4]))
            for blk in range(NBLK):
                dve.tensor_scalar(m_lat[:, blk, 0:QRANK], m_lat[:, blk, 0:QRANK], m_st[:, 1, blk:blk + 1], None, ALU.mult)
                a = dve.tensor_scalar(m_lat[:, blk, QRANK:QRANK + KVRANK], m_lat[:, blk, QRANK:QRANK + KVRANK],
                                      m_st[:, 1, 2 + blk:3 + blk], None, ALU.mult)
            a.then_inc(S("lat_normed"), 1)
            dve.wait_ge(S("gm_std"), 1)
            chain(dve.reciprocal(m_st[:, 3, 16:32], m_st[:, 4, 0:16]))
            v3 = m_v.rearrange("p a (h d) -> p (a h) d", d=GD)
            chain(dve.tensor_tensor(v3, v3, wide(m_st[:, 3, 16:32], GD), ALU.mult))
            dve.wait_ge(S("in_vg"), 16)
            for blk in range(NBLK):
                a = dve.tensor_tensor(m_v[:, blk, :], m_v[:, blk, :], m_vgain, ALU.mult)
            a.then_inc(S("v_normed"), 1)
            transposed_dve(dve, [lat_gain[:, c:c + 1] for c in range(QCH + KVCH)], "lt")
            for k in range(QCH + KVCH):
                ahead_lo(dve, first["w_uq"] + k)
            dve.wait_ge(S("lat_ready"), 1)
            for blk in range(NBLK):
                a = dve.tensor_copy(m_qk[:, 2 * blk + 1, :, NOPE:],
                                    m_lat[:, blk, LAT - ROPE:LAT].unsqueeze(1).broadcast_to([P, MH, ROPE]))
            a.then_inc(S("k_pe"), 1)
            dve.wait_ge(S("mixed"), 1)
            dve.wait_ge(S("in_bs"), 16)
            for blk in range(NBLK):
                a = dve.tensor_tensor(m_cat[:, blk, 0:512].rearrange("p (h d) -> p h d", d=GD),
                                      bank[4 + blk][:, :].rearrange("p (h d) -> p h d", d=GD), wide(m_bs, GD), ALU.add)
            chain(a)
            a = dve.tensor_tensor(m_cat[:, :, 0:512], m_cat[:, :, 0:512], m_u, ALU.mult)
            a.then_inc(S("gm_done"), 1)
            dve.wait_ge(S("qk_squared"), 1)
            chain(dve.tensor_reduce(m_st[:, 0, :], m_sq.rearrange("p a h d -> p (a h) d"), AX.X, ALU.add))
            dve.tensor_scalar(m_st[:, 1, :], m_st[:, 0, :], 1.0 / QK, EPS, ALU.mult, ALU.add).then_inc(S("qk_var"), 1)
            dve.wait_ge(S("qk_std"), 1)
            chain(dve.reciprocal(m_st[:, 0, :], m_st[:, 2, :]))
            qk3 = m_qk.rearrange("p a h d -> p (a h) d")
            chain(dve.tensor_tensor(qk3, qk3, wide(m_st[:, 0, :], QK), ALU.mult))
            dve.wait_ge(S("in_qkg"), 32)
            for b in range(2 * NBLK):
                a = dve.tensor_tensor(m_qk[:, b, :, :], m_qk[:, b, :, :],
                                      m_qkgain[:, b % 2, :].unsqueeze(1).broadcast_to([P, MH, QK]), ALU.mult)
            chain(a)
            dve.wait_ge(S("sincos"), 1)
            for blk in range(NBLK):
                rows = qk3[:, 16 * blk:16 * blk + 16, :]
                x1, x2 = rows[:, :, NOPE:NOPE + HALF], rows[:, :, NOPE + HALF:QK]
                sin = m_ang[:, 6, blk, :].unsqueeze(1).broadcast_to([P, 16, HALF])
                cos = m_ang[:, 7, blk, :].unsqueeze(1).broadcast_to([P, 16, HALF])
                for k, (xx, cs) in enumerate(((x1, cos), (x2, sin), (x1, sin), (x2, cos))):
                    a = dve.tensor_tensor(m_rt[:, k, :, :], xx, cs, ALU.mult)
                chain(a)
                dve.tensor_tensor(x1, m_rt[:, 0, :, :], m_rt[:, 1, :, :], ALU.subtract)
                chain(dve.tensor_tensor(x2, m_rt[:, 2, :, :], m_rt[:, 3, :, :], ALU.add))
                dve.tensor_copy(m_st[:, 7, blk:blk + 1], qk3[:, 16 * blk, 0:1]).then_inc(S("roped"), 1)
            dve.wait_ge(S("c_mask"), 1)
            for h in range(MH):
                dve.wait_ge(S("s_ready"), h + 1)
                chain(dve.scalar_tensor_tensor(out=m_p[:, h, :], in0=bank[4 + h % 2][:, 0:3 * P], scalar=float(QK) ** -0.5,
                                               in1=m_mask, op0=ALU.mult, op1=ALU.add))
                dve.tensor_reduce(m_st[:, 5, h:h + 1], m_p[:, h, 0:P], AX.X, ALU.max, negate=True)
                dve.tensor_reduce(m_st[:, 6, h:h + 1], m_p[:, h, P:3 * P], AX.X, ALU.max, negate=True).then_inc(S("s_max"), 1)
            dve.wait_ge(S("probs"), MH)
            chain(dve.reciprocal(m_st[:, 4, 0:16], m_st[:, 7, 0:16]))
            dve.wait_ge(S("attended"), 1)
            for blk in range(NBLK):
                a = dve.tensor_tensor(m_cat[:, blk, 512:1024].rearrange("p (h d) -> p h d", d=VD),
                                      bank[4 + blk][:, :].rearrange("p (h d) -> p h d", d=VD),
                                      wide(m_st[:, 4, blk * MH:(blk + 1) * MH], VD), ALU.mult)
            a.then_inc(S("cat_ready"), 1)
            transposed_dve(dve, [None] * KC, "ct")
            for k in range(KC):
                ahead_lo(dve, first["w_out"] + k)
            add_banks(dve, first["w_q0"])

            for layer in range(2):
                if layer:
                    conv_dve(dve)
                peer_dve(dve, layer)

        def conv_pe(pe):
            n0 = first["pw1"]
            norm_pe(pe, 2)
            pe.wait_ge(S("n2_lo"), KC)
            for c in range(KC):
                if c >= 2:
                    pe.wait_ge(S("glu"), c - 1)
                cols_product(pe, n0 + 2 * c, bank[4 + 2 * (c % 2)][:, 0:SEQ])
                cols_product(pe, n0 + 2 * c + 1, bank[5 + 2 * (c % 2)][:, 0:SEQ])
            for b in range(PE_CONV):
                c = DVE_CONV + b
                pe.wait_ge(S("glu"), c + 1)
                pe.wait_ge(S("diag"), TAPS * (b + 1))
                for k in range(TAPS):
                    a = pe.matmul(bank[b][:, 0:SEQ], c_diag[:, TAPS * b + k, :], c_pad[:, c, k:k + SEQ],
                                  start=k == 0, stop=k == TAPS - 1)
                a.then_inc(S("conv_tapped"), 1)
            for c in range(KC):
                pe.wait_ge(S("conv_squared"), c + 1)
                a = pe.matmul(bank[4][:, 0:SEQ], ones, c_sq[:, c, :], start=c == 0, stop=c == KC - 1)
            a.then_inc(S("conv_summed"), 1)
            rows_product(pe, "pw2", KC, [(0, 512), (512, 1024)], ready="conv_lo")

        def peer_pe(pe, layer):
            norm_pe(pe, 1 + 2 * layer)
            nq, nu, nv = first[f"w_q{layer}"], first[f"u{layer}"], first[f"v{layer}"]
            base = layer * (LISTS + NKEYS)
            pe.wait_ge(S(f"n{1 + 2 * layer}_lo"), KC)
            pe.wait_ge(S("in_keys"), 16 * (layer + 1))
            if layer:
                pe.wait_ge(S("conv_var"), 1)

            with pe.Fori(0, 2) as i:
                def query(u):
                    pe.wait_ge(S("fbank_free"), base + 8 * i + u + 1)
                    cols_product(pe, nq + u, bank[4 + u % 2][:, 0:SEQ], 2 * i)

                def score(u):
                    pe.wait_ge(S("fbank_free"), base + 8 * i + u + 3)
                    for blk in range(NBLK):
                        a = pe.matmul(bank[2 * (u // 4) + blk][:, u % 4 * P:(u % 4 + 1) * P],
                                      qT[:, u % 2, blk * P:(blk + 1) * P],
                                      keysT[:, bass.ds(8 * i + u, 1), :].rearrange("p a n -> p (a n)"), start=True, stop=True)
                    a.then_inc(S(f"scored{layer}"), 1)

                query(0)
                for u in range(1, 8):
                    query(u)
                    score(u - 1)
                score(7)
                pe.wait_ge(S(f"scores_out{layer}"), 2 * i + 2)

            def experts(a, b):
                with pe.Fori(a, b) as i:
                    for u in range(4):
                        pe.wait_ge(S("fbank_free"), base + LISTS + 4 * i + u + 1)
                        cols_product(pe, nu + u, bank[4 + u % 2][:, 0:SEQ], i)

            experts(0, NKEYS // 4 - 2)
            pe.wait_ge(S(f"gates{layer}"), 1)
            for k, src in enumerate((pick_i, pick_j, pick_s)):
                for blk in range(NBLK):
                    out = bank[6 + k // 2][:, (k % 2) * SEQ + blk * P:(k % 2) * SEQ + (blk + 1) * P]
                    a = pe.transpose(out, src[:, blk * PH:(blk + 1) * PH, :].rearrange("p h k -> p (h k)"), ident[:, :])
            a.then_inc(S(f"pickT_t{layer}"), 1)
            experts(NKEYS // 4 - 2, NKEYS // 4)
            pe.wait_ge(S("fbank_free"), base + 2 + LISTS + NKEYS)

            def gmat(g, slot):
                pe.wait_ge(S(f"hot_i{layer}"), g + 1)
                pe.wait_ge(S(f"hot_j{layer}"), g + 1)
                pe.wait_ge(S(f"hot_j2{layer}"), g + 1)
                for k in range(4):
                    a = pe.matmul(bank[4 + slot][:, k * P:(k + 1) * P], hot_i[:, slot, k, :], hot_j[:, slot, k, :],
                                  start=True, stop=True)
                a.then_inc(S(f"gmat{layer}"), 1)

            with pe.Fori(0, SEQ // 8) as i:
                for u in range(2):
                    gmat(2 * i + u, u)

            def values(i, begin, end):
                for u in range(4):
                    j, n = 4 * i + u, nv + u
                    pe.wait_ge(S("slab_lo"), n + 1 + 4 * i)
                    pe.wait_ge(S(f"w_lo{layer}"), j + 1)
                    for blk in range(NBLK):
                        w = slice(blk * P, (blk + 1) * P)
                        for a, b in ((hT_hi, part_hi), (hT_hi, part_lo), (hT_lo, part_hi)):
                            for c in range(2):
                                mm = pe.matmul(bank[2 * blk + c][:, :], a[:, u % W_SLOTS, w],
                                               b[:, n % PARTS, 512 * c:512 * (c + 1)],
                                               start=begin and u == 0 and a is hT_hi and b is part_hi,
                                               stop=end and u == 3 and a is hT_lo)
                    mm.then_inc(S("slab_used"), 1)

            values(0, True, False)
            with pe.Fori(1, NKEYS // 4 - 1) as i:
                values(i, False, False)
            values(NKEYS // 4 - 1, False, True)

        @block.tensor
        def _(pe):
            pe.wait_ge(S("c_ident"), 1)
            norm_pe(pe, 0)
            halves = [(0, 512), (512, 1024)]
            rows_product(pe, "w_in_gm", KC, halves, ready="n0_lo")
            pe.wait_ge(S("gm_gelu"), 4)
            rows_product(pe, "w_in_lat", KC, [(0, 512), (512, LAT)])
            pe.wait_ge(S("lat_normed"), 1)
            transposed_pe(pe, m_lat, QCH + KVCH, "lt")
            pe.wait_ge(S("v_normed"), 1)
            pe.wait_ge(S("ws_causal"), 1)
            for blk in range(NBLK):
                for h in range(GH):
                    a = pe.matmul(bank[4 + blk][:, h * GD:(h + 1) * GD], m_ws[:, h, :], m_v[:, blk, h * GD:(h + 1) * GD],
                                  start=True, stop=True)
            a.then_inc(S("mixed"), 1)
            rows_product(pe, "w_uq", QCH, [(0, 4 * QK), (4 * QK, 8 * QK)], ready="lt_lo")
            pe.wait_ge(S("q_ready"), 1)
            rows_product(pe, "w_ukv", KVCH, halves, QCH, ready="lt_lo")
            for r in range(8):
                blk, which, half = r // 4, r // 2 % 2, r % 2
                pe.wait_ge(S("roped"), blk + 1)
                if r >= 2:
                    pe.wait_ge(S("qkT"), r - 1)
                for h in range(4):
                    a = pe.transpose(bank[6 + r % 2][0:QK, h * P:(h + 1) * P], m_qk[:, 2 * blk + which, 4 * half + h, :],
                                     ident[:, :])
                a.then_inc(S("qkT_t"), 1)
            pe.wait_ge(S("qkT"), 8)
            pe.wait_ge(S("gm_done"), 1)
            for h in range(MH):
                if h >= 2:
                    pe.wait_ge(S("s_max"), h - 1)
                q, k = m_qkT[0:QK, 0, h, :], m_qkT[0:QK, 1, h, :]
                pe.matmul(bank[4 + h % 2][:, 0:P], q[:, 0:P], k[:, 0:P], start=True, stop=True)
                pe.matmul(bank[4 + h % 2][:, P:3 * P], q[:, P:2 * P], k, start=True, stop=True).then_inc(S("s_ready"), 1)
            for h in range(MH):
                pe.wait_ge(S("probs"), h + 1)
                if h >= 2:
                    pe.wait_ge(S("pT"), h - 1)
                for c in range(3):
                    a = pe.transpose(bank[6 + h % 2][:, c * P:(c + 1) * P], m_p[:, h, c * P:(c + 1) * P], ident[:, :])
                a.then_inc(S("pT_t"), 1)
            pe.wait_ge(S("s_max"), MH)
            for h in range(MH):
                pe.wait_ge(S("pT"), h + 1)
                o = slice(h * VD, (h + 1) * VD)
                pe.matmul(bank[4][:, o], m_pT[:, h, 0, :], m_val[:, 0, h, :], start=True, stop=True)
                pe.matmul(bank[5][:, o], m_pT[:, h, 1, :], m_val[:, 0, h, :], start=True, stop=False)
                a = pe.matmul(bank[5][:, o], m_pT[:, h, 2, :], m_val[:, 1, h, :], start=False, stop=True)
            a.then_inc(S("attended"), 1)
            pe.wait_ge(S("cat_ready"), 1)
            transposed_pe(pe, m_cat, KC, "ct")
            rows_product(pe, "w_out", KC, halves, ready="ct_lo")

            for layer in range(2):
                if layer:
                    conv_pe(pe)
                peer_pe(pe, layer)

def kernel(**inputs):
    import numpy as _np
    import concourse.bacc as _bacc
    from concourse import mybir as _mybir
    from concourse.bass_utils import run_bass_kernel_spmd as _run

    a = {k: _np.asarray(v) for k, v in inputs.items()}

    def columns(w):
        return w.reshape(8, 128, 16, 128).transpose(2, 1, 0, 3).reshape(16, 128, 1024)

    pw1 = columns(a["conv_w_pw1"][0]).reshape(2, 8, 128, 1024).transpose(1, 0, 2, 3).reshape(16, 128, 1024)
    arrays = {k: a[k] for k in (
        "x", "w_in", "gm_v_gain", "mla_w_uq", "mla_w_ukv", "mla_q_gain", "mla_k_gain", "w_out", "conv_w_pw2",
        "conv_b_pw2")}

    def on_partitions(*vectors):
        return _np.stack([v.reshape(-1, 128).T for v in vectors], axis=1)

    arrays["positions"] = a["positions"][0].reshape(2, 128).T
    arrays["norm_gains"] = on_partitions(a["mix_norm_even"][0], a["ffn_norm"][0], a["mix_norm_odd"][0], a["ffn_norm"][1])
    arrays["latent_gains"] = _np.concatenate([a["mla_q_lat_gain"][0].reshape(3, 128).T,
                                              a["mla_kv_lat_gain"][0].reshape(2, 128).T], axis=1)
    arrays["conv_columns"] = on_partitions(a["conv_b_pw1"][0, 0:1024], a["conv_b_pw1"][0, 1024:2048],
                                           a["conv_b_dw"][0], a["conv_norm_gain"][0])
    arrays["gm_w_sT"] = a["gm_w_s"][0].transpose(2, 0, 1)
    arrays["gm_b_sT"] = a["gm_b_s"][0].T
    arrays["conv_w_pw1"] = pw1
    arrays["conv_w_dwT"] = a["conv_w_dw"][0].reshape(31, 8, 128).transpose(2, 1, 0)
    arrays["peer_w_q"] = _np.stack([columns(w) for w in a["peer_w_q"]])
    arrays["peer_keysT"] = a["peer_sub_keys"].transpose(0, 4, 2, 1, 3).reshape(2, 128, 16, 128)
    arrays["peer_u"] = a["peer_u"].reshape(2, 128, 128, 8, 128).transpose(0, 2, 4, 3, 1).reshape(2, 128, 128, 1024)
    arrays["peer_v"] = a["peer_v"].reshape(2, 128, 128, 1024).transpose(0, 2, 1, 3)
    arrays = {k: _np.ascontiguousarray(v) for k, v in arrays.items()}

    nc = _bacc.Bacc("TRN2", target_bir_lowering=False, num_devices=1)
    t = {k: nc.dram_tensor(k, v.shape, _mybir.dt.from_np(v.dtype), kind="ExternalInput").ap() for k, v in arrays.items()}
    t["out"] = nc.dram_tensor("out", (1, 256, 1024), _mybir.dt.float32, kind="ExternalOutput").ap()
    build(nc, t)
    r = _run(nc, [arrays], core_ids=[0])
    return r.results[0]["out"]
```

```python
from contextlib import ExitStack

import numpy as np

import concourse.bass as bass
from concourse import mybir

ALU = mybir.AluOpType
ACT = mybir.ActivationFunctionType
AX = mybir.AxisListType
F32 = mybir.dt.float32
F32R = mybir.dt.float32r
U32 = mybir.dt.uint32
I32 = mybir.dt.int32

P = 128
D = 1024
SEQ = 256
NBLK = SEQ // P
KC = D // P
EPS = 1e-6
NEG = -1e30

GH, GD = 8, 64
MH, NOPE, ROPE, VD = 8, 64, 32, 64
QK = NOPE + ROPE
HALF = ROPE // 2
QRANK, KVRANK = 384, 256
LAT = QRANK + KVRANK + ROPE
INW = 2 * GH * GD + LAT
QCH, KVCH = QRANK // P, KVRANK // P
THETA = 10000.0

TAPS = 31

PH = 8
NKEYS = 128
TOPK = 16
LISTS = 2 * PH
UNITS = NBLK * PH
ROWS = [(0, 1, 16), (1, 3, 8), (4, 12, 3)]
ROW_START = [0] + [16 + 8 * (a - 1) for a in range(1, 4)] + [40 + 3 * (a - 4) for a in range(4, 16)]
CANDS = 76
PICK_SLABS = 64
GATE_SLAB = PICK_SLABS + 4
SCRATCH_SLAB = 96
GATED = NKEYS - GATE_SLAB
PICK_STEPS = 45
LISTS_READ = 20

SLAB = 1024
RAW = 4
PARTS = 4
AHEAD = 3
W_SLOTS = 4
DVE_CONV = 5
DVE_TAPS = 23
PE_SHARES = [(5, 0), (4, DVE_TAPS), (6, 0), (7, 0)]
CONV_ORDER = [0, 1, 2, 3, 5, 6, 4, 7]


def slab_plan():
    plan, first = [], {}

    def add(name, count, width):
        first[name] = len(plan)
        plan.extend((name, k, width) for k in range(count))

    add("w_in_lat", KC, LAT)
    add("w_in_gm", KC, 1024)
    add("w_uq", QCH, MH * QK)
    add("w_ukv", KVCH, MH * (NOPE + VD))
    add("w_out", KC, D)
    for layer in range(2):
        if layer:
            add("pw1", 2 * KC, SLAB)
            add("pw2", KC, D)
        add(f"w_q{layer}", LISTS, SLAB)
        add(f"u{layer}", NKEYS, SLAB)
        add(f"v{layer}", NKEYS, SLAB)
    return plan, first


def build(nc, t):
    plan, first = slab_plan()
    NSLAB = len(plan)

    ctx = ExitStack()
    with ctx:
        def sb(name, shape, dt=F32):
            return ctx.enter_context(nc.sbuf_tensor(name, shape, dt))

        sems = {}

        def S(name):
            if name not in sems:
                sems[name] = ctx.enter_context(nc.semaphore(name))
            return sems[name]

        big = sb("big", [P, NKEYS * SEQ])
        x_res = sb("x_res", [P, NBLK, D])
        hT_hi = sb("hT_hi", [P, KC, SEQ], F32R)
        hT_lo = sb("hT_lo", [P, KC, SEQ], F32R)
        raw = sb("raw", [P, RAW, SLAB])
        part_hi = sb("part_hi", [P, PARTS, SLAB], F32R)
        part_lo = sb("part_lo", [P, PARTS, SLAB], F32R)
        ident = sb("ident", [P, P])
        iota = sb("iota", [P, P])
        norm_gain = sb("norm_gain", [P, 4, KC])
        lat_gain = sb("lat_gain", [P, QCH + KVCH])
        conv_cols = sb("conv_cols", [P, 4, KC])
        stat = sb("stat", [P, 4, 4])
        warm = sb("warm", [P, 2])
        eps = sb("eps", [P, 1])
        act_j = sb("act_j", [P, 2, 4])
        row_start = sb("row_start", [P, TOPK])
        row_step = sb("row_step", [P, TOPK - 1])
        pick_i = sb("pick_i", [P, UNITS, TOPK])
        pick_j = sb("pick_j", [P, UNITS, TOPK])
        pick_s = sb("pick_s", [P, UNITS, TOPK])
        gate_sum = sb("gate_sum", [P, 2, UNITS])
        pickT = sb("pickT", [P, 3, SEQ])
        x_hold = nc.dram_tensor("x_hold", (P, NBLK * D), F32, kind="Internal").ap()
        hots_mem = x_res[:, :, :].rearrange("p b (s k c) -> p b s k c", s=2, c=P)
        hot_i, hot_j = hots_mem[:, 0], hots_mem[:, 1]
        bank = [ctx.enter_context(nc.psum_tensor(f"bank{b}", [P, 512], F32)) for b in range(8)]

        used = [0]

        def part_of_big(*shape):
            n = int(np.prod(shape))
            v = big[:, used[0]:used[0] + n]
            used[0] += n
            assert used[0] <= NKEYS * SEQ
            if len(shape) == 2:
                return v.rearrange("p (a b) -> p a b", b=shape[1])
            if len(shape) == 3:
                return v.rearrange("p (a b c) -> p a b c", b=shape[1], c=shape[2])
            if len(shape) == 4:
                return v.rearrange("p (a b c d) -> p a b c d", b=shape[1], c=shape[2], d=shape[3])
            return v

        m_u = part_of_big(NBLK, 512)
        m_v = part_of_big(NBLK, 512)
        m_vsq = part_of_big(NBLK, 512)
        m_lat = part_of_big(NBLK, LAT)
        m_ws = part_of_big(GH, P)
        m_vgain = part_of_big(512)
        m_qkgain = part_of_big(2, QK)
        m_bs = part_of_big(GH)
        m_qk = part_of_big(NBLK * 2, MH, QK)
        m_val = part_of_big(NBLK, MH, VD)
        m_sq = part_of_big(NBLK * 2, MH, QK)
        m_qkT = part_of_big(2, MH, SEQ)
        m_p = part_of_big(MH, 3 * P)
        m_pT = part_of_big(MH, 3, P)
        m_cat = part_of_big(NBLK, D)
        m_mask = part_of_big(3 * P)
        m_rt = part_of_big(2 * 4, NBLK, MH, HALF)
        m_ang = part_of_big(8, NBLK, HALF)
        m_freq = part_of_big(HALF)
        m_posi = part_of_big(NBLK)
        m_pos = part_of_big(NBLK)
        m_st = part_of_big(12, 2 * UNITS)

        act_all = big[:, :].rearrange("p (j t) -> p j t", t=SEQ)
        used[0] = NKEYS * SEQ // 2
        h_tok = part_of_big(NBLK, D)
        qT = part_of_big(2, SEQ)
        keysT = part_of_big(LISTS, NKEYS)
        assert used[0] <= SCRATCH_SLAB * SEQ
        used[0] = SCRATCH_SLAB * SEQ
        scores = part_of_big(UNITS, 2 * NKEYS)
        stage = part_of_big(2, 2, 2, NKEYS)
        top_v = part_of_big(2, 2, TOPK)
        top_iu = part_of_big(2, 2, TOPK).bitcast(U32)
        top_if = part_of_big(2, 2, TOPK)
        cand = part_of_big(2, CANDS)
        best_v = part_of_big(2, TOPK)
        best_pu = part_of_big(2, TOPK).bitcast(U32)
        best_p = part_of_big(2, TOPK)
        step_i = part_of_big(2, TOPK)
        col_b = part_of_big(2, TOPK)
        sum_i = part_of_big(2, TOPK)
        sum_r = part_of_big(2, TOPK)
        dec_ge = part_of_big(2, TOPK, TOPK)
        dec_m = part_of_big(2, TOPK, TOPK)
        dec_n = part_of_big(2, TOPK, TOPK)
        dec_e = part_of_big(2, TOPK, TOPK)
        assert used[0] <= NKEYS * SEQ

        used[0] = 0
        c_pad = part_of_big(KC, TAPS - 1 + SEQ)
        c_sig = part_of_big(2, SEQ)
        c_acc = part_of_big(KC, SEQ)
        c_sq = part_of_big(KC, SEQ)
        c_odd = part_of_big(2, SEQ)
        c_std = part_of_big(SEQ)
        c_rstd = part_of_big(SEQ)
        c_bias2 = part_of_big(D)
        ones = part_of_big(P)
        taps = part_of_big(KC, TAPS)
        diags = [(c, k) for c, k0 in PE_SHARES for k in range(k0, TAPS)]
        c_diag = part_of_big(len(diags), P)

        def slab_src(name, k):
            if name == "w_in_gm":
                return t["w_in"][0, k * P:(k + 1) * P, 0:1024]
            if name == "w_in_lat":
                return t["w_in"][0, k * P:(k + 1) * P, 1024:INW]
            if name == "w_uq":
                return t["mla_w_uq"][0, k * P:(k + 1) * P, :]
            if name == "w_ukv":
                return t["mla_w_ukv"][0, k * P:(k + 1) * P, :]
            if name == "w_out":
                return t["w_out"][0, k * P:(k + 1) * P, :]
            if name == "pw2":
                return t["conv_w_pw2"][0, k * P:(k + 1) * P, :]
            src = {"pw1": t["conv_w_pw1"]}.get(name)
            if src is None:
                src = t[{"w_q": "peer_w_q", "u": "peer_u", "v": "peer_v"}[name[:-1]]][int(name[-1])]
            return src[bass.ds(k, 1)].rearrange("a p n -> (a p) n")

        def load_slab(sp, name, k, n, width, i=0):
            if n >= RAW:
                sp.wait_ge(S("slab_lo"), n - RAW + 1 + 4 * i)
            sp.dma_start(raw[:, n % RAW, 0:width], slab_src(name, k)).then_inc(S(f"slab_landed{n % RAW}"), 16)

        def split_hi(act, n, i=0):
            w = plan[n][2]
            act.wait_ge(S(f"slab_landed{n % RAW}"), 16 * (n // RAW + 1) + 16 * i)
            if n >= PARTS:
                act.wait_ge(S("slab_used"), n - PARTS + 1 + 4 * i)
            act.activation(part_hi[:, n % PARTS, 0:w], raw[:, n % RAW, 0:w], ACT.Copy).then_inc(S("slab_hi"), 1)

        def split_lo(dve, n, i=0):
            w = plan[n][2]
            dve.wait_ge(S("slab_hi"), n + 1 + 4 * i)
            dve.tensor_tensor(part_lo[:, n % PARTS, 0:w], raw[:, n % RAW, 0:w],
                              part_hi[:, n % PARTS, 0:w].bitcast(F32), ALU.subtract).then_inc(S("slab_lo"), 1)

        def ahead_hi(act, n, i=0):
            if not (isinstance(i, int) and n + AHEAD + 4 * i >= NSLAB):
                split_hi(act, n + AHEAD, i)

        def ahead_lo(dve, n, i=0):
            if not (isinstance(i, int) and n + AHEAD + 4 * i >= NSLAB):
                split_lo(dve, n + AHEAD, i)

        def matmul3(pe, out, a_hi, a_lo, b_hi, b_lo, start, stop):
            pe.matmul(out, a_hi, b_hi, start=start, stop=False)
            pe.matmul(out, a_hi, b_lo, start=False, stop=False)
            return pe.matmul(out, a_lo, b_hi, start=False, stop=stop)

        def rows_product(pe, name, cols, ready, ks, total, chunk0=0, ready0=0, banks=0):
            for m, k in enumerate(ks):
                n = first[name] + k
                pe.wait_ge(S("slab_lo"), n + 1)
                pe.wait_ge(S(ready), ready0 + m + 1)
                for blk in range(NBLK):
                    for c, (a, b) in enumerate(cols):
                        tk = slice(blk * P, (blk + 1) * P)
                        mm = matmul3(pe, bank[banks + 2 * blk + c][:, 0:b - a], hT_hi[:, chunk0 + m, tk],
                                     hT_lo[:, chunk0 + m, tk], part_hi[:, n % PARTS, a:b],
                                     part_lo[:, n % PARTS, a:b], k == 0, k == total - 1)
                    if blk == 0 and k == total - 1 and name in ("w_out", "pw2"):
                        mm.then_inc(S("half_done"), 1)
                mm.then_inc(S("slab_used"), 1)

        def cols_product(pe, n, out, i=0, ready=None):
            pe.wait_ge(S("slab_lo"), n + 1 + 4 * i)
            for c in range(KC):
                if ready:
                    pe.wait_ge(S(ready), c + 1)
                w = slice(c * P, (c + 1) * P)
                mm = matmul3(pe, out, part_hi[:, n % PARTS, w], part_lo[:, n % PARTS, w],
                             hT_hi[:, c, :], hT_lo[:, c, :], c == 0, c == KC - 1)
            mm.then_inc(S("slab_used"), 1)

        def norm_act(act, g):
            act.activation(warm[:, 0:1], warm[:, 1:2], ACT.Sqrt)
            for blk in range(NBLK):
                if g == 0:
                    act.wait_ge(S(f"x_loaded{blk}"), 16)
                else:
                    act.wait_ge(S("x_ready" if blk else "x_half_ready"), g)
                act.activation(h_tok[:, blk, :], x_res[:, blk, :], ACT.Square,
                               accum_out=stat[:, g, blk:blk + 1]).then_inc(S("x_squared"), 1)
                act.wait_ge(S("x_squared"), NBLK * g + blk + 1)
                act.activation(stat[:, g, 2 + blk:3 + blk], stat[:, g, blk:blk + 1], ACT.Sqrt, bias=eps[:, :],
                               scale=1.0 / D).then_inc(S("x_std"), 1)
            if g % 2:
                act.dma_start(x_hold, x_res[:, :, :].rearrange("p b d -> p (b d)")).then_inc(S("x_saved"), 16)

        def norm_dve(dve, g):
            for blk in range(NBLK):
                dve.wait_ge(S("x_std"), NBLK * g + blk + 1)
                dve.reciprocal(stat[:, g, blk:blk + 1], stat[:, g, 2 + blk:3 + blk]).then_inc(S("x_rstd"), 1)
                dve.wait_ge(S("x_rstd"), NBLK * g + blk + 1)
                dve.tensor_scalar(h_tok[:, blk, :], x_res[:, blk, :], stat[:, g, blk:blk + 1], None,
                                  ALU.mult).then_inc(S("h_ready"), 1)

        def norm_pe(pe, g):
            for blk in range(NBLK):
                pe.wait_ge(S("h_ready"), NBLK * g + blk + 1)
                for c in range(KC):
                    a = pe.transpose(bank[norm_banks(g)[c // 2]][:, (c % 2 * NBLK + blk) * P:(c % 2 * NBLK + blk + 1) * P],
                                     h_tok[:, blk, c * P:(c + 1) * P], ident[:, :])
                    if blk == NBLK - 1:
                        a.then_inc(S(f"n{g}_t"), 1)

        def pw1_bank(c):
            return (4 + 2 * c) % 8

        def conv_steps(c):
            return (TAPS + 1) * (c + 1) if c < DVE_CONV - 1 else (TAPS + 1) * c + DVE_TAPS + 2

        def norm_gains(g):
            return [norm_gain[:, g, c:c + 1] for c in range(KC)]

        def norm_banks(g):
            return [4, 5, 6, 7] if g == 0 else [0, 1, 2, 3]

        def transposed_pe(pe, src, chunks, tag, banks=(6, 7), at=0):
            for c in range(chunks):
                r, half = c // 2, c % 2
                if half == 0 and r >= len(banks):
                    pe.wait_ge(S(f"{tag}_lo"), min(2 * (r - len(banks) + 1), chunks))
                for blk in range(NBLK):
                    a = pe.transpose(bank[banks[r % len(banks)]][:, (2 * half + blk) * P:(2 * half + blk + 1) * P],
                                     src[:, blk, (at + c) * P:(at + c + 1) * P], ident[:, :])
                a.then_inc(S(f"{tag}_t"), 1)

        def transposed_act(act, gains, tag, banks=(6, 7), at=0):
            n = len(gains)
            for c in range(n):
                act.wait_ge(S(f"{tag}_t"), min(2 * (c // 2) + 2, n))
                act.activation(hT_hi[:, at + c, :], bank[banks[c // 2 % len(banks)]][:, c % 2 * SEQ:(c % 2 + 1) * SEQ], ACT.Copy,
                               scale=gains[c] if gains[c] is not None else 1.0).then_inc(S(f"{tag}_hi"), 1)

        def transposed_dve(dve, gains, tag, banks=(6, 7), at=0):
            n = len(gains)
            for c in range(n):
                dve.wait_ge(S(f"{tag}_hi"), min(2 * (c // 2) + 2, n))
                src = bank[banks[c // 2 % len(banks)]][:, c % 2 * SEQ:(c % 2 + 1) * SEQ]
                dve.scalar_tensor_tensor(out=hT_lo[:, at + c, :], in0=src, scalar=gains[c] if gains[c] is not None else 1.0,
                                         in1=hT_hi[:, at + c, :].bitcast(F32), op0=ALU.mult,
                                         op1=ALU.subtract).then_inc(S(f"{tag}_lo"), 1)

        def qk_of(mem, w):
            return mem.rearrange("p (b w) h d -> p b w h d", w=2)[:, :, w]

        def stat_of(row, w):
            return m_st[:, row, w * UNITS:(w + 1) * UNITS].rearrange("p (b h) -> p b h", h=MH)

        def normed(eng, w, step):
            v = qk_of(m_qk, w)
            step(eng.tensor_tensor(v, v, stat_of(10, w).unsqueeze(3).broadcast_to([P, NBLK, MH, QK]), ALU.mult))

        def gained(eng, w, step):
            v = qk_of(m_qk, w)
            step(eng.tensor_tensor(v, v, m_qkgain[:, w, :].unsqueeze(1).unsqueeze(1).broadcast_to([P, NBLK, MH, QK]), ALU.mult))

        def rope(eng, w, step):
            v = qk_of(m_qk, w)
            x1, x2 = v[:, :, :, NOPE:NOPE + HALF], v[:, :, :, NOPE + HALF:QK]
            sin, cos = (m_ang[:, k, :, :].unsqueeze(2).broadcast_to([P, NBLK, MH, HALF]) for k in (6, 7))
            for k, (xx, cs) in enumerate(((x1, cos), (x2, sin), (x1, sin), (x2, cos))):
                a = eng.tensor_tensor(m_rt[:, 4 * w + k], xx, cs, ALU.mult)
            step(a)
            eng.tensor_tensor(x1, m_rt[:, 4 * w], m_rt[:, 4 * w + 1], ALU.subtract)
            return eng.tensor_tensor(x2, m_rt[:, 4 * w + 2], m_rt[:, 4 * w + 3], ALU.add)

        block = ctx.enter_context(nc.Block())

        @block.sync
        def _(sp):
            for blk in range(NBLK):
                sp.dma_start(x_res[:, blk, :], t["x"][0, blk * P:(blk + 1) * P, :]).then_inc(S(f"x_loaded{blk}"), 16)
            for n in range(first["w_q0"]):
                load_slab(sp, plan[n][0], plan[n][1], n, plan[n][2])

            def loop(name, count):
                with sp.Fori(0, count // 4) as i:
                    for u in range(4):
                        load_slab(sp, name, 4 * i + u, first[name] + u, SLAB, i)

            for layer in range(2):
                if layer:
                    loop("pw1", 2 * KC)
                    for k in range(KC):
                        load_slab(sp, "pw2", k, first["pw2"] + k, D)
                loop(f"w_q{layer}", LISTS)
                loop(f"u{layer}", NKEYS)
                loop(f"v{layer}", NKEYS)
            for blk in range(NBLK):
                sp.wait_ge(S("x_ready" if blk else "x_half_ready"), 4)
                sp.dma_start(t["out"][0, blk * P:(blk + 1) * P, :], x_res[:, blk, :]).then_inc(S("stored"), 16)
            sp.wait_ge(S("stored"), 16 * NBLK)

        @block.gpsimd
        def _(pool):
            small = [
                ("in_ng", norm_gain[:, :, :], t["norm_gains"]),
                ("in_lg", lat_gain[:, :], t["latent_gains"]),
                ("in_pos", m_posi.bitcast(I32), t["positions"]),
                ("in_vg", m_vgain, t["gm_v_gain"].rearrange("a h d -> a (h d)").broadcast_to([P, 512])),
                ("in_qkg", m_qkgain[:, 0, :], t["mla_q_gain"].broadcast_to([P, QK])),
                ("in_qkg", m_qkgain[:, 1, :], t["mla_k_gain"].broadcast_to([P, QK])),
                ("in_ws", m_ws, t["gm_w_sT"]),
                ("in_bs", m_bs, t["gm_b_sT"]),
                ("in_cc", conv_cols[:, :, :], t["conv_columns"]),
            ]
            pool.memset(ident[:, :], 0.0).then_inc(S("pool_step"), 1)
            pool.wait_ge(S("pool_step"), 1)
            pool.affine_select(out=ident[:, :], in_=ident[:, :], compare_op=ALU.not_equal, fill=1.0, base=0,
                               pattern=[[-1, P]], channel_multiplier=1).then_inc(S("c_ident"), 1)
            pool.memset(eps[:, :], EPS)
            pool.memset(warm[:, :], 1.0).then_inc(S("c_warm"), 1)
            for s, dst, src in small:
                pool.dma_start(dst, src).then_inc(S(s), 16)
            pool.iota(iota[:, :], pattern=[[1, P]], base=0, channel_multiplier=0,
                      allow_small_or_imprecise_dtypes=True).then_inc(S("c_iota"), 1)
            pool.memset(row_step[:, :], 0.0).then_inc(S("fbank_free"), 2)
            pool.wait_ge(S("fbank_free"), 2)
            for k in range(HALF):
                f = pool.memset(m_freq[:, k:k + 1], float(np.float32(THETA) ** (-np.float32(k) / np.float32(HALF))))
            f.then_inc(S("c_freq"), 1)
            for a in range(TOPK):
                pool.memset(row_start[:, a:a + 1], float(ROW_START[a]))
                if a:
                    f = pool.memset(row_step[:, a - 1:a], float(ROW_START[a] - ROW_START[a - 1]))
            f.then_inc(S("c_rows"), 1)
            pool.memset(m_mask, 0.0).then_inc(S("pool_step"), 1)
            pool.wait_ge(S("pool_step"), 2)
            pool.affine_select(out=m_mask[:, 0:P], in_=m_mask[:, 0:P], compare_op=ALU.is_ge, fill=NEG, base=0,
                               pattern=[[-1, P]], channel_multiplier=1)
            pool.affine_select(out=m_mask[:, 2 * P:3 * P], in_=m_mask[:, 2 * P:3 * P], compare_op=ALU.is_ge, fill=NEG,
                               base=0, pattern=[[-1, P]], channel_multiplier=1).then_inc(S("c_mask"), 1)
            pool.wait_ge(S("in_ws"), 16)
            pool.affine_select(out=m_ws, in_=m_ws, compare_op=ALU.is_ge, fill=0.0, base=0,
                               pattern=[[0, GH], [1, P]], channel_multiplier=-1).then_inc(S("ws_causal"), 1)
            steps = [0]

            def step(ins):
                steps[0] += 1
                ins.then_inc(S("pool_chain"), 1)
                pool.wait_ge(S("pool_chain"), steps[0])

            pool.wait_ge(S("gm_rstd"), 1)
            pool.wait_ge(S("gm_gelu"), 4)
            v3 = m_v.rearrange("p a (h d) -> p (a h) d", d=GD)
            step(pool.tensor_tensor(v3, v3, m_st[:, 7, 0:16].unsqueeze(2).broadcast_to([P, 16, GD]), ALU.mult))
            pool.wait_ge(S("in_vg"), 16)
            pool.tensor_tensor(m_v, m_v, m_vgain.unsqueeze(1).broadcast_to([P, NBLK, 512]), ALU.mult).then_inc(S("v_normed"), 1)
            pool.wait_ge(S("in_qkg"), 32)
            pool.wait_ge(S("q_rstd"), 1)
            normed(pool, 0, step)
            gained(pool, 0, step)
            pool.wait_ge(S("sincos"), 1)
            rope(pool, 0, step).then_inc(S("q_roped"), 1)
            for layer in range(2):
                if layer:
                    pool.wait_ge(S("x_ready"), 2)
                    pool.dma_start(taps, t["conv_w_dwT"]).then_inc(S("in_taps"), 16)
                    pool.memset(c_pad[:, :, 0:TAPS - 1], 0.0)
                    pool.memset(ones, 1.0).then_inc(S("c_padded"), 1)
                    pool.dma_start(c_bias2, t["conv_b_pw2"].broadcast_to([P, D])).then_inc(S("in_b2"), 16)
                    pool.wait_ge(S("conv_tapped"), len(PE_SHARES))
                else:
                    pool.wait_ge(S("x_ready"), 1)
                pool.dma_start(keysT, t["peer_keysT"][layer]).then_inc(S("in_keys"), 16)

                def fourth_lo(i):
                    n = first[f"u{layer}"] + 3
                    pool.wait_ge(S("slab_lo"), n + 4 * i)
                    pool.wait_ge(S("slab_hi"), n + 1 + 4 * i)
                    pool.sem_inc(S("pool_waits_passed"), 1)
                    pool.tensor_tensor(part_lo[:, n % PARTS, :], raw[:, n % RAW, :], part_hi[:, n % PARTS, :].bitcast(F32),
                                       ALU.subtract).then_inc(S("slab_lo"), 1)

                fourth_lo(0)
                pool.wait_ge(S(f"scored{layer}"), LISTS)
                pool.memset(act_all[:, GATE_SLAB:SCRATCH_SLAB, :], 1.0)
                with pool.Fori(1, PICK_SLABS // 4) as i:
                    fourth_lo(i)
                pool.wait_ge(S(f"picked{layer}"), PICK_STEPS * UNITS // 2)
                pool.memset(act_all[:, SCRATCH_SLAB:, :], 1.0).then_inc(S("act_ones"), 1)

        def conv_act(act):
            n0 = first["pw1"]
            norm_act(act, 2)
            transposed_act(act, norm_gains(2), "n2", norm_banks(2))
            act.activation(warm[:, 0:1], warm[:, 1:2], ACT.Sigmoid)
            act.wait_ge(S("in_taps"), 16)
            act.wait_ge(S("in_cc"), 16)
            left = list(enumerate(diags))

            def diagonal():
                m, (c, k) = left.pop(0)
                act.activation(c_diag[:, m, :], ident[:, :], ACT.Copy, scale=taps[:, c, k:k + 1]).then_inc(S("diag"), 1)

            for c in range(KC):
                ahead_hi(act, n0 + 2 * c)
                for _ in range(8):
                    diagonal()
                ahead_hi(act, n0 + 2 * c + 1)
                act.wait_ge(S("slab_used"), n0 + 2 * c + 2)
                if c >= 2:
                    act.wait_ge(S("glu"), c - 1)
                act.activation(c_sig[:, c % 2, :], bank[pw1_bank(c) + 1][:, 0:SEQ], ACT.Sigmoid,
                               bias=conv_cols[:, 1, c:c + 1]).then_inc(S("sig_ready"), 1)
            while left:
                diagonal()
            act.activation(warm[:, 0:1], warm[:, 1:2], ACT.Sqrt)
            for c in CONV_ORDER:
                if c >= DVE_CONV:
                    act.wait_ge(S("conv_tapped"), PE_SHARES.index((c, 0)) + 1)
                    act.activation(c_acc[:, c, :], bank[4 + c - DVE_CONV][:, 0:SEQ], ACT.Identity,
                                   bias=conv_cols[:, 2, c:c + 1]).then_inc(S("conv_out"), 1)
                    act.wait_ge(S("conv_out"), c - DVE_CONV + 1)
                else:
                    act.wait_ge(S("tap_done"), conv_steps(c))
                act.activation(c_sq[:, c, :], c_acc[:, c, :], ACT.Square).then_inc(S("conv_squared"), 1)
            act.wait_ge(S("conv_var"), 1)
            act.activation(c_std, c_std, ACT.Sqrt).then_inc(S("conv_std"), 1)
            act.activation(warm[:, 0:1], warm[:, 1:2], ACT.Silu)
            for c in range(KC):
                act.wait_ge(S("conv_normed"), c + 1)
                act.activation(hT_hi[:, c, :], c_sq[:, c, :], ACT.Silu)
                act.activation(c_acc[:, c, :], c_sq[:, c, :], ACT.Silu).then_inc(S("conv_silu"), 1)
            for k in range(KC):
                ahead_hi(act, first["pw2"] + k)

        def peer_act(act, layer):
            norm_act(act, 1 + 2 * layer)
            transposed_act(act, norm_gains(1 + 2 * layer), f"n{1 + 2 * layer}", norm_banks(1 + 2 * layer))
            nq, nu, nv = first[f"w_q{layer}"], first[f"u{layer}"], first[f"v{layer}"]
            with act.Fori(0, 2) as i:
                for u in range(8):
                    ahead_hi(act, nq + u, 2 * i)
                    act.wait_ge(S("slab_used"), nq + u + 1 + 8 * i)
                    if u >= 2:
                        act.wait_ge(S(f"scored{layer}"), 8 * i + u - 1)
                    act.activation(qT[:, u % 2, :], bank[4 + u % 2][:, 0:SEQ], ACT.Copy).then_inc(S("fbank_free"), 1)
                    if u in (4, 7):
                        r = u // 4 - (u == 4)
                        act.wait_ge(S(f"scored{layer}"), 8 * i + (4 if u == 4 else 8))
                        for blk in range(NBLK):
                            a = act.activation(scores[:, bass.ds(blk * PH + 4 * i + 2 * r, 2), :],
                                               bank[2 * r + blk][:, :].rearrange("p (h n) -> p h n", h=2), ACT.Copy)
                        a.then_inc(S(f"scores_out{layer}"), 1)

            def expert(u, i):
                ahead_hi(act, nu + u, 4 * i)
                act.wait_ge(S("slab_used"), nu + u + 1 + 16 * i)
                act.activation(act_all[:, bass.ds(16 * i + u, 1), :], bank[4 + u % 2][:, 0:SEQ].rearrange("p (a t) -> p a t", a=1),
                               ACT.Gelu_apprx_tanh).then_inc(S("fbank_free"), 1)

            def staged(pair, slot):
                act.activation(stage[:, slot].rearrange("p h c n -> p h (c n)"), scores[:, bass.ds(2 * pair, 2), :],
                               ACT.Copy).then_inc(S(f"staged{layer}"), 1)

            def sixteen(i, more):
                for u in range(16):
                    expert(u, i)
                    if more and u in (9, 15):
                        half = u // 15
                        act.wait_ge(picked, PICK_STEPS * (2 * i + half) + LISTS_READ)
                        staged(2 * i + 2 + half, half)

            picked = S(f"picked{layer}")
            act.wait_ge(S(f"scores_out{layer}"), 4)
            staged(0, 0)
            staged(1, 1)
            act.activation(warm[:, 0:1], warm[:, 1:2], ACT.Gelu_apprx_tanh)
            with act.Fori(0, PICK_SLABS // 16 - 1) as i:
                sixteen(i, True)
            sixteen(PICK_SLABS // 16 - 1, False)
            for u in range(4):
                expert(u, PICK_SLABS // 16)
                if u == 1:
                    act.wait_ge(S(f"gate_shift{layer}"), 1)
                    act.activation(pick_s[:, :, :], pick_s[:, :, :], ACT.Exp).then_inc(S(f"gate_exp{layer}"), 1)
                    act.activation(warm[:, 0:1], warm[:, 1:2], ACT.Gelu_apprx_tanh)

            def hots(g, slot):
                act.activation(act_j[:, slot, :], pickT[:, 1, bass.ds(4 * g, 4)], ACT.Copy, scale=-1.0).then_inc(S(f"act_j{layer}"), 1)
                act.wait_ge(S(f"act_j{layer}"), g + 1)
                for k in range(4):
                    a = act.activation(hot_j[:, slot, k, :], iota[:, :], ACT.Abs, bias=act_j[:, slot, k:k + 1])
                a.then_inc(S(f"far_j{layer}"), 1)
                act.wait_ge(S(f"far_j{layer}"), g + 1)
                act.activation(hot_j[:, slot, :, :], hot_j[:, slot, :, :], ACT.Relu, bias=warm[:, 1:2],
                               scale=-1.0).then_inc(S(f"hot_j{layer}"), 1)

            act.wait_ge(S(f"pickT{layer}"), 1)
            act.wait_ge(S("x_saved"), 16 * (layer + 1))
            hots(0, 0)
            hots(1, 1)

            def early_hi(u, blk):
                w = slice(blk * P, (blk + 1) * P)
                act.activation(hT_hi[:, u, w], act_all[:, u, w], ACT.Copy).then_inc(S(f"w_hi{layer}"), 1)

            def gelu_and_hots(i, last):
                for u in range(4):
                    n = nu + GATE_SLAB + u
                    ahead_hi(act, n, i)
                    act.wait_ge(S("slab_used"), n + 1 + 4 * i)
                    b = bank[4 + u % 2][:, 0:SEQ]
                    act.activation(b, b, ACT.Gelu_apprx_tanh).then_inc(S(f"gelued{layer}"), 1)
                    if last and u == 3:
                        act.wait_ge(S(f"gated{layer}"), SEQ // 8)
                        for k in range(W_SLOTS):
                            early_hi(k, 0)
                    act.wait_ge(S(f"gmat{layer}"), 4 * i + u + 1)
                    hots(4 * i + u + 2, u % 2)

            with act.Fori(0, GATED // 4 - 1) as i:
                gelu_and_hots(i, False)
            gelu_and_hots(GATED // 4 - 1, True)
            ahead_hi(act, nv)
            for g in range(GATED + 2, SEQ // 4):
                act.wait_ge(S(f"gmat{layer}"), g - 1)
                hots(g, g % 2)
            act.wait_ge(S(f"gated{layer}"), SEQ // 4)
            for u in range(W_SLOTS):
                early_hi(u, 1)
            act.wait_ge(S("x_saved"), 16 * (layer + 1))
            act.dma_start(x_res[:, :, :].rearrange("p b d -> p (b d)"), x_hold).then_inc(S("x_back"), 16)

            def weight_hi(u, i):
                if isinstance(i, int) and 4 * i + u >= NKEYS:
                    return
                act.wait_ge(S("slab_used"), nv + u - W_SLOTS + 1 + 4 * i)
                act.activation(hT_hi[:, u % W_SLOTS, :], act_all[:, bass.ds(4 * i + u, 1), :].rearrange("p a t -> p (a t)"),
                               ACT.Copy).then_inc(S(f"w_hi{layer}"), 1)

            def values(i):
                for u in range(4):
                    weight_hi(u + 2, i)
                    ahead_hi(act, nv + u, i)

            ahead_hi(act, nv + 1)
            weight_hi(4, 0)
            ahead_hi(act, nv + 2)
            weight_hi(5, 0)
            ahead_hi(act, nv + 3)
            with act.Fori(1, NKEYS // 4 - 1) as i:
                values(i)
            values(NKEYS // 4 - 1)

        @block.scalar
        def _(act):
            act.wait_ge(S("c_warm"), 1)
            norm_act(act, 0)
            for n in range(AHEAD):
                split_hi(act, n)
            act.wait_ge(S("in_ng"), 16)
            act.wait_ge(S("in_lg"), 16)
            transposed_act(act, norm_gains(0), "n0", norm_banks(0))

            nl, ng, nuq, nukv, no = (first[k] for k in ("w_in_lat", "w_in_gm", "w_uq", "w_ukv", "w_out"))
            for k in range(KC):
                ahead_hi(act, nl + k)
            act.wait_ge(S("slab_used"), ng)
            for blk in range(NBLK):
                act.activation(m_lat[:, blk, 0:512], bank[2 * blk][:, :], ACT.Copy)
                a = act.activation(m_lat[:, blk, 512:LAT], bank[2 * blk + 1][:, 0:LAT - 512], ACT.Copy)
            a.then_inc(S("lat_ready"), 1)
            ahead_hi(act, ng)
            act.wait_ge(S("lat_ready"), 1)
            for blk in range(NBLK):
                act.activation(m_sq[:, blk, 0:4, :], m_lat[:, blk, 0:QRANK], ACT.Square, accum_out=m_st[:, 0, blk:blk + 1])
                a = act.activation(m_sq[:, 2 + blk, 0:4, 0:64], m_lat[:, blk, QRANK:QRANK + KVRANK], ACT.Square,
                                   accum_out=m_st[:, 0, 2 + blk:3 + blk])
            a.then_inc(S("lat_squared"), 1)
            ahead_hi(act, ng + 1)
            act.wait_ge(S("lat_var"), 1)
            act.activation(m_st[:, 2, 0:4], m_st[:, 1, 0:4], ACT.Sqrt).then_inc(S("lat_std"), 1)
            ahead_hi(act, ng + 2)
            act.wait_ge(S("ang_ready"), 1)
            act.activation(m_ang[:, 6:8, :, :], m_ang[:, 4:6, :, :], ACT.Sin).then_inc(S("sincos"), 1)
            ahead_hi(act, ng + 3)
            for k in range(4, KC):
                ahead_hi(act, ng + k)
            act.wait_ge(S("slab_used"), nuq)
            transposed_act(act, [lat_gain[:, c:c + 1] for c in range(QCH + KVCH)], "lt", norm_banks(1))
            for dst, c in ((m_v, 1), (m_u, 0)):
                for blk in range(NBLK):
                    act.activation(dst[:, blk, :], bank[4 + 2 * blk + c][:, :], ACT.Gelu_apprx_tanh).then_inc(S("gm_gelu"), 1)
            ahead_hi(act, nuq)
            act.wait_ge(S("gm_gelu"), 2)
            act.activation(m_vsq, m_v, ACT.Square).then_inc(S("gm_squared"), 1)
            ahead_hi(act, nuq + 1)
            act.wait_ge(S("gm_var"), 1)
            act.activation(m_st[:, 4, 0:16], m_st[:, 3, 0:16], ACT.Sqrt).then_inc(S("gm_std"), 1)
            ahead_hi(act, nuq + 2)
            act.wait_ge(S("slab_used"), nukv)
            for blk in range(NBLK):
                for c in range(2):
                    a = act.activation(m_qk[:, 2 * blk, 4 * c:4 * c + 4, :], bank[2 * blk + c][:, 0:4 * QK], ACT.Copy)
            a.then_inc(S("qkv_out"), 1)
            act.wait_ge(S("qkv_out"), 1)
            act.activation(qk_of(m_sq, 0), qk_of(m_qk, 0), ACT.Square).then_inc(S("qk_squared"), 1)
            ahead_hi(act, nukv)
            act.wait_ge(S("qk_var"), 1)
            act.activation(m_st[:, 9, 0:16], m_st[:, 8, 0:16], ACT.Sqrt).then_inc(S("qk_std"), 1)
            ahead_hi(act, nukv + 1)
            act.wait_ge(S("slab_used"), no)
            for blk in range(NBLK):
                for c in range(2):
                    kv = bank[4 + 2 * blk + c][:, :].rearrange("p (h e) -> p h e", e=NOPE + VD)
                    a = act.activation(m_qk[:, 2 * blk + 1, 4 * c:4 * c + 4, 0:NOPE], kv[:, :, 0:NOPE], ACT.Copy)
            a.then_inc(S("qkv_out"), 1)
            act.wait_ge(S("qkv_out"), 2)
            act.wait_ge(S("k_pe"), 1)
            act.activation(qk_of(m_sq, 1), qk_of(m_qk, 1), ACT.Square).then_inc(S("qk_squared"), 1)
            for blk in range(NBLK):
                for c in range(2):
                    kv = bank[4 + 2 * blk + c][:, :].rearrange("p (h e) -> p h e", e=NOPE + VD)
                    a = act.activation(m_val[:, blk, 4 * c:4 * c + 4, :], kv[:, :, NOPE:], ACT.Copy)
            a.then_inc(S("qkv_out"), 1)
            act.wait_ge(S("qk_var"), 2)
            act.activation(m_st[:, 9, 16:32], m_st[:, 8, 16:32], ACT.Sqrt).then_inc(S("qk_std"), 1)
            transposed_act(act, [None] * 4, "cg")
            for k in range(4):
                ahead_hi(act, no + k)
            for r in range(8):
                act.wait_ge(S("qkT_t"), r + 1)
                which, blk, half = r // 4, r // 2 % 2, r % 2
                act.activation(m_qkT[0:QK, which, 4 * half:4 * half + 4, blk * P:(blk + 1) * P],
                               bank[6 + r % 2][0:QK, :].rearrange("p (h t) -> p h t", t=P), ACT.Copy).then_inc(S("qkT"), 1)
            for h in range(MH + 2):
                if h < MH:
                    act.wait_ge(S("s_max"), h + 1)
                    for blk, (a0, a1) in enumerate(((0, P), (P, 3 * P))):
                        a = act.activation(m_p[:, h, a0:a1], m_p[:, h, a0:a1], ACT.Exp, bias=m_st[:, 5 + blk, h:h + 1],
                                           accum_out=m_st[:, 11, blk * MH + h:blk * MH + h + 1])
                    a.then_inc(S("probs"), 1)
                if h >= 2:
                    act.wait_ge(S("pT_t"), h - 1)
                    act.activation(m_pT[:, h - 2, :, :], bank[6 + h % 2][:, 0:3 * P].rearrange("p (a t) -> p a t", t=P),
                                   ACT.Copy).then_inc(S("pT"), 1)
            transposed_act(act, [None] * 4, "ca", at=4)
            for k in range(4, KC):
                ahead_hi(act, no + k)

            for layer in range(2):
                if layer:
                    conv_act(act)
                peer_act(act, layer)

        def add_banks(dve, n, g):
            for blk in range(NBLK):
                if blk:
                    dve.wait_ge(S("slab_used"), n)
                else:
                    dve.wait_ge(S("half_done"), g)
                for c in range(2):
                    a = dve.tensor_tensor(x_res[:, blk, 512 * c:512 * (c + 1)], bank[2 * blk + c][:, :],
                                          x_res[:, blk, 512 * c:512 * (c + 1)], ALU.add)
                a.then_inc(S("x_ready" if blk else "x_half_ready"), 1)

        def conv_dve(dve):
            n0 = first["pw1"]
            norm_dve(dve, 2)
            transposed_dve(dve, norm_gains(2), "n2", norm_banks(2))
            dve.wait_ge(S("in_taps"), 16)
            dve.wait_ge(S("in_cc"), 16)
            dve.wait_ge(S("c_padded"), 1)

            def tap(c, k):
                acc = c_odd[:, c % 2, :] if k % 2 else c_acc[:, c, :]
                count = DVE_TAPS if c == DVE_CONV - 1 else TAPS
                if k == count + 1:
                    dve.wait_ge(S("tap_done"), STEPS * c + k)
                    dve.wait_ge(S("conv_tapped"), PE_SHARES.index((c, count)) + 1)
                    a = dve.tensor_tensor(c_acc[:, c, :], bank[3][:, 0:SEQ], c_acc[:, c, :], ALU.add)
                elif k == count:
                    dve.wait_ge(S("tap_done"), STEPS * c + k)
                    a = dve.tensor_tensor(c_acc[:, c, :], c_acc[:, c, :], c_odd[:, c % 2, :], ALU.add)
                elif k < 2:
                    if k == 0:
                        dve.wait_ge(S("glu"), c + 1)
                    elif c >= 2:
                        dve.wait_ge(S("tap_done"), STEPS * (c - 1))
                    z, w = c_pad[:, c, k:k + SEQ], taps[:, c, k:k + 1]
                    if k:
                        a = dve.tensor_scalar(acc, z, w, None, ALU.mult)
                    else:
                        a = dve.tensor_scalar(acc, z, w, conv_cols[:, 2, c:c + 1], ALU.mult, ALU.add)
                else:
                    dve.wait_ge(S("tap_done"), STEPS * c + k - 1)
                    a = dve.scalar_tensor_tensor(out=acc, in0=c_pad[:, c, k:k + SEQ], scalar=taps[:, c, k:k + 1], in1=acc,
                                                 op0=ALU.mult, op1=ALU.add)
                a.then_inc(S("tap_done"), 1)

            STEPS = TAPS + 1
            work = [(c, k) for c in range(DVE_CONV) for k in range(conv_steps(c) - STEPS * c)]
            for c in range(KC):
                ahead_lo(dve, n0 + 2 * c)
                ahead_lo(dve, n0 + 2 * c + 1)
                dve.wait_ge(S("sig_ready"), c + 1)
                dve.scalar_tensor_tensor(out=c_pad[:, c, TAPS - 1:], in0=bank[pw1_bank(c)][:, 0:SEQ],
                                         scalar=conv_cols[:, 0, c:c + 1], in1=c_sig[:, c % 2, :],
                                         op0=ALU.add, op1=ALU.mult).then_inc(S("glu"), 1)
                for _ in range(7):
                    tap(*work.pop(0))
            for c, k in work:
                tap(c, k)
            dve.wait_ge(S("in_b2"), 16)
            for blk in range(NBLK):
                a = dve.tensor_tensor(x_res[:, blk, :], x_res[:, blk, :], c_bias2, ALU.add)
            a.then_inc(S("bias2_added"), 1)
            dve.wait_ge(S("conv_summed"), 1)
            dve.tensor_scalar(c_std, bank[7][:, 0:SEQ], 1.0 / D, EPS, ALU.mult, ALU.add).then_inc(S("conv_var"), 1)
            dve.wait_ge(S("conv_std"), 1)
            dve.reciprocal(c_rstd, c_std).then_inc(S("conv_rstd"), 1)
            dve.wait_ge(S("conv_rstd"), 1)
            dve.wait_ge(S("conv_squared"), KC)
            for c in range(KC + 2):
                if c < KC:
                    dve.scalar_tensor_tensor(out=c_sq[:, c, :], in0=c_acc[:, c, :], scalar=conv_cols[:, 3, c:c + 1],
                                             in1=c_rstd, op0=ALU.mult, op1=ALU.mult).then_inc(S("conv_normed"), 1)
                if c >= 2:
                    dve.wait_ge(S("conv_silu"), c - 1)
                    dve.tensor_tensor(hT_lo[:, c - 2, :], c_acc[:, c - 2, :], hT_hi[:, c - 2, :].bitcast(F32),
                                      ALU.subtract).then_inc(S("conv_lo"), 1)
            for k in range(KC):
                ahead_lo(dve, first["pw2"] + k)
            dve.wait_ge(S("bias2_added"), 1)
            add_banks(dve, first["w_q1"], 3)

        def peer_dve(dve, layer):
            norm_dve(dve, 1 + 2 * layer)
            transposed_dve(dve, norm_gains(1 + 2 * layer), f"n{1 + 2 * layer}", norm_banks(1 + 2 * layer))
            nq, nu, nv = first[f"w_q{layer}"], first[f"u{layer}"], first[f"v{layer}"]
            with dve.Fori(0, LISTS // 4) as i:
                for u in range(4):
                    ahead_lo(dve, nq + u, i)

            SPLITS = PICK_SLABS * 2 // UNITS
            picked = S(f"picked{layer}")
            dve.wait_ge(S(f"scores_out{layer}"), 4)
            dve.wait_ge(S("c_rows"), 1)
            dve.wait_ge(S("c_iota"), 1)
            lists = [(h, c) for h in range(2) for c in range(2)]

            def pick(i, half):
                done, split, pair = [0], [0], 2 * i + half

                def step(ins):
                    done[0] += 1
                    ins.then_inc(picked, 1)
                    return done[0]

                def after(n):
                    dve.wait_ge(picked, PICK_STEPS * pair + n)

                def after8(n):
                    dve.wait_ge(picked, PICK_STEPS * pair + n)
                    dve.sem_inc(S("waits_passed"), 1)

                def slab():
                    n = SPLITS * half + split[0]
                    if n % 4 == 0:
                        n, split[0] = n + 1, split[0] + 1
                        dve.wait_ge(S("slab_lo"), nu + n + AHEAD + 2 * SPLITS * i)
                    ahead_lo(dve, nu + n, SPLITS // 2 * i)
                    split[0] += 1

                def per_row(v, n):
                    return v.unsqueeze(3).broadcast_to([P, 2, v.shape[2], n])

                def per_pick(v):
                    return v.unsqueeze(2).broadcast_to([P, 2, TOPK, v.shape[2]])

                slab()
                dve.wait_ge(S(f"staged{layer}"), pair + 1)
                dve.sem_inc(S("waits_passed"), 1)
                found = [step(dve.max(top_v[:, h, c, 0:8], stage[:, half, h, c, :])) for h, c in lists]
                after8(found[-1])
                for h, c in lists:
                    f = step(dve.max_index(top_iu[:, h, c, 0:8], top_v[:, h, c, 0:8], stage[:, half, h, c, :]))
                slab()
                after8(f)
                for h, c in lists:
                    f = step(dve.match_replace(stage[:, half, h, c, :], top_v[:, h, c, 0:8], stage[:, half, h, c, :], -3e38))
                after8(f)
                for h, c in lists:
                    f = step(dve.max(top_v[:, h, c, 8:16], stage[:, half, h, c, :]))
                slab()
                after8(f)
                for h, c in lists:
                    f = step(dve.max_index(top_iu[:, h, c, 8:16], top_v[:, h, c, 8:16], stage[:, half, h, c, :]))
                assert f == LISTS_READ
                at = 0
                for a0, rows, cols in ROWS:
                    for h in range(2):
                        s = dve.tensor_tensor(
                            cand[:, h, at:at + rows * cols].rearrange("p (a b) -> p a b", b=cols),
                            top_v[:, h, 0, a0:a0 + rows].unsqueeze(2).broadcast_to([P, rows, cols]),
                            top_v[:, h, 1, 0:cols].unsqueeze(1).broadcast_to([P, rows, cols]), ALU.add)
                    at += rows * cols
                summed = step(s)
                after(f)
                s = step(dve.tensor_copy(top_if, top_iu))
                after(s)
                step(dve.tensor_tensor(step_i[:, :, 0:15], top_if[:, :, 0, 1:16], top_if[:, :, 0, 0:15], ALU.subtract))
                after8(summed)
                for h in range(2):
                    f = step(dve.max(best_v[:, h, 0:8], cand[:, h, :]))
                after8(f)
                for h in range(2):
                    f = step(dve.max_index(best_pu[:, h, 0:8], best_v[:, h, 0:8], cand[:, h, :]))
                slab()
                after8(f)
                for h in range(2):
                    f = step(dve.match_replace(cand[:, h, :], best_v[:, h, 0:8], cand[:, h, :], -3e38))
                after8(f)
                for h in range(2):
                    f = step(dve.max(best_v[:, h, 8:16], cand[:, h, :]))
                slab()
                after8(f)
                for h in range(2):
                    f = step(dve.max_index(best_pu[:, h, 8:16], best_v[:, h, 8:16], cand[:, h, :]))
                after(f)
                f = step(dve.tensor_copy(best_p, best_pu))
                slab()
                after(f)
                ge = step(dve.tensor_tensor(dec_ge[:, :, :, 0:15], per_row(best_p, 15),
                                            row_start[:, 1:16].unsqueeze(1).unsqueeze(1).broadcast_to([P, 2, TOPK, 15]), ALU.is_ge))
                step(dve.tensor_copy(pick_s[:, bass.ds(2 * pair, 2), :], best_v))
                after(ge)
                m1 = step(dve.tensor_tensor(dec_m[:, :, :, 0:15], dec_ge[:, :, :, 0:15],
                                            row_step[:, :].unsqueeze(1).unsqueeze(1).broadcast_to([P, 2, TOPK, 15]), ALU.mult))
                m2 = step(dve.tensor_tensor(dec_n[:, :, :, 0:15], dec_ge[:, :, :, 0:15], per_pick(step_i[:, :, 0:15]), ALU.mult))
                after(m1)
                r1 = step(dve.tensor_reduce(sum_r, dec_m[:, :, :, 0:15], AX.X, ALU.add))
                after(m2)
                r2 = step(dve.tensor_reduce(sum_i, dec_n[:, :, :, 0:15], AX.X, ALU.add))
                after(r1)
                b = step(dve.tensor_tensor(col_b, best_p, sum_r, ALU.subtract))
                after(r2)
                step(dve.tensor_tensor(pick_i[:, bass.ds(2 * pair, 2), :], sum_i,
                                       top_if[:, :, 0, 0:1].broadcast_to([P, 2, TOPK]), ALU.add))
                after(b)
                e = step(dve.tensor_tensor(dec_e, per_row(col_b, TOPK), per_pick(iota[:, 0:TOPK].unsqueeze(1).broadcast_to([P, 2, TOPK])),
                                           ALU.is_equal))
                after(e)
                e = step(dve.tensor_tensor(dec_n, dec_e, per_pick(top_if[:, :, 1, :]), ALU.mult))
                after(e)
                step(dve.tensor_reduce(pick_j[:, bass.ds(2 * pair, 2), :], dec_n, AX.X, ALU.add))
                assert done[0] == PICK_STEPS and split[0] == SPLITS, (done, split)
                after(PICK_STEPS)

            with dve.Fori(0, UNITS // 4) as i:
                pick(i, 0)
                pick(i, 1)

            dve.tensor_tensor(pick_s[:, :, 1:16], pick_s[:, :, 1:16], pick_s[:, :, 0:1].broadcast_to([P, UNITS, 15]),
                              ALU.subtract).then_inc(S(f"gate_steps{layer}"), 1)
            dve.wait_ge(S(f"gate_steps{layer}"), 1)
            dve.tensor_tensor(pick_s[:, :, 0:1], pick_s[:, :, 0:1], pick_s[:, :, 0:1],
                              ALU.subtract).then_inc(S(f"gate_shift{layer}"), 1)
            for n in range(PICK_SLABS, PICK_SLABS + 2):
                ahead_lo(dve, nu + n)
            dve.wait_ge(S(f"gate_exp{layer}"), 1)
            dve.tensor_reduce(gate_sum[:, 0, :], pick_s[:, :, :], AX.X, ALU.add).then_inc(S(f"gate_steps{layer}"), 1)
            dve.wait_ge(S(f"gate_steps{layer}"), 2)
            dve.reciprocal(gate_sum[:, 1, :], gate_sum[:, 0, :]).then_inc(S(f"gate_steps{layer}"), 1)
            dve.wait_ge(S(f"gate_steps{layer}"), 3)
            dve.tensor_tensor(pick_s[:, :, :], pick_s[:, :, :],
                              gate_sum[:, 1, :].unsqueeze(2).broadcast_to([P, UNITS, TOPK]),
                              ALU.mult).then_inc(S(f"gates{layer}"), 1)

            for n in range(PICK_SLABS + 2, GATE_SLAB):
                ahead_lo(dve, nu + n)

            dve.wait_ge(S(f"pickT_t{layer}"), 1)
            dve.tensor_copy(pickT[:, 0:2, :], bank[6][:, :].rearrange("p (a t) -> p a t", t=SEQ))
            dve.tensor_copy(pickT[:, 2, :], bank[7][:, 0:SEQ]).then_inc(S(f"pickT{layer}"), 1)
            dve.wait_ge(S(f"pickT{layer}"), 1)
            dve.wait_ge(S("x_saved"), 16 * (layer + 1))

            def hots(g, slot):
                for k in range(4):
                    tk = bass.ds(4 * g + k, 1)
                    a = dve.tensor_scalar(hot_i[:, slot, k, :], iota[:, :], pickT[:, 0, tk], pickT[:, 2, tk],
                                          ALU.is_equal, ALU.mult)
                a.then_inc(S(f"hot_i{layer}"), 1)

            def gate(g, slot):
                dve.wait_ge(S(f"gmat{layer}"), g + 1)
                a = act_all[:, :, bass.ds(4 * g, 4)]
                dve.tensor_tensor(a, bank[6 + slot][:, :].rearrange("p (t j) -> p j t", t=4), a,
                                  ALU.mult).then_inc(S(f"gated{layer}"), 1)

            hots(0, 0)
            hots(1, 1)
            dve.wait_ge(S("act_ones"), layer + 1)

            def early_lo(u, blk):
                w = slice(blk * P, (blk + 1) * P)
                dve.wait_ge(S(f"w_hi{layer}"), W_SLOTS * blk + u + 1)
                dve.tensor_tensor(hT_lo[:, u, w], act_all[:, u, w], hT_hi[:, u, w].bitcast(F32),
                                  ALU.subtract).then_inc(S(f"w_lo{layer}"), 1)

            def gelu_and_gate(i, last):
                for u in range(4):
                    dve.wait_ge(S(f"gelued{layer}"), 4 * i + u + 1)
                    a = act_all[:, bass.ds(GATE_SLAB + 4 * i + u, 1), :].rearrange("p a t -> p (a t)")
                    dve.tensor_tensor(a, bank[4 + u % 2][:, 0:SEQ], a, ALU.mult).then_inc(S("fbank_free"), 1)
                    ahead_lo(dve, nu + GATE_SLAB + u, i)
                    if last and u == 3:
                        for k in range(W_SLOTS):
                            early_lo(k, 0)
                    dve.wait_ge(S("fbank_free"), 2 + (layer + 1) * (LISTS + NKEYS) - GATED + 4 * i + u + 1)
                    gate(4 * i + u, u % 2)
                    hots(4 * i + u + 2, u % 2)
                    dve.wait_ge(S(f"gated{layer}"), 4 * i + u + 1)

            with dve.Fori(0, GATED // 4 - 1) as i:
                gelu_and_gate(i, False)
            gelu_and_gate(GATED // 4 - 1, True)
            ahead_lo(dve, nv)
            for g in range(GATED, SEQ // 4):
                gate(g, g % 2)
                if g + 2 < SEQ // 4:
                    hots(g + 2, g % 2)
            dve.wait_ge(S(f"gated{layer}"), SEQ // 4)
            for u in range(W_SLOTS):
                early_lo(u, 1)

            def weight_lo(u, i):
                if isinstance(i, int) and 4 * i + u >= NKEYS:
                    return
                dve.wait_ge(S(f"w_hi{layer}"), W_SLOTS + 4 * i + u + 1)
                dve.tensor_tensor(hT_lo[:, u % W_SLOTS, :], act_all[:, bass.ds(4 * i + u, 1), :].rearrange("p a t -> p (a t)"),
                                  hT_hi[:, u % W_SLOTS, :].bitcast(F32), ALU.subtract).then_inc(S(f"w_lo{layer}"), 1)

            def values(i):
                for u in range(4):
                    weight_lo(u + 2, i)
                    ahead_lo(dve, nv + u, i)

            ahead_lo(dve, nv + 1)
            weight_lo(4, 0)
            ahead_lo(dve, nv + 2)
            weight_lo(5, 0)
            ahead_lo(dve, nv + 3)
            with dve.Fori(1, NKEYS // 4 - 1) as i:
                values(i)
            values(NKEYS // 4 - 1)
            dve.wait_ge(S("x_back"), 16 * (layer + 1))
            add_banks(dve, nv + NKEYS, 2 * layer + 2)

        @block.vector
        def _(dve):
            norm_dve(dve, 0)
            for n in range(AHEAD):
                split_lo(dve, n)
            dve.wait_ge(S("in_ng"), 16)
            dve.wait_ge(S("in_lg"), 16)
            transposed_dve(dve, norm_gains(0), "n0", norm_banks(0))
            count = [0]

            def chain(ins):
                count[0] += 1
                ins.then_inc(S("dve_chain"), 1)
                dve.wait_ge(S("dve_chain"), count[0])

            def wide(v, n):
                return v.unsqueeze(2).broadcast_to([P, v.shape[1], n])

            nl, ng, nuq, nukv, no = (first[k] for k in ("w_in_lat", "w_in_gm", "w_uq", "w_ukv", "w_out"))
            for k in range(KC):
                ahead_lo(dve, nl + k)
            dve.wait_ge(S("in_pos"), 16)
            dve.wait_ge(S("c_freq"), 1)
            chain(dve.tensor_copy(m_pos, m_posi.bitcast(I32)))
            for blk in range(NBLK):
                a = dve.tensor_scalar(m_ang[:, 0, blk, :], m_freq, m_pos[:, blk:blk + 1], None, ALU.mult)
            chain(a)
            for k, shift in ((0, 0.0), (1, 0.25)):
                magic = 1.5 * 2.0 ** 23
                chain(dve.tensor_scalar(m_ang[:, 1, :, :], m_ang[:, 0, :, :], float(1 / (2 * np.pi)), shift, ALU.mult, ALU.add))
                chain(dve.tensor_scalar(m_ang[:, 2, :, :], m_ang[:, 1, :, :], magic, None, ALU.add))
                chain(dve.tensor_scalar(m_ang[:, 2, :, :], m_ang[:, 2, :, :], magic, None, ALU.subtract))
                two_pi = 2 * np.pi
                c1 = 6.28125
                c2 = float(np.float32(np.round((two_pi - c1) * 2.0 ** 20) / 2.0 ** 20))
                c3 = float(np.float32(two_pi - c1 - c2))
                src = m_ang[:, 0, :, :]
                for c in (c1, c2, c3):
                    chain(dve.scalar_tensor_tensor(out=m_ang[:, 3, :, :], in0=m_ang[:, 2, :, :], scalar=-c, in1=src,
                                                   op0=ALU.mult, op1=ALU.add))
                    src = m_ang[:, 3, :, :]
                chain(dve.tensor_scalar(m_ang[:, 3, :, :], m_ang[:, 3, :, :], float(np.pi / 2) if k else 0.0,
                                        float(np.float32(3.1415925)), ALU.add, ALU.min))
                a = dve.tensor_scalar(m_ang[:, 4 + k, :, :], m_ang[:, 3, :, :], -float(np.float32(3.1415925)), None, ALU.max)
                if k:
                    a.then_inc(S("ang_ready"), 1)
                else:
                    chain(a)
            ahead_lo(dve, ng)
            dve.wait_ge(S("lat_squared"), 1)
            dve.tensor_scalar(m_st[:, 1, 0:2], m_st[:, 0, 0:2], 1.0 / QRANK, EPS, ALU.mult, ALU.add)
            dve.tensor_scalar(m_st[:, 1, 2:4], m_st[:, 0, 2:4], 1.0 / KVRANK, EPS, ALU.mult, ALU.add).then_inc(S("lat_var"), 1)
            ahead_lo(dve, ng + 1)
            dve.wait_ge(S("lat_std"), 1)
            chain(dve.reciprocal(m_st[:, 1, 0:4], m_st[:, 2, 0:4]))
            for blk in range(NBLK):
                dve.tensor_scalar(m_lat[:, blk, 0:QRANK], m_lat[:, blk, 0:QRANK], m_st[:, 1, blk:blk + 1], None, ALU.mult)
                a = dve.tensor_scalar(m_lat[:, blk, QRANK:QRANK + KVRANK], m_lat[:, blk, QRANK:QRANK + KVRANK],
                                      m_st[:, 1, 2 + blk:3 + blk], None, ALU.mult)
            a.then_inc(S("lat_normed"), 1)
            ahead_lo(dve, ng + 2)
            for blk in range(NBLK):
                a = dve.tensor_copy(m_qk[:, 2 * blk + 1, :, NOPE:],
                                    m_lat[:, blk, LAT - ROPE:LAT].unsqueeze(1).broadcast_to([P, MH, ROPE]))
            a.then_inc(S("k_pe"), 1)
            ahead_lo(dve, ng + 3)
            for k in range(4, KC):
                ahead_lo(dve, ng + k)
            transposed_dve(dve, [lat_gain[:, c:c + 1] for c in range(QCH + KVCH)], "lt", norm_banks(1))
            ahead_lo(dve, nuq)
            dve.wait_ge(S("gm_squared"), 1)
            chain(dve.tensor_reduce(m_st[:, 7, 16:32], m_vsq.rearrange("p a (h d) -> p (a h) d", d=GD), AX.X, ALU.add))
            dve.tensor_scalar(m_st[:, 3, 0:16], m_st[:, 7, 16:32], 1.0 / GD, EPS, ALU.mult, ALU.add).then_inc(S("gm_var"), 1)
            ahead_lo(dve, nuq + 1)
            dve.wait_ge(S("gm_std"), 1)
            dve.reciprocal(m_st[:, 7, 0:16], m_st[:, 4, 0:16]).then_inc(S("gm_rstd"), 1)
            ahead_lo(dve, nuq + 2)
            dve.wait_ge(S("qk_squared"), 1)
            chain(dve.tensor_reduce(stat_of(3, 1), qk_of(m_sq, 0), AX.X, ALU.add))
            dve.tensor_scalar(m_st[:, 8, 0:16], m_st[:, 3, 16:32], 1.0 / QK, EPS, ALU.mult, ALU.add).then_inc(S("qk_var"), 1)
            ahead_lo(dve, nukv)
            dve.wait_ge(S("qk_std"), 1)
            dve.reciprocal(m_st[:, 10, 0:16], m_st[:, 9, 0:16]).then_inc(S("q_rstd"), 1)
            ahead_lo(dve, nukv + 1)
            dve.wait_ge(S("qk_squared"), 2)
            chain(dve.tensor_reduce(stat_of(4, 1), qk_of(m_sq, 1), AX.X, ALU.add))
            dve.tensor_scalar(m_st[:, 8, 16:32], m_st[:, 4, 16:32], 1.0 / QK, EPS, ALU.mult, ALU.add).then_inc(S("qk_var"), 1)
            dve.wait_ge(S("mixed"), 1)
            dve.wait_ge(S("in_bs"), 16)
            for blk in range(NBLK):
                a = dve.tensor_tensor(m_cat[:, blk, 0:512].rearrange("p (h d) -> p h d", d=GD),
                                      bank[blk][:, :].rearrange("p (h d) -> p h d", d=GD), wide(m_bs, GD), ALU.add)
            chain(a)
            dve.wait_ge(S("gm_gelu"), 4)
            dve.tensor_tensor(m_cat[:, :, 0:512], m_cat[:, :, 0:512], m_u, ALU.mult).then_inc(S("gm_done"), 1)
            dve.wait_ge(S("qk_std"), 2)
            chain(dve.reciprocal(m_st[:, 10, 16:32], m_st[:, 9, 16:32]))
            dve.wait_ge(S("in_qkg"), 32)
            normed(dve, 1, chain)
            transposed_dve(dve, [None] * 4, "cg")
            gained(dve, 1, chain)
            ahead_lo(dve, no)
            dve.wait_ge(S("sincos"), 1)
            rope(dve, 1, chain).then_inc(S("k_roped"), 1)
            for k in range(1, 4):
                ahead_lo(dve, no + k)
            dve.wait_ge(S("c_mask"), 1)
            for h in range(MH):
                dve.wait_ge(S("s_ready"), h + 1)
                chain(dve.scalar_tensor_tensor(out=m_p[:, h, :], in0=bank[4 + h % 2][:, 0:3 * P], scalar=float(QK) ** -0.5,
                                               in1=m_mask, op0=ALU.mult, op1=ALU.add))
                dve.tensor_reduce(m_st[:, 5, h:h + 1], m_p[:, h, 0:P], AX.X, ALU.max, negate=True)
                dve.tensor_reduce(m_st[:, 6, h:h + 1], m_p[:, h, P:3 * P], AX.X, ALU.max, negate=True).then_inc(S("s_max"), 1)
            dve.wait_ge(S("probs"), MH)
            chain(dve.reciprocal(m_st[:, 4, 0:16], m_st[:, 11, 0:16]))
            dve.wait_ge(S("attended"), 1)
            for blk in range(NBLK):
                a = dve.tensor_tensor(m_cat[:, blk, 512:1024].rearrange("p (h d) -> p h d", d=VD),
                                      bank[4 + blk][:, :].rearrange("p (h d) -> p h d", d=VD),
                                      wide(m_st[:, 4, blk * MH:(blk + 1) * MH], VD), ALU.mult)
            a.then_inc(S("cat_ready"), 1)
            transposed_dve(dve, [None] * 4, "ca", at=4)
            for k in range(4, KC):
                ahead_lo(dve, no + k)
            add_banks(dve, first["w_q0"], 1)

            for layer in range(2):
                if layer:
                    conv_dve(dve)
                peer_dve(dve, layer)

        def conv_pe(pe):
            n0 = first["pw1"]
            norm_pe(pe, 2)
            for c in range(KC):
                if c >= 4:
                    pe.wait_ge(S("glu"), c - 3)
                cols_product(pe, n0 + 2 * c, bank[pw1_bank(c)][:, 0:SEQ], ready=None if c else "n2_lo")
                cols_product(pe, n0 + 2 * c + 1, bank[pw1_bank(c) + 1][:, 0:SEQ])
            m = 0
            for c, k0 in PE_SHARES:
                pe.wait_ge(S("glu"), KC if k0 else c + 1)
                pe.wait_ge(S("diag"), m + TAPS - k0)
                out = bank[3 if k0 else 4 + c - DVE_CONV][:, 0:SEQ]
                for k in range(k0, TAPS):
                    a = pe.matmul(out, c_diag[:, m, :], c_pad[:, c, k:k + SEQ], start=k == k0, stop=k == TAPS - 1)
                    m += 1
                a.then_inc(S("conv_tapped"), 1)
            for m, c in enumerate(CONV_ORDER):
                pe.wait_ge(S("conv_squared"), m + 1)
                a = pe.matmul(bank[7][:, 0:SEQ], ones, c_sq[:, c, :], start=m == 0, stop=m == KC - 1)
            a.then_inc(S("conv_summed"), 1)
            rows_product(pe, "pw2", [(0, 512), (512, 1024)], "conv_lo", range(KC), KC)

        def peer_pe(pe, layer):
            norm_pe(pe, 1 + 2 * layer)
            nq, nu, nv = first[f"w_q{layer}"], first[f"u{layer}"], first[f"v{layer}"]
            base = layer * (LISTS + NKEYS)
            for i in range(2):
                def query(u):
                    pe.wait_ge(S("fbank_free"), base + 8 * i + u + 1)
                    cols_product(pe, nq + u, bank[4 + u % 2][:, 0:SEQ], 2 * i, ready=None if u or i else f"n{1 + 2 * layer}_lo")

                def score(u):
                    if u == 0:
                        pe.wait_ge(S("in_keys"), 16 * (layer + 1))
                        if i:
                            pe.wait_ge(S(f"scores_out{layer}"), 2)
                    pe.wait_ge(S("fbank_free"), base + 8 * i + u + 3)
                    for blk in range(NBLK):
                        a = pe.matmul(bank[2 * (u // 4) + blk][:, u % 4 * P:(u % 4 + 1) * P],
                                      qT[:, u % 2, blk * P:(blk + 1) * P],
                                      keysT[:, 8 * i + u, :], start=True, stop=True)
                    a.then_inc(S(f"scored{layer}"), 1)

                query(0)
                for u in range(1, 8):
                    query(u)
                    score(u - 1)
                score(7)

            def experts(a, b):
                with pe.Fori(a, b) as i:
                    for u in range(4):
                        pe.wait_ge(S("fbank_free"), base + LISTS + 4 * i + u + 1)
                        cols_product(pe, nu + u, bank[4 + u % 2][:, 0:SEQ], i)

            experts(0, GATE_SLAB // 4)
            pe.wait_ge(S(f"gates{layer}"), 1)
            for k, src in enumerate((pick_i, pick_j, pick_s)):
                for blk in range(NBLK):
                    out = bank[6 + k // 2][:, (k % 2) * SEQ + blk * P:(k % 2) * SEQ + (blk + 1) * P]
                    a = pe.transpose(out, src[:, blk * PH:(blk + 1) * PH, :].rearrange("p h k -> p (h k)"), ident[:, :])
            a.then_inc(S(f"pickT_t{layer}"), 1)

            def gmat(g, slot):
                pe.wait_ge(S(f"hot_i{layer}"), g + 1)
                pe.wait_ge(S(f"hot_j{layer}"), g + 1)
                for k in range(4):
                    a = pe.matmul(bank[6 + slot][:, k * P:(k + 1) * P], hot_i[:, slot, k, :], hot_j[:, slot, k, :],
                                  start=True, stop=True)
                a.then_inc(S(f"gmat{layer}"), 1)

            with pe.Fori(0, GATED // 4) as i:
                for u in range(4):
                    pe.wait_ge(S("fbank_free"), base + LISTS + GATE_SLAB + 4 * i + u + 1)
                    cols_product(pe, nu + GATE_SLAB + u, bank[4 + u % 2][:, 0:SEQ], i)
                    gmat(4 * i + u, u % 2)

            def value(u, i, blk, begin=False, end=False):
                n, w = nv + u, slice(blk * P, (blk + 1) * P)
                for a, b in ((hT_hi, part_hi), (hT_hi, part_lo), (hT_lo, part_hi)):
                    for c in range(2):
                        mm = pe.matmul(bank[2 * blk + c][:, :], a[:, u % W_SLOTS, w],
                                       b[:, n % PARTS, 512 * c:512 * (c + 1)],
                                       start=begin and a is hT_hi and b is part_hi, stop=end and a is hT_lo)
                return mm

            assert SEQ // 4 - GATED == W_SLOTS == 4
            for u in range(W_SLOTS):
                pe.wait_ge(S("slab_lo"), nv + u + 1)
                pe.wait_ge(S(f"w_lo{layer}"), u + 1)
                value(u, 0, 0, begin=u == 0)
                gmat(GATED + u, u % 2)
            for u in range(W_SLOTS):
                pe.wait_ge(S(f"w_lo{layer}"), W_SLOTS + u + 1)
                value(u, 0, 1, begin=u == 0).then_inc(S("slab_used"), 1)

            def values(i, end):
                for u in range(4):
                    pe.wait_ge(S("slab_lo"), nv + u + 1 + 4 * i)
                    pe.wait_ge(S(f"w_lo{layer}"), W_SLOTS + 4 * i + u + 1)
                    last = end and u == 3
                    mm = value(u, i, 0, end=last)
                    if last:
                        mm.then_inc(S("half_done"), 1)
                    value(u, i, 1, end=last).then_inc(S("slab_used"), 1)

            with pe.Fori(1, NKEYS // 4 - 1) as i:
                values(i, False)
            values(NKEYS // 4 - 1, True)

        @block.tensor
        def _(pe):
            pe.wait_ge(S("c_ident"), 1)
            norm_pe(pe, 0)
            halves = [(0, 512), (512, 1024)]
            rows_product(pe, "w_in_lat", [(0, 512), (512, LAT)], "n0_lo", range(KC), KC)
            rows_product(pe, "w_in_gm", halves, "n0_lo", range(0, KC - 1), KC, banks=4)
            pe.wait_ge(S("lat_normed"), 1)
            transposed_pe(pe, m_lat, QCH + KVCH, "lt", norm_banks(1))
            rows_product(pe, "w_in_gm", halves, "n0_lo", range(KC - 1, KC), KC, chunk0=KC - 1, ready0=KC - 1, banks=4)
            pe.wait_ge(S("lt_lo"), QCH + KVCH)
            rows_product(pe, "w_uq", [(0, 4 * QK), (4 * QK, 8 * QK)], "lt_lo", range(QCH), QCH)
            pe.wait_ge(S("gm_gelu"), 4)
            rows_product(pe, "w_ukv", halves, "lt_lo", range(KVCH), KVCH, chunk0=QCH, ready0=QCH, banks=4)
            pe.wait_ge(S("qkv_out"), 1)
            pe.wait_ge(S("v_normed"), 1)
            pe.wait_ge(S("ws_causal"), 1)
            for blk in range(NBLK):
                for h in range(GH):
                    a = pe.matmul(bank[blk][:, h * GD:(h + 1) * GD], m_ws[:, h, :], m_v[:, blk, h * GD:(h + 1) * GD],
                                  start=True, stop=True)
            a.then_inc(S("mixed"), 1)
            pe.wait_ge(S("gm_done"), 1)
            pe.wait_ge(S("qkv_out"), 3)
            transposed_pe(pe, m_cat, 4, "cg")
            rows_product(pe, "w_out", halves, "cg_lo", range(0, 4), KC)
            for r in range(8):
                which, blk, half = r // 4, r // 2 % 2, r % 2
                pe.wait_ge(S("k_roped" if which else "q_roped"), 1)
                if r >= 2:
                    pe.wait_ge(S("qkT"), r - 1)
                for h in range(4):
                    a = pe.transpose(bank[6 + r % 2][0:QK, h * P:(h + 1) * P], m_qk[:, 2 * blk + which, 4 * half + h, :],
                                     ident[:, :])
                a.then_inc(S("qkT_t"), 1)
            pe.wait_ge(S("qkT"), 8)
            for h in range(MH + 3):
                if h < MH:
                    if h >= 2:
                        pe.wait_ge(S("s_max"), h - 1)
                    q, k = m_qkT[0:QK, 0, h, :], m_qkT[0:QK, 1, h, :]
                    pe.matmul(bank[4 + h % 2][:, 0:P], q[:, 0:P], k[:, 0:P], start=True, stop=True)
                    pe.matmul(bank[4 + h % 2][:, P:3 * P], q[:, P:2 * P], k, start=True, stop=True).then_inc(S("s_ready"), 1)
                if h >= 3:
                    r = h - 3
                    pe.wait_ge(S("probs"), r + 1)
                    if r >= 2:
                        pe.wait_ge(S("pT"), r - 1)
                    for c in range(3):
                        a = pe.transpose(bank[6 + r % 2][:, c * P:(c + 1) * P], m_p[:, r, c * P:(c + 1) * P], ident[:, :])
                    a.then_inc(S("pT_t"), 1)
            pe.wait_ge(S("s_max"), MH)
            for h in range(MH):
                pe.wait_ge(S("pT"), h + 1)
                o = slice(h * VD, (h + 1) * VD)
                pe.matmul(bank[4][:, o], m_pT[:, h, 0, :], m_val[:, 0, h, :], start=True, stop=True)
                pe.matmul(bank[5][:, o], m_pT[:, h, 1, :], m_val[:, 0, h, :], start=True, stop=False)
                a = pe.matmul(bank[5][:, o], m_pT[:, h, 2, :], m_val[:, 1, h, :], start=False, stop=True)
            a.then_inc(S("attended"), 1)
            pe.wait_ge(S("cat_ready"), 1)
            transposed_pe(pe, m_cat, 4, "ca", at=4)
            rows_product(pe, "w_out", halves, "ca_lo", range(4, KC), KC, chunk0=4)

            for layer in range(2):
                if layer:
                    conv_pe(pe)
                peer_pe(pe, layer)

def kernel(**inputs):
    import numpy as _np
    import concourse.bacc as _bacc
    from concourse import mybir as _mybir
    from concourse.bass_utils import run_bass_kernel_spmd as _run

    a = {k: _np.asarray(v) for k, v in inputs.items()}

    def columns(w):
        return w.reshape(8, 128, 16, 128).transpose(2, 1, 0, 3).reshape(16, 128, 1024)

    pw1 = columns(a["conv_w_pw1"][0]).reshape(2, 8, 128, 1024).transpose(1, 0, 2, 3).reshape(16, 128, 1024)
    arrays = {k: a[k] for k in (
        "x", "w_in", "gm_v_gain", "mla_w_uq", "mla_w_ukv", "mla_q_gain", "mla_k_gain", "w_out", "conv_w_pw2",
        "conv_b_pw2")}

    def on_partitions(*vectors):
        return _np.stack([v.reshape(-1, 128).T for v in vectors], axis=1)

    arrays["positions"] = a["positions"][0].reshape(2, 128).T
    arrays["norm_gains"] = on_partitions(a["mix_norm_even"][0], a["ffn_norm"][0], a["mix_norm_odd"][0], a["ffn_norm"][1])
    arrays["latent_gains"] = _np.concatenate([a["mla_q_lat_gain"][0].reshape(3, 128).T,
                                              a["mla_kv_lat_gain"][0].reshape(2, 128).T], axis=1)
    arrays["conv_columns"] = on_partitions(a["conv_b_pw1"][0, 0:1024], a["conv_b_pw1"][0, 1024:2048],
                                           a["conv_b_dw"][0], a["conv_norm_gain"][0])
    arrays["gm_w_sT"] = a["gm_w_s"][0].transpose(2, 0, 1)
    arrays["gm_b_sT"] = a["gm_b_s"][0].T
    arrays["conv_w_pw1"] = pw1
    arrays["conv_w_dwT"] = a["conv_w_dw"][0].reshape(31, 8, 128).transpose(2, 1, 0)
    arrays["peer_w_q"] = _np.stack([columns(w) for w in a["peer_w_q"]])
    arrays["peer_keysT"] = a["peer_sub_keys"].transpose(0, 4, 2, 1, 3).reshape(2, 128, 16, 128)
    arrays["peer_u"] = a["peer_u"].reshape(2, 128, 128, 8, 128).transpose(0, 2, 4, 3, 1).reshape(2, 128, 128, 1024)
    arrays["peer_v"] = a["peer_v"].reshape(2, 128, 128, 1024).transpose(0, 2, 1, 3)
    arrays = {k: _np.ascontiguousarray(v) for k, v in arrays.items()}

    nc = _bacc.Bacc("TRN2", target_bir_lowering=False, num_devices=1)
    t = {k: nc.dram_tensor(k, v.shape, _mybir.dt.from_np(v.dtype), kind="ExternalInput").ap() for k, v in arrays.items()}
    t["out"] = nc.dram_tensor("out", (1, 256, 1024), _mybir.dt.float32, kind="ExternalOutput").ap()
    build(nc, t)
    r = _run(nc, [arrays], core_ids=[0])
    return r.results[0]["out"]
```
